# Optimizing a Trainium2 kernel written in Bass

```python
import jax, jax.numpy as jnp
from jax import lax
import numpy as np

D_MODEL = 1024
BATCH = 1
SEQ = 1024
DEPTH = 2

GRID_W = 64
CTX_LEN = 256
HEAD_DIM = 64
EPS = 1e-6
NEG_INF = -1e30
A_HEADS = 8
A_KV_HEADS = 2
A_GROUP = A_HEADS // A_KV_HEADS
A_WINDOW = 128
A_BLOCK = 128
A_WIDTH = A_HEADS * HEAD_DIM
A_KV_WIDTH = A_KV_HEADS * HEAD_DIM
ROPE_BASE = 10000.0
B_GROUPS = 4
B_WIDTH = B_GROUPS * HEAD_DIM
CONV_W = 3
R_HEADS = 4
R_WIDTH = R_HEADS * HEAD_DIM
R_CHUNK = 128
F_GROUPS = 4
F_WIDTH = F_GROUPS * HEAD_DIM
N_BRANCH = 4

IN_NAMES = ("a_q", "a_k", "a_v", "a_z", "b_u", "b_b", "b_c", "b_z", "r_q", "r_k", "r_v", "r_z", "f_u", "f_z", "merge")
IN_SIZES = (A_WIDTH, A_KV_WIDTH, A_KV_WIDTH, A_WIDTH, B_WIDTH, B_WIDTH, B_WIDTH, B_WIDTH,
            R_WIDTH, R_WIDTH, R_WIDTH, R_WIDTH, F_WIDTH, F_WIDTH, N_BRANCH * D_MODEL)
IN_WIDTH = sum(IN_SIZES)
CTX_KV_NAMES = ("a_k", "a_v", "r_k", "r_v")

kernel_name = "hybrid_gated_branch_diffusion_trunk"

def _rmsnorm(x, g):
    xf = x.astype(jnp.float32)
    y = xf * lax.rsqrt(jnp.mean(xf * xf, axis=-1, keepdims=True) + EPS)
    return (y * g.astype(jnp.float32)).astype(x.dtype)

def _head_norm(y):
    mu = jnp.mean(y, axis=-1, keepdims=True)
    var = jnp.mean(jnp.square(y - mu), axis=-1, keepdims=True)
    return (y - mu) * lax.rsqrt(var + EPS)

def _in_proj(h, w_in, names):
    offs = np.cumsum((0,) + IN_SIZES)
    sel = [i for i, nm in enumerate(IN_NAMES) if nm in names]
    if len(sel) == len(IN_NAMES):
        w = w_in
    else:
        w = jnp.concatenate([w_in[:, int(offs[i]):int(offs[i + 1])] for i in sel], axis=1)
    p = h @ w
    sizes = [IN_SIZES[i] for i in sel]
    parts = jnp.split(p, [int(s) for s in np.cumsum(sizes)[:-1]], axis=-1)
    return {IN_NAMES[i]: part for i, part in zip(sel, parts)}

def _split_heads(t, h):
    b, n, _ = t.shape
    return t.reshape(b, n, h, HEAD_DIM)

def _axial_rope(n):
    rows = n // GRID_W
    row = jnp.broadcast_to(jnp.arange(rows)[:, None], (rows, GRID_W)).reshape(-1).astype(jnp.float32)
    col = jnp.broadcast_to(jnp.arange(GRID_W)[None, :], (rows, GRID_W)).reshape(-1).astype(jnp.float32)
    half = HEAD_DIM // 2
    inv = ROPE_BASE ** (-jnp.arange(0, half, 2, dtype=jnp.float32) / half)
    ang = jnp.stack([row[:, None] * inv, col[:, None] * inv], axis=1)
    return jnp.cos(ang), jnp.sin(ang)

def _apply_rope(t, cos, sin):
    b, n, h, d = t.shape
    t = t.reshape(b, n, h, 2, 2, d // 4)
    t1, t2 = t[..., 0, :], t[..., 1, :]
    c = cos[None, :, None].astype(t.dtype)
    s = sin[None, :, None].astype(t.dtype)
    out = jnp.stack([t1 * c - t2 * s, t2 * c + t1 * s], axis=-2)
    return out.reshape(b, n, h, d)

def _window_attention(q, k, v, kc, vc, sink):
    b, s, h, d = q.shape
    nb = s // A_BLOCK
    scale = d ** -0.5
    qb = q.reshape(b, nb, A_BLOCK, A_KV_HEADS, A_GROUP, d)
    pad = ((0, 0), (A_BLOCK, A_BLOCK), (0, 0), (0, 0))
    kp = jnp.pad(k, pad).reshape(b, nb + 2, A_BLOCK, A_KV_HEADS, d)
    vp = jnp.pad(v, pad).reshape(b, nb + 2, A_BLOCK, A_KV_HEADS, d)
    kb = jnp.concatenate([kp[:, :-2], kp[:, 1:-1], kp[:, 2:]], axis=2)
    vb = jnp.concatenate([vp[:, :-2], vp[:, 1:-1], vp[:, 2:]], axis=2)
    s_loc = jnp.einsum("bnqkgd,bnjkd->bnkgqj", qb, kb).astype(jnp.float32) * scale
    blk = jnp.arange(nb)[:, None] * A_BLOCK
    qpos = blk + jnp.arange(A_BLOCK)[None, :]
    kpos = blk - A_BLOCK + jnp.arange(3 * A_BLOCK)[None, :]
    valid = ((jnp.abs(qpos[:, :, None] - kpos[:, None, :]) <= A_WINDOW)
             & (kpos[:, None, :] >= 0) & (kpos[:, None, :] < s))
    s_loc = jnp.where(valid[None, :, None, None], s_loc, NEG_INF)
    s_ctx = jnp.einsum("bnqkgd,bjkd->bnkgqj", qb, kc).astype(jnp.float32) * scale
    sink_l = jnp.broadcast_to(sink.reshape(A_KV_HEADS, A_GROUP)[:, :, None, None].astype(jnp.float32),
                              s_loc.shape[:-1] + (1,))
    p = jax.nn.softmax(jnp.concatenate([s_loc, s_ctx, sink_l], axis=-1), axis=-1)
    nloc = 3 * A_BLOCK
    nctx = kc.shape[1]
    o = (jnp.einsum("bnkgqj,bnjkd->bnqkgd", p[..., :nloc].astype(v.dtype), vb)
         + jnp.einsum("bnkgqj,bjkd->bnqkgd", p[..., nloc:nloc + nctx].astype(v.dtype), vc))
    return o.reshape(b, s, h * d)

def _context_attention(qc, kc, vc, sink):
    b, L, h, d = qc.shape
    qg = qc.reshape(b, L, A_KV_HEADS, A_GROUP, d)
    sc = jnp.einsum("bqkgd,bjkd->bkgqj", qg, kc).astype(jnp.float32) * (d ** -0.5)
    sink_l = jnp.broadcast_to(sink.reshape(A_KV_HEADS, A_GROUP)[:, :, None, None].astype(jnp.float32),
                              sc.shape[:-1] + (1,))
    p = jax.nn.softmax(jnp.concatenate([sc, sink_l], axis=-1), axis=-1)
    o = jnp.einsum("bkgqj,bjkd->bqkgd", p[..., :L].astype(vc.dtype), vc)
    return o.reshape(b, L, h * d)

def _short_conv(u, w, bias):
    up = jnp.pad(u, ((0, 0), (1, 1), (0, 0)))
    return up[:, :-2] * w[0] + up[:, 1:-1] * w[1] + up[:, 2:] * w[2] + bias

def _retention_states(k, v, lg, r0):
    b, h, n, d = k.shape
    nc = n // R_CHUNK
    idx = jnp.arange(R_CHUNK, dtype=jnp.float32)
    kc_ = k.reshape(b, h, nc, R_CHUNK, d)
    vc_ = v.reshape(b, h, nc, R_CHUNK, d)
    zeta = jnp.exp(lg[:, None] * (R_CHUNK - 1 - idx))
    incr = jnp.einsum("bhncd,bhnce->nbhde", kc_ * zeta[None, :, None, :, None], vc_)
    g_chunk = jnp.exp(lg * R_CHUNK)[None, :, None, None]

    def step(r, u):
        return g_chunk * r + u, r

    r_fin, r_prev = lax.scan(step, r0, incr)
    return r_prev, r_fin

def _retention_outputs(q, k, v, lg, r_prev):
    b, h, n, d = q.shape
    nc = n // R_CHUNK
    idx = jnp.arange(R_CHUNK, dtype=jnp.float32)
    q_ = q.reshape(b, h, nc, R_CHUNK, d)
    k_ = k.reshape(b, h, nc, R_CHUNK, d)
    v_ = v.reshape(b, h, nc, R_CHUNK, d)
    diff = idx[:, None] - idx[None, :]
    decay = jnp.where(diff >= 0, jnp.exp(lg[:, None, None] * jnp.maximum(diff, 0.0)), 0.0)
    sc = jnp.einsum("bhncd,bhnmd->bhncm", q_, k_) * decay[None, :, None]
    inner = jnp.einsum("bhncm,bhnme->bhnce", sc, v_)
    xi = jnp.exp(lg[:, None] * (idx + 1.0))
    cross = jnp.einsum("bhncd,nbhde->bhnce", q_ * xi[None, :, None, :, None], r_prev)
    return (inner + cross).reshape(b, h, n, d)

def _bidir_retention(q, k, v, qc, kc, vc, log_gamma):
    b, h, _, d = q.shape
    r0 = jnp.zeros((b, h, d, d), jnp.float32)
    y, yc = 0.0, 0.0
    for direction in range(2):
        lg = log_gamma[direction]
        fl = (lambda t: jnp.flip(t, axis=2)) if direction == 1 else (lambda t: t)
        prev_c, state_c = _retention_states(fl(kc), fl(vc), lg, r0)
        prev_x, _ = _retention_states(fl(k), fl(v), lg, state_c)
        y = y + fl(_retention_outputs(fl(q), fl(k), fl(v), lg, prev_x))
        if qc is not None:
            yc = yc + fl(_retention_outputs(fl(qc), fl(kc), fl(vc), lg, prev_c))
    y = _head_norm(y)
    yc = _head_norm(yc) if qc is not None else None
    return y, yc

def _fourier(u):
    b, n, _ = u.shape
    ug = u.reshape(b, n, F_GROUPS, HEAD_DIM).astype(jnp.float32)
    y = jnp.fft.fft2(ug, axes=(1, 3), norm="ortho").real
    return y.reshape(b, n, F_WIDTH).astype(u.dtype)

def _merge(ys, zs, merge_logits, w_os, w_out):
    b, n, _ = merge_logits.shape
    gates = jax.nn.sigmoid(merge_logits.reshape(b, n, N_BRANCH, D_MODEL))
    total = 0.0
    for i in range(N_BRANCH):
        total = total + gates[:, :, i] * ((ys[i] * jax.nn.silu(zs[i])) @ w_os[i])
    return total @ w_out

def _to_heads_first(t):
    return jnp.transpose(t, (0, 2, 1, 3)).astype(jnp.float32)

def _from_heads_first(t, dtype):
    b, h, n, d = t.shape
    return jnp.transpose(t, (0, 2, 1, 3)).reshape(b, n, h * d).astype(dtype)

def _layer(x, xc, mod_x, mod_c, cos, sin, g_pre, g_post, w_in, sink, conv_w, conv_b,
           ret_decay, w_o_attn, w_o_conv, w_o_ret, w_o_fourier, w_out, update_ctx):
    shift_x, scale_x, gate_x = jnp.split(mod_x, 3, axis=-1)
    shift_c, scale_c, gate_c = jnp.split(mod_c, 3, axis=-1)
    hx = _rmsnorm(x, g_pre) * (1.0 + scale_x) + shift_x
    hc = _rmsnorm(xc, g_pre) * (1.0 + scale_c) + shift_c
    px = _in_proj(hx, w_in, IN_NAMES)
    pc = _in_proj(hc, w_in, IN_NAMES if update_ctx else CTX_KV_NAMES)
    w_os = (w_o_attn, w_o_conv, w_o_ret, w_o_fourier)
    k_scale = HEAD_DIM ** -0.5

    q_a = _apply_rope(_split_heads(px["a_q"], A_HEADS), cos, sin)
    k_a = _apply_rope(_split_heads(px["a_k"], A_KV_HEADS), cos, sin)
    v_a = _split_heads(px["a_v"], A_KV_HEADS)
    k_ac = _split_heads(pc["a_k"], A_KV_HEADS)
    v_ac = _split_heads(pc["a_v"], A_KV_HEADS)
    y_a = _window_attention(q_a, k_a, v_a, k_ac, v_ac, sink)

    y_b = px["b_b"] * _short_conv(px["b_c"] * px["b_u"], conv_w, conv_b)

    log_gamma = jax.nn.log_sigmoid(ret_decay.astype(jnp.float32))
    q_r = _to_heads_first(_apply_rope(_split_heads(px["r_q"], R_HEADS), cos, sin))
    k_r = _to_heads_first(_apply_rope(_split_heads(px["r_k"], R_HEADS), cos, sin)) * k_scale
    v_r = _to_heads_first(_split_heads(px["r_v"], R_HEADS))
    k_rc = _to_heads_first(_split_heads(pc["r_k"], R_HEADS)) * k_scale
    v_rc = _to_heads_first(_split_heads(pc["r_v"], R_HEADS))
    q_rc = _to_heads_first(_split_heads(pc["r_q"], R_HEADS)) if update_ctx else None
    y_r, y_rc = _bidir_retention(q_r, k_r, v_r, q_rc, k_rc, v_rc, log_gamma)
    y_r = _from_heads_first(y_r, x.dtype)

    y_f = _fourier(px["f_u"])

    y = _merge((y_a, y_b, y_r, y_f), (px["a_z"], px["b_z"], px["r_z"], px["f_z"]), px["merge"], w_os, w_out)
    x_new = x + gate_x * _rmsnorm(y, g_post)
    if not update_ctx:
        return x_new, xc

    yc_a = _context_attention(_split_heads(pc["a_q"], A_HEADS), k_ac, v_ac, sink)
    yc_b = pc["b_b"] * _short_conv(pc["b_c"] * pc["b_u"], conv_w, conv_b)
    yc_r = _from_heads_first(y_rc, xc.dtype)
    yc_f = _fourier(pc["f_u"])
    yc = _merge((yc_a, yc_b, yc_r, yc_f), (pc["a_z"], pc["b_z"], pc["r_z"], pc["f_z"]), pc["merge"], w_os, w_out)
    xc_new = xc + gate_c * _rmsnorm(yc, g_post)
    return x_new, xc_new

def setup_inputs(seed: int = 0) -> dict:
    key = jax.random.key(seed)
    ks = jax.random.split(key, 18)
    f32 = jnp.float32

    def nrm(k, shape, scale):
        return jax.random.normal(k, shape, f32) * scale

    decay_base = jnp.log(2.0 ** (5.0 + jnp.arange(R_HEADS, dtype=f32)) - 1.0)
    return {
        "x": nrm(ks[0], (BATCH, SEQ, D_MODEL), 1.0),
        "c": nrm(ks[1], (BATCH, D_MODEL), 1.0),
        "ctx": nrm(ks[2], (BATCH, CTX_LEN, D_MODEL), 1.0),
        "c_ctx": nrm(ks[3], (D_MODEL,), 1.0),
        "w_ada": nrm(ks[4], (DEPTH, D_MODEL, 3 * D_MODEL), 0.5 * D_MODEL ** -0.5),
        "b_ada": nrm(ks[5], (DEPTH, 3 * D_MODEL), 0.02),
        "norm_pre": 1.0 + nrm(ks[6], (DEPTH, D_MODEL), 0.05),
        "norm_post": 1.0 + nrm(ks[7], (DEPTH, D_MODEL), 0.05),
        "w_in": nrm(ks[8], (DEPTH, D_MODEL, IN_WIDTH), D_MODEL ** -0.5),
        "attn_sink": nrm(ks[9], (DEPTH, A_HEADS), 0.5),
        "conv_w": nrm(ks[10], (DEPTH, CONV_W, B_WIDTH), CONV_W ** -0.5),
        "conv_b": nrm(ks[11], (DEPTH, B_WIDTH), 0.02),
        "ret_decay": decay_base + nrm(ks[12], (DEPTH, 2, R_HEADS), 0.1),
        "w_o_attn": nrm(ks[13], (DEPTH, A_WIDTH, D_MODEL), A_WIDTH ** -0.5),
        "w_o_conv": nrm(ks[14], (DEPTH, B_WIDTH, D_MODEL), B_WIDTH ** -0.5),
        "w_o_ret": nrm(ks[15], (DEPTH, R_WIDTH, D_MODEL), R_WIDTH ** -0.5),
        "w_o_fourier": nrm(ks[16], (DEPTH, F_WIDTH, D_MODEL), F_WIDTH ** -0.5),
        "w_out": nrm(ks[17], (DEPTH, D_MODEL, D_MODEL), D_MODEL ** -0.5),
    }

def reference(x, c, ctx, c_ctx, w_ada, b_ada, norm_pre, norm_post, w_in, attn_sink, conv_w, conv_b,
              ret_decay, w_o_attn, w_o_conv, w_o_ret, w_o_fourier, w_out):
    n = x.shape[1]
    cos, sin = _axial_rope(n)
    silu_c = jax.nn.silu(c)
    silu_cc = jax.nn.silu(c_ctx)
    xc = ctx
    for l in range(DEPTH):
        mod_x = (silu_c @ w_ada[l] + b_ada[l])[:, None, :]
        mod_c = (silu_cc @ w_ada[l] + b_ada[l])[None, None, :]
        x, xc = _layer(x, xc, mod_x, mod_c, cos, sin, norm_pre[l], norm_post[l], w_in[l], attn_sink[l],
                       conv_w[l], conv_b[l], ret_decay[l], w_o_attn[l], w_o_conv[l], w_o_ret[l],
                       w_o_fourier[l], w_out[l], l < DEPTH - 1)
    return x


_drawn_inputs = setup_inputs


def setup_inputs(seed=0):
    import zlib

    import numpy as np

    out = dict(_drawn_inputs(seed))
    spreads = {}
    factors = {'norm_post': 2.73, 'attn_sink': 8.0, 'conv_b': 8.0}
    for name, (base, spread) in spreads.items():
        noise = np.random.default_rng([zlib.crc32(name.encode()), seed]).standard_normal(out[name].shape)
        drawn = base * np.exp(spread * noise) if base else spread * noise
        out[name] = __import__('jax').numpy.asarray(drawn.astype(out[name].dtype))
    for name, factor in factors.items():
        out[name] = (out[name] * factor).astype(out[name].dtype)
    return out
```

```python
from contextlib import ExitStack

import concourse.bass as bass
from concourse import mybir
import numpy as np

F32 = mybir.dt.float32
F32R = mybir.dt.float32r
BF16 = mybir.dt.bfloat16
ALU = mybir.AluOpType
ACT = mybir.ActivationFunctionType
AX = mybir.AxisListType

P = 128
D = 1024
KT = D // P
SEQ = 1024
CTX = 256
DEPTH = 2
GRID_W = 64
HD = 64
EPS = 1e-6
NEG = -1e30
HEADS = 8
RH = 4
SCALE = HD ** -0.5
UNIT = 512
RING = 4
LOOK = 3
SBUF_START = 16512

A_Q, A_K, A_V, A_Z, B_U, B_B, B_C, B_Z, R_Q, R_K, R_V, R_Z, F_U, F_Z, MERGE = (
    0, 4, 5, 6, 10, 12, 14, 16, 18, 20, 22, 24, 26, 28, 30)
Z_A, Z_B, Z_R, Z_F, ZT = 0, 4, 6, 8, 10
BRANCH = ((Z_A, 4), (Z_B, 2), (Z_R, 2), (Z_F, 2))


class Pass:

    def __init__(self, layer, ctx, full):
        self.layer, self.ctx, self.full = layer, ctx, full
        self.s = 1 if ctx else 0
        self.T = CTX if ctx else SEQ
        self.BW = min(512, self.T)
        self.NB = self.T // self.BW
        self.NT = self.T // P
        self.TB = self.BW // P


class Count:

    def __init__(self, eng):
        self.eng, self.n, self.i, self.per = eng, {}, None, {}

    def now(self, name, more=0):
        v = self.n.get(name, 0) + more
        if self.i is not None and self.per.get(name):
            return self.i * self.per[name] + v
        return v

    def take(self, name, by=1):
        self.n[name] = self.n.get(name, 0) + by
        return self.now(name)

    def up(self, name, by=1):
        self.n[name] = self.n.get(name, 0) + by
        return by

    def skip(self, name, by):
        self.n[name] = self.n.get(name, 0) + by

    def loop(self, times, body, **per):
        before = dict(self.n)
        with self.eng.Fori(0, times) as i:
            self.i, self.per = i, per
            body(i)
            self.i, self.per = None, {}
        for name in self.n:
            made = self.n[name] - before.get(name, 0)
            assert made == per.get(name, 0), (name, made, per.get(name, 0))
            self.n[name] = before.get(name, 0) + times * made


def tables():
    out = {}
    n = np.arange(SEQ)
    half = HD // 2
    inv = (10000.0 ** (-np.arange(0, half, 2, dtype=np.float64) / half)).astype(np.float32)
    pos = np.stack([n // GRID_W, n % GRID_W]).astype(np.float32)
    p = np.arange(P) % HD
    axis, r = p // 32, p % 32
    ang = (pos[axis] * inv[r % 16][:, None]).astype(np.float64)
    sign = np.where(r < 16, -1.0, 1.0)[:, None]
    out["rope"] = np.stack([np.cos(ang), sign * np.sin(ang)], 1).astype(np.float32)
    for size, name in ((SEQ, "dft_x"), (CTX, "dft_c")):
        k = np.arange(size)
        a = 2 * np.pi * (np.outer(k, k) % size) / size
        out[name] = np.stack([np.cos(a), np.sin(a)]).astype(np.float32)
    k = np.arange(HD)
    a = 2 * np.pi * (np.outer(k, k) % HD) / HD
    bd = np.zeros((2, P, 2, P), np.float64)
    for s, size in enumerate((SEQ, CTX)):
        norm = (size * HD) ** -0.5
        for g in range(2):
            bd[s, g * HD:(g + 1) * HD, 0, g * HD:(g + 1) * HD] = np.cos(a) * norm
            bd[s, g * HD:(g + 1) * HD, 1, g * HD:(g + 1) * HD] = -np.sin(a) * norm
    out["dft_head"] = bd.astype(np.float32)
    i, j = np.arange(P)[:, None], np.arange(P)[None, :]
    out["mask"] = np.stack([np.where(j >= i, 0, NEG), np.where(j <= i, 0, NEG)], 1).astype(np.float32)
    out["ident"] = np.eye(P, dtype=np.float32)
    xidx = np.where(i < HD, j + 1, P - j)
    out["ret"] = np.stack([np.maximum(j - i, 0), SCALE * (j >= i), np.maximum(i - j, 0), SCALE * (i >= j), xidx], 1).astype(np.float32)
    sel = np.zeros((P, 2), np.float32)
    sel[[0, 64], 0] = 1
    sel[[32, 96], 1] = 1
    small = np.concatenate([sel, (P - 1 - i).astype(np.float32), i.astype(np.float32)], 1)
    out["small"] = small
    return out


def trunk(nc, a, out):
    with ExitStack() as ctx:
        def at(name, shape, offset, dt=F32):
            words = int(np.prod(shape[1:])) * (1 if dt != BF16 else 0.5)
            assert SBUF_START + 4 * (offset + words) <= 229368, name
            return nc.alloc_sbuf_tensor_at(name, shape, dt, offset=SBUF_START + 4 * offset)

        hT = [at("hT_hi", [P, KT, SEQ], 0, F32R), at("hT_lo", [P, KT, SEQ], 8192, F32R)]
        Z = 16384
        z_pass = {0: at("z_x", [P, 2, ZT, 512], Z), 1: at("z_c", [P, 1, ZT, 256], Z)}
        RAW = Z + 2 * ZT * 512
        raw = at("w_raw", [P, RING, UNIT], RAW)
        w_hi = at("w_hi", [P, RING, UNIT], RAW + 2048, F32R)
        w_lo = at("w_lo", [P, RING, UNIT], RAW + 4096, F32R)
        W = RAW + 6144
        C = W + 18432

        class Const:
            top = C

        def const(name, shape, dt=F32):
            t = at(name, shape, Const.top, dt)
            words = int(np.prod(shape[1:]))
            Const.top += -(-(words if dt != BF16 else (words + 1) // 2) // 8) * 8
            return t

        ident = const("ident", [P, P])
        ones = const("ones", [P, P])
        ident_bf = const("ident_bf", [P, P], BF16)
        mask_bf = const("mask_bf", [P, 2, P], BF16)
        kd_c = const("keysT_ctx", [P, 2, CTX])
        v_c = const("values_ctx", [P, 2, P])
        state_c = const("state_ctx", [P, RH, HD])
        small = const("small", [P, 4])
        cT = const("cT", [P, 2, KT])
        sT = const("silu_cT", [P, 2, KT])
        sT_hi = const("silu_hi", [P, 2, KT], F32R)
        sT_lo = const("silu_lo", [P, 2, KT], F32R)
        gpre = const("norm_preT", [P, KT])
        mod = const("modT", [P, 2, 2, KT])
        sink = const("sink", [P, 2, HEADS])
        decay = const("decay", [P, 2 * RH])
        lg = const("log_gamma", [P, 2 * RH])
        lt = const("log_tmp", [P, 6, 2 * RH])
        lgd = const("log_gamma_dir", [P, RH])
        gch = const("gamma_chunk", [P, RH])
        zeta = const("zeta", [P, 2, RH])
        convw = const("conv_wT", [P, 2, 4])
        stat = const("token_stats", [P, 3, 8])
        soft = const("softmax_stats", [P, 2, 8])

        rope = at("rope", [P, 2, SEQ], W + 14336)
        buf = [at("proj_raw0", [P, SEQ], W + 10496), at("proj_raw1", [P, SEQ], W + 11520)]
        turned = at("rope_turned", [P, SEQ], W + 12544)
        m_rows = at("mod_rows", [P, 3 * D], W)
        m_lhs = at("mod_lhs", [P, 2, KT, 4, 32], W + 3072, F32R)
        m_bias = at("mod_bias", [P, 3 * D], W + 5120)
        m_gpost = at("mod_gpost", [P, D], W + 8192)
        m_gate = at("mod_gate", [P, D], W + 9216)
        x_tile = at("x_tile", [P, 8, D], W + 10240)
        m_mask = at("mask_f32", [P, 2, P], W + 10240)
        n_sq = at("norm_square", [P, D], W)
        n_tmp = at("norm_tmp", [P, 2, 512], W + 1024)
        qT = at("a_qT", [P, 4, SEQ], W)
        kd = at("a_kT", [P, 2, SEQ], W + 4096)
        v_x = at("a_v", [P, 8, P], W + 6144)
        prob = at("a_prob", [P, 2, 640], W + 10496)
        probT = at("a_probT", [P, 5, 4, P], W + 10496 + 1280)
        c_u = at("b_u", [P, 2, SEQ], W)
        c_b = at("b_b", [P, 2, SEQ], W + 2048)
        c_cu = at("b_cu", [P, 2, SEQ + 4], W + 4096)
        c_y = at("b_y", [P, 2, SEQ], W + 6400)
        qd = at("r_qT", [P, RH, SEQ], W)
        rk = at("r_kT", [P, 2, SEQ], W + 4096)
        rv = at("r_v", [P, 8, 2, P], W + 6144)
        r_prev = at("r_prev", [P, 8, RH, HD], W + 8192)
        r_inc = at("r_inc", [P, 8, RH, HD], W + 10496)
        r_y = at("r_y", [P, 8, RH, HD], W + 10496)
        r_kz = at("r_kzeta", [P, 2, RH, 2, HD], W + 12544)
        r_tab = at("r_table", [P, 5, P], W + 15360)
        xi = at("r_xi", [P, RH, P], W + 14336)
        dt_ = at("r_decay", [P, RH, P], W + 14848)
        r_sc = at("r_scoresT", [P, 2, RH, P], W + 16384)
        r_qx = at("r_qxi", [P, 2, RH, P], W + 17408)
        r_e = at("r_exp", [P, 2, P], W + 16384)
        r_sq = at("r_square", [P, 8, RH, HD], W + 14336)
        r_stat = at("r_stat", [P, 4, 8 * RH], W + 16384)
        f_u = at("f_uT", [P, 2, SEQ], W)
        f_ab = [at("f_ab_hi", [P, 8, 2, 2, P], W + 2048, F32R), at("f_ab_lo", [P, 8, 2, 2, P], W + 6144, F32R)]
        f_bd = at("f_head", [P, 2 * P], W + 16384)
        yT = {1: [at("yT_hi", [P, ZT, 512], W, F32R), at("yT_lo", [P, ZT, 512], W + 5120, F32R)]}
        tot = [at("total_hi", [P, KT, 512], W + 10240, F32R), at("total_lo", [P, KT, 512], W + 14336, F32R)]
        y_post = at("y_post", [P, 4, D], W)
        x_post = at("x_post", [P, 4, D], W + 4096)
        sq_junk = at("square_junk", [P, 512], W + 8192)
        tmp_blk = [at(f"merge_tmp{b}", [P, 4, 512], Z + b * ZT * 512) for b in range(2)]
        gp_blk = [at(f"gate_row{b}", [P, D], Z + b * ZT * 512 + 2048) for b in range(2)]
        assert Const.top - 0 <= 53210, Const.top

        ps = ctx.enter_context(nc.psum_tensor("ps", [P, 8, 512], F32))

        x_mid = nc.dram_tensor("x_mid", (SEQ, D), F32, kind="Internal").ap()
        c_mid = nc.dram_tensor("c_mid", (CTX, D), F32, kind="Internal").ap()
        gate_rows = nc.dram_tensor("gate_rows", (DEPTH, 2, D), F32, kind="Internal").ap()

        names = (
            "act_own", "dve_own",
            "w_high", "w_split", "w_slot", "w_used",
            "const_in", "small_in", "gate_out", "x_out", "rope_in", "ret_in", "head_in", "post_in",
            "silu_c", "mod_lhs", "mod_saved", "mod_cols", "mod_gate", "gate_made", "log_exp", "log_one", "log_ln",
            "log_gamma", "zeta_exp",
            "square", "mean", "root", "normed", "turned", "hT_pre", "hT_high",
            "proj_out", "raw_free", "v_turned",
            "score", "max", "prob", "prob_scaled", "probT", "probT_saved", "pv", "pv_free",
            "ret_exp", "ret_tab", "k_turned", "kz", "inc", "inc_saved", "sT", "sc", "ret_y", "ret_y_saved",
            "ret_mean", "ret_square", "ret_var", "ret_root", "ret_norm", "ret_yT",
            "four", "four_hi", "four_done",
            "gate", "opart_free", "y_hi", "y_split", "tot_done",
            "y_out", "out_square", "out_mean", "out_root", "x_new",
        )
        sem = {n: ctx.enter_context(nc.semaphore(n)) for n in names}
        landed = [ctx.enter_context(nc.semaphore(f"w_landed{r}")) for r in range(RING)]
        x_in = [ctx.enter_context(nc.semaphore(f"x_in{b}")) for b in range(2)]
        ended = {who: ctx.enter_context(nc.semaphore(f"ended_{who}")) for who in ("act", "dve", "pe")}
        block = ctx.enter_context(nc.Block())

        def stage_end(eng, tally, who):
            eng.drain().then_inc(ended[who], tally.up(f"ended_{who}"))
            for other in ended:
                if other != who:
                    eng.wait_ge(ended[other], tally.take(f"ended_{other}"))

        passes = []
        for layer in range(DEPTH):
            passes.append(Pass(layer, True, layer < DEPTH - 1))
            passes.append(Pass(layer, False, True))

        units, tile_no, raw_no = 0, {}, {}
        for n, p in enumerate(passes):
            p.tiles = list(range(MERGE)) if p.full else [A_K, A_V, R_K, R_K + 1, R_V, R_V + 1]
            for t in p.tiles:
                tile_no[n, t] = len(tile_no)
                if t < A_Z or B_C <= t < B_Z or R_Q <= t < R_Z:
                    raw_no[n, t] = len(raw_no)
            p.n = n
            p.units = 2 * len(p.tiles) + (48 if p.ctx else 0)
            if p.full:
                p.units += (2 if p.ctx else 32) + p.NB * (12 * KT + 2 * KT)
            units += p.units
        total_units = units

        def z_tile(p, tile, count=1):
            return z_pass[p.s][:, 0:p.NB, tile:tile + count, :]

        def banks(first, p):
            return ps[:, first:first + p.NB, 0:p.BW]

        @block.sync
        def _(eng):
            tally = Count(eng)
            unit = [0]

            def load(source, shape=None):
                src = source() if callable(source) else source
                r = unit[0] % RING
                unit[0] += 1
                dst = raw[:, r, :]
                if shape:
                    dst = dst.rearrange(f"p ({' '.join(shape)}) -> p {' '.join(shape)}", **shape)
                eng.wait_ge(sem["w_split"], tally.take("w_split"))
                if tally.i is not None:
                    eng.sem_inc(sem["w_slot"], 1)
                eng.dma_start(dst, src).then_inc(landed[r], tally.up(f"w_landed{r}", 16))

            def rounds(times, body, units):
                assert units % RING == 0
                tally.loop(times, body, w_split=units, **{f"w_landed{r}": 16 * units // RING for r in range(RING)})

            def cols(w, k0, col, kk=4):
                return w[k0 * P:(k0 + kk) * P, bass.ds(eng.snap(col), P)].rearrange("(k p) n -> p k n", p=P)

            k4 = {"k": 4, "n": P}

            def tiles(l, first, count):
                w = a["w_in"][l]

                def body(i):
                    for t in range(2):
                        for u in range(2):
                            load(cols(w, 4 * u, i * (2 * P) + (first + t) * P), k4)
                rounds(count // 2, body, 4)

            def modulation(l):
                def body(i):
                    for n in range(2):
                        for k in range(KT):
                            load(a["w_ada"][l][k * P:(k + 1) * P, bass.ds(eng.snap(i * 1024 + n * 512), 512)])
                rounds(3, body, 16)

            def fourier(p):
                if p.ctx:
                    for n in range(2):
                        load(a["dft_c"][:, n * P:(n + 1) * P, :].rearrange("c p n -> p c n"), {"c": 2, "n": 256})
                    return
                for half in range(2):
                    for n in range(8):
                        for c in range(2):
                            load(a["dft_x"][c, n * P:(n + 1) * P, half * 512:(half + 1) * 512])

            def merge(l):
                wo = ((a["w_o_attn"][l], 0), (a["w_o_rest"][l], 0), (a["w_o_rest"][l], 2), (a["w_o_rest"][l], 2))

                def body(i):
                    for j in range(4):
                        for u in range(2):
                            load(cols(a["w_in"][l], 4 * u, i * P + (MERGE + 8 * j) * P), k4)
                        load(cols(*wo[j], i * P), k4)
                rounds(KT, body, 12)
                for half in range(2):
                    for k in range(KT):
                        load(a["w_out"][l][k * P:(k + 1) * P, half * 512:(half + 1) * 512])

            for p in passes:
                l = p.layer
                if p.ctx:
                    modulation(l)
                if not p.full:
                    tiles(l, A_K, 2)
                    tiles(l, R_K, 4)
                    continue
                tiles(l, A_Q, F_U)
                tiles(l, F_U, 2)
                fourier(p)
                tiles(l, F_Z, 2)
                for b in range(p.NB):
                    merge(l)

        @block.gpsimd
        def _(eng):
            tally = Count(eng)
            eng.sem_inc(sem["w_split"], tally.up("w_split", RING))

            def four(i):
                for r in range(RING):
                    eng.wait_ge(sem["w_high"], tally.take("w_high"))
                    eng.tensor_tensor(w_lo[:, r, :], raw[:, r, :], w_hi[:, r, :].bitcast(F32),
                                           ALU.subtract).then_inc(sem["w_split"], tally.up("w_split"))
            tally.loop(total_units // RING, four, w_high=RING, w_split=RING)
            for r in range(total_units % RING):
                eng.wait_ge(sem["w_high"], tally.take("w_high"))
                eng.tensor_tensor(w_lo[:, r, :], raw[:, r, :], w_hi[:, r, :].bitcast(F32),
                                       ALU.subtract).then_inc(sem["w_split"], tally.up("w_split"))

        @block.tensor
        def _(eng):
            tally = Count(eng)
            eng.sem_inc(sem["w_used"], tally.up("w_used", RING))
            eng.sem_inc(sem["ret_y"], tally.up("ret_y", 2))
            tally.skip("w_split", RING)
            unit = [0]

            def mm(dst, lhsT, rhs, start, stop):
                return eng.matmul(dst, lhsT, rhs, start=start, stop=stop)

            def slot():
                eng.wait_ge(sem["w_split"], tally.take("w_split"))
                unit[0] += 1
                return (unit[0] - 1) % RING

            def three(dst, a_hi, a_lo, b_hi, b_lo, start, stop):
                mm(dst, a_hi, b_hi, start, False)
                mm(dst, a_hi, b_lo, False, False)
                return mm(dst, a_lo, b_hi, False, stop)

            def modulation():
                eng.wait_ge(sem["mod_lhs"], tally.take("mod_lhs"))

                def body(i):
                    for n in range(2):
                        eng.wait_ge(sem["mod_saved"], tally.take("mod_saved"))
                        for k in range(KT):
                            r = slot()
                            mm(ps[:, n, :], m_lhs[:, 0, k, :, :], w_hi[:, r, :], k == 0, False)
                            mm(ps[:, n, :], m_lhs[:, 1, k, :, :], w_lo[:, r, :], False, k == KT - 1).then_inc(sem["w_used"], tally.up("w_used"))
                tally.loop(3, body, mod_saved=2, w_split=16, w_used=16)
                eng.wait_ge(sem["mod_saved"], tally.take("mod_saved", 2))
                for c in range(2 * KT):
                    dst = ps[:, 2, 2 * c:2 * c + 2]
                    mm(dst, m_rows[:, c * P:(c + 1) * P], small[:, 0:2], True, False)
                    last = mm(dst, m_bias[0:1, c * P:(c + 1) * P], ones[0:1, 0:2], False, True)
                last.then_inc(sem["mod_cols"], tally.up("mod_cols"))
                for h in range(2):
                    dst, c = ps[0:2, 3 + h, :], 2 * D + h * 512
                    mm(dst, small[:, 0:2], m_rows[:, c:c + 512], True, False)
                    last = mm(dst, ones[0:1, 0:2], m_bias[0:1, c:c + 512], False, True)
                last.then_inc(sem["mod_gate"], tally.up("mod_gate"))

            def norm(p):
                for b in range(p.NB):
                    eng.wait_ge(sem["normed"], tally.take("normed", p.TB))
                    for k in range(KT):
                        eng.wait_ge(sem["hT_pre"], tally.take("hT_pre"))
                        for t in range(p.TB):
                            last = eng.transpose(ps[:, k % 4, t * P:(t + 1) * P],
                                                 x_tile[:, b * p.TB + t, k * P:(k + 1) * P], ident[:, :])
                        last.then_inc(sem["turned"], tally.up("turned"))

            def project(p, count):
                def body(i):
                    for t in range(2):
                        eng.wait_ge(sem["proj_out"], tally.take("proj_out"))
                        for u in range(2):
                            r = slot()
                            for b in range(p.NB):
                                for k in range(4):
                                    kk, at_ = 4 * u + k, slice(b * p.BW, (b + 1) * p.BW)
                                    w = slice(k * P, (k + 1) * P)
                                    last = three(ps[:, 2 * t + b, 0:p.BW], w_hi[:, r, w], w_lo[:, r, w],
                                                 hT[0][:, kk, at_], hT[1][:, kk, at_], kk == 0, kk == KT - 1)
                            last.then_inc(sem["w_used"], tally.up("w_used"))
                tally.loop(count // 2, body, proj_out=2, w_split=4, w_used=4)

            def turn_values(p, t, before):
                eng.wait_ge(sem["proj_out"], 2 + tile_no[p.n, t] + 1)
                if before is not None:
                    eng.wait_ge(sem["raw_free"], 2 + raw_no[p.n, before] + 1)
                src = buf[raw_no[p.n, t] % 2]
                for n in range(p.NT):
                    last = eng.transpose(ps[:, 4 + n // 4, (n % 4) * P:(n % 4 + 1) * P],
                                         src[:, n * P:(n + 1) * P], ident[:, :])
                last.then_inc(sem["v_turned"], tally.up("v_turned"))

            def attention(p):
                steps = [(qb, h) for qb in range(p.NT) for h in range(HEADS)]

                def window(qb):
                    if p.ctx:
                        return 0, 0
                    return max(qb - 1, 0), min(qb + 1, p.NT - 1) + 1

                def scores(n):
                    qb, h = steps[n]
                    kv, rows, c = h // 4, slice(h % 2 * HD, h % 2 * HD + HD), 2 * (n % 2)
                    lo, hi = window(qb)
                    q = qT[rows, h // 2, qb * P:(qb + 1) * P]
                    eng.wait_ge(sem["prob"], tally.take("prob"))
                    if hi > lo:
                        L = (hi - lo) * P
                        parts = []
                        if lo < qb:
                            parts.append((512 - L, 0))
                        if hi - 1 > qb:
                            parts.append((512 - P, 1))
                        mm(ps[:, c, 512 - L:512], q, kd[rows, kv, lo * P:hi * P], True, not parts)
                        for m, (col, which) in enumerate(parts):
                            mm(ps[:, c, col:col + P], ident_bf[:, :], mask_bf[:, which, :], False, m == len(parts) - 1)
                    mm(ps[:, c + 1, 0:CTX], q, kd_c[rows, kv, :], True, True).then_inc(sem["score"], tally.up("score"))

                def turn(n):
                    qb, h = steps[n]
                    lo, hi = window(qb)
                    eng.wait_ge(sem["prob_scaled"], tally.take("prob_scaled"))
                    eng.wait_ge(sem["probT_saved"], tally.take("probT_saved"))
                    for j in range(hi - lo + 2):
                        last = eng.transpose(ps[:, 4 + j // 4, (j % 4) * P:(j % 4 + 1) * P],
                                             prob[:, n % 2, j * P:(j + 1) * P], ident[:, :])
                    last.then_inc(sem["probT"], tally.up("probT"))

                def values(n):
                    qb, h = steps[n]
                    lo, hi = window(qb)
                    kv = h // 4
                    eng.wait_ge(sem["pv_free"], tally.take("pv_free"))
                    for j in range(hi - lo + 2):
                        v = v_x[:, lo + j, kv * HD:kv * HD + HD] if j < hi - lo else \
                            v_c[:, j - (hi - lo), kv * HD:kv * HD + HD]
                        last = mm(ps[0:HD, 6 + kv, :], v, probT[:, j, :, :], j == 0, j == hi - lo + 1)
                    last.then_inc(sem["pv"], tally.up("pv"))

                scores(0)
                for n in range(len(steps)):
                    if n + 1 < len(steps):
                        scores(n + 1)
                    if n and n % 4 == 0:
                        eng.wait_ge(sem["probT_saved"], tally.now("probT_saved", 1))
                        values(n - 1)
                    turn(n)
                eng.wait_ge(sem["probT_saved"], tally.now("probT_saved", 1))
                values(len(steps) - 1)

            def states(p):
                for n in range(p.NT):
                    c = slice(n * P, (n + 1) * P)
                    for j in range(2):
                        last = eng.transpose(ps[:, 4 + n % 2, j * P:(j + 1) * P], rk[:, j, c], ident[:, :])
                    last.then_inc(sem["k_turned"], tally.up("k_turned"))
                    eng.wait_ge(sem["kz"], tally.take("kz"))
                    eng.wait_ge(sem["inc_saved"], tally.take("inc_saved"))
                    for h in range(RH):
                        v = rv[:, n, h // 2, h % 2 * HD:h % 2 * HD + HD]
                        last = mm(ps[:, 6 + n % 2, h * HD:(h + 1) * HD], r_kz[:, n % 2, h, :, :], v, True, True)
                    last.then_inc(sem["inc"], tally.up("inc"))

            def retention(p):
                def scores(n):
                    c = slice(n * P, (n + 1) * P)
                    for h in range(RH):
                        rows = slice(h % 2 * HD, h % 2 * HD + HD)
                        last = mm(ps[:, n % 2 + 4 * (h % 2), h // 2 * P:(h // 2 + 1) * P], rk[rows, h // 2, c],
                                  qd[rows, h, c], True, True)
                    last.then_inc(sem["sT"], tally.up("sT"))
                scores(0)
                for n in range(p.NT):
                    if n + 1 < p.NT:
                        scores(n + 1)
                    eng.wait_ge(sem["sc"], tally.take("sc"))
                    eng.wait_ge(sem["ret_y_saved"], tally.take("ret_y_saved"))
                    for h in range(RH):
                        dst = ps[:, 2 + n % 2, h * HD:(h + 1) * HD]
                        v = rv[:, n, h // 2, h % 2 * HD:h % 2 * HD + HD]
                        mm(dst, r_sc[:, n % 2, h, :], v, True, False)
                        last = mm(dst, r_qx[:, n % 2, h, :], r_prev[:, n, h, :], False, True)
                    last.then_inc(sem["ret_y"], tally.up("ret_y"))
                eng.wait_ge(sem["ret_norm"], tally.take("ret_norm"))
                for j in range(2):
                    for b in range(p.NB):
                        for t in range(p.TB):
                            last = eng.transpose(ps[:, 4 + 2 * j + b, t * P:(t + 1) * P],
                                                 r_y[:, b * p.TB + t, 2 * j:2 * j + 2, :], ident[:, :])
                        last.then_inc(sem["ret_yT"], tally.up("ret_yT"))

            def fourier(p):
                eng.wait_ge(sem["proj_out"], 2 + tile_no[p.n, F_U + 1] + 1)
                eng.wait_ge(sem["head_in"], tally.take("head_in", 16))
                for n in range(p.NT):
                    eng.wait_ge(sem["four_done"], tally.take("four_done"))
                    for j in range(2):
                        last = mm(ps[:, 4 + n % 2, j * 256:(j + 1) * 256], f_u[:, j, n * P:(n + 1) * P],
                                  f_bd[:, :], True, True)
                    last.then_inc(sem["four"], tally.up("four"))
                eng.wait_ge(sem["four_done"], tally.now("four_done", 2))
                for half in range(p.NB):
                    for n in range(p.NT):
                        for c in range(2):
                            if not p.ctx or c == 0:
                                r = slot()
                            w = slice(c * p.BW, (c + 1) * p.BW) if p.ctx else slice(0, 512)
                            for j in range(2):
                                last = three(ps[:, 4 + 2 * half + j, 0:p.BW], f_ab[0][:, n, j, c, :],
                                             f_ab[1][:, n, j, c, :], w_hi[:, r, w], w_lo[:, r, w],
                                             n == 0 and c == 0, n == p.NT - 1 and c == 1)
                            if not p.ctx or c == 1:
                                last.then_inc(sem["w_used"], tally.up("w_used"))

            def merge(p, b):
                at_ = slice(b * p.BW, (b + 1) * p.BW)

                def body(i, first=False):
                    for j, (tile, count) in enumerate(BRANCH):
                        eng.wait_ge(sem["gate"], tally.take("gate"))
                        for u in range(2):
                            r = slot()
                            for k in range(4):
                                kk, w = 4 * u + k, slice(k * P, (k + 1) * P)
                                last = three(ps[:, j % 2, 0:p.BW], w_hi[:, r, w], w_lo[:, r, w],
                                             hT[0][:, kk, at_], hT[1][:, kk, at_], kk == 0, kk == KT - 1)
                            last.then_inc(sem["w_used"], tally.up("w_used"))
                        eng.wait_ge(sem["opart_free"], tally.take("opart_free"))
                        r = slot()
                        if first:
                            eng.wait_ge(sem["y_split"], tally.take("y_split"))
                        for k in range(count):
                            kk = k + (2 if j == 3 else 0)
                            w = slice(kk * P, (kk + 1) * P)
                            last = three(ps[:, 2 + j % 2, 0:p.BW], w_hi[:, r, w], w_lo[:, r, w],
                                         yT[1][0][:, tile + k, 0:p.BW], yT[1][1][:, tile + k, 0:p.BW],
                                         k == 0, k == count - 1)
                        last.then_inc(sem["w_used"], tally.up("w_used"))
                body(0, True)
                tally.loop(KT - 1, body, gate=4, w_split=12, w_used=12, opart_free=4)
                eng.wait_ge(sem["gate"], tally.now("gate", 2))
                eng.wait_ge(sem["opart_free"], tally.now("opart_free", 2))
                eng.wait_ge(sem["tot_done"], tally.take("tot_done", KT))
                for half in range(2):
                    for k in range(KT):
                        r = slot()
                        for t in range(p.TB):
                            w = slice(t * P, (t + 1) * P)
                            last = three(ps[:, 4 - 4 * half + t, :], tot[0][:, k, w], tot[1][:, k, w],
                                         w_hi[:, r, :], w_lo[:, r, :], k == 0, k == KT - 1)
                        last.then_inc(sem["w_used"], tally.up("w_used"))

            stage_end(eng, tally, "pe")
            for p in passes:
                if p.ctx:
                    modulation()
                    stage_end(eng, tally, "pe")
                norm(p)
                stage_end(eng, tally, "pe")
                if not p.full:
                    project(p, 2)
                    turn_values(p, A_V, None)
                    project(p, 4)
                    turn_values(p, R_V, A_V)
                    turn_values(p, R_V + 1, R_V)
                    stage_end(eng, tally, "pe")
                    states(p)
                    stage_end(eng, tally, "pe")
                    continue
                project(p, 6)
                turn_values(p, A_V, None)
                project(p, 4)
                stage_end(eng, tally, "pe")
                attention(p)
                stage_end(eng, tally, "pe")
                project(p, 8)
                stage_end(eng, tally, "pe")
                project(p, 6)
                turn_values(p, R_V, A_V)
                turn_values(p, R_V + 1, R_V)
                project(p, 2)
                stage_end(eng, tally, "pe")
                states(p)
                retention(p)
                stage_end(eng, tally, "pe")
                project(p, 2)
                fourier(p)
                project(p, 2)
                stage_end(eng, tally, "pe")
                for b in range(p.NB):
                    merge(p, b)
                    stage_end(eng, tally, "pe")

        @block.scalar
        def _(eng):
            tally = Count(eng)
            eng.sem_inc(sem["probT_saved"], tally.up("probT_saved", 1))
            eng.sem_inc(sem["proj_out"], tally.up("proj_out", 2))
            eng.sem_inc(sem["prob"], tally.up("prob", 2))
            eng.sem_inc(sem["inc_saved"], tally.up("inc_saved", 2))
            eng.sem_inc(sem["ret_y_saved"], tally.up("ret_y_saved", 2))
            eng.sem_inc(sem["gate"], tally.up("gate", 2))
            tally.skip("hT_pre", 4)
            tally.skip("ret_y", 2)
            tally.skip("w_used__done", RING)
            split = [0]

            def act(dst, src, func=ACT.Copy, **kw):
                return eng.activation(dst, src, func, **kw)

            def split_high(count):
                for _ in range(count):
                    if split[0] >= total_units:
                        return
                    r = split[0] % RING
                    split[0] += 1
                    eng.wait_ge(landed[r], tally.take(f"w_landed{r}", 16))
                    eng.wait_ge(sem["w_used"], tally.take("w_used"))
                    act(w_hi[:, r, :], raw[:, r, :]).then_inc(sem["w_high"], tally.up("w_high"))

            def constants():
                eng.dma_start(ident[:, :], a["ident"]).then_inc(sem["const_in"], tally.up("const_in", 16))
                eng.dma_start(m_mask[:, :, :], a["mask"]).then_inc(sem["const_in"], tally.up("const_in", 16))
                eng.dma_start(small[:, :], a["small"]).then_inc(sem["const_in"], tally.up("const_in", 16))
                split_high(LOOK)

            def modulation(l):
                eng.dma_start(cT[:, :, :], a["c_cols"]).then_inc(sem["small_in"], tally.up("small_in", 16))
                eng.dma_start(gpre[:, :], a["norm_pre_cols"][l]).then_inc(sem["small_in"], tally.up("small_in", 16))
                eng.dma_start(convw[:, :, :], a["conv_cols"][l]).then_inc(sem["small_in"], tally.up("small_in", 16))
                eng.dma_start(m_bias[0:1, :], a["b_ada"][l:l + 1, :]).then_inc(sem["small_in"], tally.up("small_in", 16))
                eng.dma_start(m_gpost[0:2, :], a["norm_post"][l:l + 1, :].partition_broadcast(2).rearrange("p a n -> p (a n)")).then_inc(sem["small_in"], tally.up("small_in", 16))
                eng.dma_start(sink[:, 0, :], a["attn_sink"][l:l + 1, :].partition_broadcast(P).rearrange("p a n -> p (a n)")).then_inc(sem["small_in"], tally.up("small_in", 16))
                eng.dma_start(decay[:, :], a["ret_decay"][l:l + 1].rearrange("a d h -> a (d h)").partition_broadcast(P)
                     .rearrange("p a n -> p (a n)")).then_inc(sem["small_in"], tally.up("small_in", 16))
                eng.wait_ge(sem["small_in"], tally.now("small_in"))
                act(sT[:, :, :], cT[:, :, :], ACT.Silu).then_inc(sem["silu_c"], tally.up("silu_c"))
                eng.wait_ge(sem["log_one"], tally.take("log_one"))
                act(lt[:, 1, :], lt[:, 0, :], ACT.Exp, scale=-1.0).then_inc(sem["log_exp"], tally.up("log_exp"))
                eng.wait_ge(sem["log_one"], tally.take("log_one"))
                act(lt[:, 3, :], lt[:, 2, :], ACT.Ln).then_inc(sem["log_ln"], tally.up("log_ln"))
                eng.wait_ge(sem["log_gamma"], tally.take("log_gamma"))
                for d in range(2):
                    act(zeta[:, d, :], lg[:, d * RH:(d + 1) * RH], ACT.Exp, scale=small[:, 2 + d:3 + d]).then_inc(sem["act_own"], tally.up("act_own"))
                act(gch[:, :], lgd[:, :], ACT.Exp, scale=float(P)).then_inc(sem["zeta_exp"], tally.up("zeta_exp"))
                split_high(48)
                tally.skip("w_used__done", 48)
                eng.wait_ge(sem["gate_made"], tally.take("gate_made", 2))
                eng.dma_start(gate_rows[l], m_gate[0:2, :]).then_inc(sem["gate_out"], tally.up("gate_out", 16))
                eng.wait_ge(sem["gate_out"], tally.now("gate_out"))

            def norm(p):
                src = (a["ctx"][0] if p.ctx else a["x"][0]) if p.layer == 0 else (c_mid if p.ctx else x_mid)
                src = src.rearrange("(t p) n -> p t n", p=P)
                for b in range(p.NB):
                    at_ = slice(b * p.TB, (b + 1) * p.TB)
                    eng.dma_start(x_tile[:, at_, :], src[:, at_, :]).then_inc(x_in[b], tally.up(f"x_in{b}", 16))
                for b in range(p.NB):
                    eng.wait_ge(x_in[b], tally.now(f"x_in{b}"))
                    for t in range(b * p.TB, (b + 1) * p.TB):
                        if tally.now("square"):
                            eng.wait_ge(sem["square"], tally.now("square"))
                        act(n_sq[:, :], x_tile[:, t, :], ACT.Square, accum_out=stat[:, 0, t:t + 1]).then_inc(sem["square"], tally.up("square"))
                    eng.wait_ge(sem["mean"], tally.take("mean"))
                    at_ = slice(b * p.TB, (b + 1) * p.TB)
                    act(stat[:, 2, at_], stat[:, 1, at_], ACT.Sqrt).then_inc(sem["root"], tally.up("root"))
                    for k in range(KT):
                        eng.wait_ge(sem["hT_pre"], tally.take("hT_pre"))
                        act(hT[0][:, k, b * p.BW:(b + 1) * p.BW], n_tmp[:, k % 2, 0:p.BW]).then_inc(sem["hT_high"], tally.up("hT_high"))

            def evacuate(p, t, dst, func=ACT.Copy):
                split_high(2)
                if dst is None:
                    eng.wait_ge(sem["raw_free"], tally.take("raw_free"))
                    dst = buf[raw_no[p.n, t] % 2][:, 0:p.T]
                if len(dst.shape) == 2:
                    dst = dst.rearrange("p (b n) -> p b n", b=p.NB)
                eng.wait_ge(sem["w_used"], tally.take("w_used__done", 2))
                act(dst, banks(2 * (tile_no[p.n, t] % 2), p), func).then_inc(sem["proj_out"], tally.up("proj_out"))

            def tile_range(p, first, last):
                for t in range(first, last):
                    for z0, zt, count in ((A_Z, Z_A, 4), (B_Z, Z_B, 2), (R_Z, Z_R, 2), (F_Z, Z_F, 2)):
                        if z0 <= t < z0 + count:
                            evacuate(p, t, z_tile(p, zt + t - z0)[:, :, 0, :], ACT.Silu)
                            break
                    else:
                        dst = None
                        if B_U <= t < B_C:
                            dst = (c_u if t < B_B else c_b)[:, t % 2, 0:p.T]
                        elif F_U <= t:
                            dst = f_u[:, t - F_U, 0:p.T]
                        evacuate(p, t, dst)

            def attention(p):
                steps = [(qb, h) for qb in range(p.NT) for h in range(HEADS)]

                def width(qb):
                    return 0 if p.ctx else (3 - (qb == 0) - (qb == p.NT - 1)) * P

                def exps(n):
                    qb, h = steps[n]
                    L, c, s = width(qb), 2 * (n % 2), n % 2
                    eng.wait_ge(sem["max"], tally.take("max"))
                    s_view = ps[:, c:c + 2, :].rearrange("p a n -> p (a n)")[:, 512 - L:512 + CTX]
                    act(prob[:, s, 0:L + CTX], s_view, ACT.Exp, bias=soft[:, s, 1:2], scale=SCALE,
                             accum_out=soft[:, s, 2:3]).then_inc(sem["act_own"], tally.up("act_own"))
                    act(soft[:, s, 3:4], soft[:, s, 1:2], ACT.Exp, bias=sink[:, 0, h:h + 1], scale=1.0).then_inc(sem["prob"], tally.up("prob"))

                def save(n):
                    qb, h = steps[n]
                    count = (width(qb) + CTX) // P
                    eng.wait_ge(sem["probT"], tally.take("probT"))
                    if n % 4 == 0 and n:
                        eng.wait_ge(sem["pv"], tally.take("pv"))
                    src = ps[:, 4:6, :].rearrange("p a (j n) -> p (a j) n", n=P)[:, 0:count, :]
                    act(probT[:, 0:count, h % 4, :], src).then_inc(sem["probT_saved"], tally.up("probT_saved"))

                for n in range(len(steps)):
                    exps(n)
                    if n:
                        save(n - 1)
                save(len(steps) - 1)
                eng.wait_ge(sem["pv"], tally.take("pv"))

            def decay_tables():
                eng.dma_start(r_tab[:, :, :], a["ret"]).then_inc(sem["ret_in"], tally.up("ret_in", 16))
                eng.wait_ge(sem["ret_in"], tally.now("ret_in"))
                for h in range(RH):
                    act(xi[:, h, :], r_tab[:, 4, :], ACT.Exp, scale=lgd[:, h:h + 1]).then_inc(sem["act_own"], tally.up("act_own"))
                for h in range(RH):
                    act(r_e[:, 0, :], r_tab[:, 0, :], ACT.Exp, scale=lg[:, h:h + 1]).then_inc(sem["act_own"], tally.up("act_own"))
                    act(r_e[:, 1, :], r_tab[:, 2, :], ACT.Exp, scale=lg[:, RH + h:RH + h + 1]).then_inc(sem["ret_exp"], tally.up("ret_exp"))
                    eng.wait_ge(sem["ret_tab"], tally.take("ret_tab"))

            def states(p):
                for n in range(p.NT):
                    eng.wait_ge(sem["inc"], tally.take("inc"))
                    act(r_inc[:, n, :, :], ps[:, 6 + n % 2, 0:RH * HD].rearrange("p (h d) -> p h d", h=RH)).then_inc(sem["inc_saved"], tally.up("inc_saved"))

            def retention(p):
                for n in range(p.NT):
                    eng.wait_ge(sem["ret_y"], tally.take("ret_y"))
                    act(r_y[:, n, :, :], ps[:, 2 + n % 2, 0:RH * HD].rearrange("p (h d) -> p h d", h=RH)).then_inc(sem["ret_y_saved"], tally.up("ret_y_saved"))
                eng.wait_ge(sem["ret_mean"], tally.take("ret_mean"))
                act(r_sq[:, 0:p.NT, :, :], r_y[:, 0:p.NT, :, :], ACT.Square).then_inc(sem["ret_square"], tally.up("ret_square"))
                eng.wait_ge(sem["ret_var"], tally.take("ret_var"))
                act(r_stat[:, 2, 0:p.NT * RH], r_stat[:, 1, 0:p.NT * RH], ACT.Sqrt).then_inc(sem["ret_root"], tally.up("ret_root"))

            def fourier(p):
                for n in range(p.NT):
                    eng.wait_ge(sem["four"], tally.take("four"))
                    act(f_ab[0][:, n, :, :, :].rearrange("p j c n -> p (j c n)"), ps[:, 4 + n % 2, :]).then_inc(sem["four_hi"], tally.up("four_hi"))
                split_high(2 if p.ctx else 32)
                tally.skip("w_used__done", 2 if p.ctx else 32)

            def merge(p, b):
                tmp = tmp_blk[b]
                for tile, count in BRANCH:
                    src = z_pass[p.s][:, b, tile:tile + count, :]
                    act(yT[1][0][:, tile:tile + count, 0:p.BW], src).then_inc(sem["y_hi"], tally.up("y_hi"))
                eng.wait_ge(sem["y_split"], tally.take("y_split__all", len(BRANCH)))

                def body(i):
                    for j in range(4):
                        split_high(3)
                        eng.wait_ge(sem["w_used"], tally.take("w_used__done", 2))
                        eng.wait_ge(sem["opart_free"], tally.take("opart_free"))
                        act(tmp[:, j % 2, 0:p.BW], ps[:, j % 2, 0:p.BW], ACT.Sigmoid).then_inc(sem["gate"], tally.up("gate"))
                        tally.skip("w_used__done", 1)
                tally.loop(KT, body, w_high=12, w_used=12, w_used__done=12, opart_free=4, gate=4,
                       **{f"w_landed{r}": 48 for r in range(RING)})
                split[0] += 12 * (KT - 1)
                dst = (out[0] if p.layer == DEPTH - 1 else x_mid) if not p.ctx else c_mid
                src = (a["ctx"][0] if p.ctx else a["x"][0]) if p.layer == 0 else (c_mid if p.ctx else x_mid)
                rows = slice(b * p.BW, (b + 1) * p.BW)
                src, dst = (m[rows, :].rearrange("(t p) n -> p t n", p=P) for m in (src, dst))
                for half in range(2):
                    split_high(8)
                    eng.wait_ge(sem["w_used"], tally.take("w_used__done", 8))
                    if half == 0:
                        eng.wait_ge(sem["gate"], tally.now("gate"))
                        eng.dma_start(x_post[:, 0:p.TB, :], src).then_inc(sem["post_in"], tally.up("post_in", 16))
                        eng.dma_start(gp_blk[b][:, :], gate_rows[p.layer, p.s:p.s + 1, :].partition_broadcast(P)
                             .rearrange("p a n -> p (a n)")).then_inc(sem["post_in"], tally.up("post_in", 16))
                    for t in range(p.TB):
                        if tally.now("out_square"):
                            eng.wait_ge(sem["out_square"], tally.now("out_square"))
                        eng.wait_ge(sem["y_out"], tally.take("y_out"))
                        act(sq_junk[:, :], y_post[:, t, half * 512:(half + 1) * 512], ACT.Square,
                                 accum_out=stat[:, 0, 4 * half + t:4 * half + t + 1]).then_inc(sem["out_square"], tally.up("out_square"))
                eng.wait_ge(sem["out_mean"], tally.take("out_mean"))
                act(stat[:, 2, 0:p.TB], stat[:, 1, 0:p.TB], ACT.Sqrt).then_inc(sem["out_root"], tally.up("out_root"))
                for t in range(p.TB):
                    eng.wait_ge(sem["x_new"], tally.take("x_new"))
                    eng.dma_start(dst[:, t, :], x_post[:, t, :]).then_inc(sem["x_out"], tally.up("x_out", 16))
                eng.wait_ge(sem["x_out"], tally.now("x_out"))

            constants()
            stage_end(eng, tally, "act")
            for p in passes:
                if p.ctx:
                    modulation(p.layer)
                    stage_end(eng, tally, "act")
                norm(p)
                stage_end(eng, tally, "act")
                if not p.full:
                    tile_range(p, A_K, A_Z)
                    tile_range(p, R_K, R_Z)
                    stage_end(eng, tally, "act")
                    states(p)
                    stage_end(eng, tally, "act")
                    continue
                if not p.ctx:
                    eng.dma_start(rope[:, :, :], a["rope"]).then_inc(sem["rope_in"], tally.up("rope_in", 16))
                tile_range(p, A_Q, B_U)
                stage_end(eng, tally, "act")
                attention(p)
                stage_end(eng, tally, "act")
                tile_range(p, B_U, R_Q)
                stage_end(eng, tally, "act")
                tile_range(p, R_Q, F_U)
                stage_end(eng, tally, "act")
                decay_tables()
                states(p)
                retention(p)
                stage_end(eng, tally, "act")
                eng.dma_start(f_bd[:, :], a["dft_head"][p.s].rearrange("p c n -> p (c n)")).then_inc(sem["head_in"], tally.up("head_in", 16))
                tile_range(p, F_U, F_Z)
                fourier(p)
                tile_range(p, F_Z, MERGE)
                stage_end(eng, tally, "act")
                for b in range(p.NB):
                    merge(p, b)
                    stage_end(eng, tally, "act")

        @block.vector
        def _(eng):
            tally = Count(eng)
            eng.sem_inc(sem["hT_pre"], tally.up("hT_pre", 4))
            eng.sem_inc(sem["raw_free"], tally.up("raw_free", 2))
            eng.sem_inc(sem["pv_free"], tally.up("pv_free", 2))
            eng.sem_inc(sem["four_done"], tally.up("four_done", 2))
            eng.sem_inc(sem["opart_free"], tally.up("opart_free", 2))
            tally.skip("prob", 2)
            tally.skip("w_used__done", RING)
            tally.skip("gate", 2)
            tally.skip("probT_saved", 1)
            tally.skip("inc_saved", 2)
            tally.skip("ret_y_saved", 2)

            def tt(dst, x, y, op=ALU.mult):
                return eng.tensor_tensor(dst, x, y, op)

            def constants():
                eng.memset(ones[:, :], 1.0).then_inc(sem["dve_own"], tally.up("dve_own"))
                eng.wait_ge(sem["const_in"], tally.take("const_in", 48))
                eng.tensor_copy(ident_bf[:, :], ident[:, :]).then_inc(sem["dve_own"], tally.up("dve_own"))
                eng.tensor_copy(mask_bf[:, :, :], m_mask[:, :, :]).then_inc(sem["dve_own"], tally.up("dve_own"))
                eng.wait_ge(sem["dve_own"], tally.now("dve_own"))

            def modulation(l):
                eng.sem_inc(sem["mod_saved"], tally.up("mod_saved", 2))
                eng.wait_ge(sem["silu_c"], tally.take("silu_c"))
                eng.tensor_copy(sT_hi[:, :, :], sT[:, :, :]).then_inc(sem["dve_own"], tally.up("dve_own"))
                eng.wait_ge(sem["dve_own"], tally.now("dve_own"))
                tt(sT_lo[:, :, :], sT[:, :, :], sT_hi[:, :, :].bitcast(F32), ALU.subtract).then_inc(sem["dve_own"], tally.up("dve_own"))
                eng.wait_ge(sem["dve_own"], tally.now("dve_own"))
                hi, lo = sT_hi[:, :, :].bitcast(F32), sT_lo[:, :, :].bitcast(F32)
                for which, g, src in ((0, 0, hi), (0, 1, hi), (0, 2, lo), (0, 3, lo), (1, 0, hi), (1, 1, hi)):
                    eng.tensor_copy(m_lhs[:, which, :, g, :],
                                         src[:, g % 2, :].unsqueeze(2).to_broadcast([P, KT, 32])).then_inc(sem["dve_own"], tally.up("dve_own"))
                for g in (2, 3):
                    ins = eng.tensor_scalar(m_lhs[:, 1, :, g, :], hi[:, 0, :].unsqueeze(2).to_broadcast([P, KT, 32]),
                                            0.0, None, ALU.mult)
                    ins.then_inc(sem["mod_lhs"], tally.up("mod_lhs")) if g == 3 else ins.then_inc(sem["dve_own"], tally.up("dve_own"))
                eng.wait_ge(sem["small_in"], tally.take("small_in", 16 * 7))
                eng.tensor_scalar(sink[:, 1, :], sink[:, 0, :], -1.0, None, ALU.mult).then_inc(sem["dve_own"], tally.up("dve_own"))
                eng.wait_ge(sem["dve_own"], tally.now("dve_own"))
                eng.tensor_scalar(lt[:, 1, :], decay[:, :], -1.0, None, ALU.mult).then_inc(sem["dve_own"], tally.up("dve_own"))
                eng.wait_ge(sem["dve_own"], tally.now("dve_own"))
                tt(lt[:, 0, :], decay[:, :], lt[:, 1, :], ALU.max).then_inc(sem["log_one"], tally.up("log_one"))
                eng.wait_ge(sem["log_exp"], tally.take("log_exp"))
                eng.tensor_scalar(lt[:, 2, :], lt[:, 1, :], 1.0, None, ALU.add).then_inc(sem["log_one"], tally.up("log_one"))
                eng.wait_ge(sem["log_one"], tally.now("log_one"))
                eng.tensor_scalar(lt[:, 4, :], lt[:, 2, :], -1.0, None, ALU.add).then_inc(sem["dve_own"], tally.up("dve_own"))
                eng.wait_ge(sem["dve_own"], tally.now("dve_own"))
                tt(lt[:, 4, :], lt[:, 1, :], lt[:, 4, :], ALU.subtract).then_inc(sem["dve_own"], tally.up("dve_own"))
                eng.wait_ge(sem["dve_own"], tally.now("dve_own"))
                eng.reciprocal(lt[:, 5, :], lt[:, 2, :]).then_inc(sem["dve_own"], tally.up("dve_own"))
                eng.wait_ge(sem["dve_own"], tally.now("dve_own"))
                tt(lt[:, 4, :], lt[:, 4, :], lt[:, 5, :]).then_inc(sem["dve_own"], tally.up("dve_own"))
                eng.wait_ge(sem["dve_own"], tally.now("dve_own"))
                eng.wait_ge(sem["log_ln"], tally.take("log_ln"))
                tt(lt[:, 4, :], lt[:, 4, :], lt[:, 3, :], ALU.add).then_inc(sem["dve_own"], tally.up("dve_own"))
                eng.wait_ge(sem["dve_own"], tally.now("dve_own"))
                eng.tensor_scalar(lt[:, 5, :], decay[:, :], 0.0, None, ALU.min).then_inc(sem["dve_own"], tally.up("dve_own"))
                eng.wait_ge(sem["dve_own"], tally.now("dve_own"))
                tt(lg[:, :], lt[:, 5, :], lt[:, 4, :], ALU.subtract).then_inc(sem["dve_own"], tally.up("dve_own"))
                eng.wait_ge(sem["dve_own"], tally.now("dve_own"))
                eng.tensor_copy(lgd[0:HD, :], lg[0:HD, 0:RH]).then_inc(sem["dve_own"], tally.up("dve_own"))
                eng.wait_ge(sem["dve_own"], tally.now("dve_own"))
                eng.tensor_copy(lgd[HD:P, :], lg[HD:P, RH:2 * RH]).then_inc(sem["log_gamma"], tally.up("log_gamma"))
                eng.wait_ge(sem["zeta_exp"], tally.take("zeta_exp"))
                eng.tensor_scalar(zeta[:, :, :], zeta[:, :, :], SCALE, None, ALU.mult).then_inc(sem["dve_own"], tally.up("dve_own"))
                for n in range(6):
                    eng.wait_ge(sem["w_used"], tally.take("w_used__done", KT))
                    eng.tensor_copy(m_rows[:, n * 512:(n + 1) * 512], ps[:, n % 2, :]).then_inc(sem["mod_saved"], tally.up("mod_saved"))
                eng.wait_ge(sem["mod_cols"], tally.take("mod_cols"))
                cols = ps[:, 2, 0:4 * KT].rearrange("p (k s) -> p k s", s=2)
                for s in range(2):
                    eng.tensor_copy(mod[:, s, 1, :], cols[:, 0:KT, s]).then_inc(sem["dve_own"], tally.up("dve_own"))
                    eng.scalar_tensor_tensor(mod[:, s, 0, :], cols[:, KT:2 * KT, s], 1.0, gpre[:, :],
                                                  ALU.add, ALU.mult).then_inc(sem["dve_own"], tally.up("dve_own"))
                eng.wait_ge(sem["mod_gate"], tally.take("mod_gate"))
                for h in range(2):
                    c = slice(h * 512, (h + 1) * 512)
                    tt(m_gate[0:2, c], ps[0:2, 3 + h, :], m_gpost[0:2, c]).then_inc(sem["gate_made"], tally.up("gate_made"))
                eng.wait_ge(sem["dve_own"], tally.now("dve_own"))

            def norm(p):
                for b in range(p.NB):
                    at_ = slice(b * p.TB, (b + 1) * p.TB)
                    eng.wait_ge(sem["square"], tally.take("square", p.TB))
                    eng.tensor_scalar(stat[:, 1, at_], stat[:, 0, at_], 1.0 / D, EPS, ALU.mult, ALU.add).then_inc(sem["mean"], tally.up("mean"))
                    eng.wait_ge(sem["root"], tally.take("root"))
                    eng.reciprocal(stat[:, 0, at_], stat[:, 2, at_]).then_inc(sem["dve_own"], tally.up("dve_own"))
                    eng.wait_ge(sem["dve_own"], tally.now("dve_own"))
                    for t in range(b * p.TB, (b + 1) * p.TB):
                        eng.tensor_scalar(x_tile[:, t, :], x_tile[:, t, :], stat[:, 0, t:t + 1], None, ALU.mult).then_inc(sem["normed"], tally.up("normed"))

                    def low(k):
                        eng.wait_ge(sem["hT_high"], tally.take("hT_high"))
                        c = slice(b * p.BW, (b + 1) * p.BW)
                        tt(hT[1][:, k, c], n_tmp[:, k % 2, 0:p.BW], hT[0][:, k, c].bitcast(F32), ALU.subtract).then_inc(sem["dve_own"], tally.up("dve_own"))
                    for k in range(KT):
                        eng.wait_ge(sem["turned"], tally.take("turned"))
                        eng.wait_ge(sem["dve_own"], tally.now("dve_own"))
                        eng.tensor_scalar(n_tmp[:, k % 2, 0:p.BW], ps[:, k % 4, 0:p.BW], mod[:, p.s, 0, k:k + 1],
                                               mod[:, p.s, 1, k:k + 1], ALU.mult, ALU.add).then_inc(sem["hT_pre"], tally.up("hT_pre"))
                        if k:
                            low(k - 1)
                    low(KT - 1)

            def placed(p, t):
                eng.wait_ge(sem["proj_out"], 2 + tile_no[p.n, t] + 1)

            def to(p, t, outs):
                src = buf[raw_no[p.n, t] % 2]
                placed(p, t)
                if not p.ctx:
                    eng.wait_ge(sem["raw_free"], tally.now("raw_free"))
                    eng.stream_shuffle(turned[:, 0:p.T], src[:, 0:p.T], [(i + 16) % 32 for i in range(32)]).then_inc(sem["dve_own"], tally.up("dve_own"))
                    eng.wait_ge(sem["dve_own"], tally.now("dve_own"))
                    tt(src[:, 0:p.T], src[:, 0:p.T], rope[:, 0, :]).then_inc(sem["dve_own"], tally.up("dve_own"))
                    tt(turned[:, 0:p.T], turned[:, 0:p.T], rope[:, 1, :]).then_inc(sem["dve_own"], tally.up("dve_own"))
                    eng.wait_ge(sem["dve_own"], tally.now("dve_own"))
                for n, (dst, row, rows) in enumerate(outs):
                    x = src[row:row + rows, 0:p.T]
                    ins = eng.tensor_copy(dst, x) if p.ctx else tt(dst, x, turned[row:row + rows, 0:p.T], ALU.add)
                    ins.then_inc(sem["raw_free"], tally.up("raw_free")) if n == len(outs) - 1 else ins.then_inc(sem["dve_own"], tally.up("dve_own"))

            def save_values(p, dst):
                eng.wait_ge(sem["v_turned"], tally.take("v_turned"))
                if p.NT == 8:
                    eng.tensor_copy(dst[:, 0:4, :], ps[:, 4, :].rearrange("p (n d) -> p n d", d=P)).then_inc(sem["dve_own"], tally.up("dve_own"))
                n0 = p.NT - p.NT // p.NB
                eng.tensor_copy(dst[:, n0:p.NT, :], ps[:, 3 + p.NB, 0:(p.NT - n0) * P]
                                     .rearrange("p (n d) -> p n d", d=P)).then_inc(sem["raw_free"], tally.up("raw_free"))

            def halves(first, second):
                return [(place[r:r + HD], row, HD) for place, row in ((first, 0), (second, HD)) for r in (0, HD)]

            def a_keys(p):
                k = kd_c if p.ctx else kd
                to(p, A_K, halves(k[:, 0, 0:p.T], k[:, 1, 0:p.T]))
                save_values(p, v_c if p.ctx else v_x)

            def r_keys(p):
                for j in range(2):
                    to(p, R_K + j, [(rk[:, j, 0:p.T], 0, P)])
                for j in range(2):
                    save_values(p, rv[:, 0:p.NT, j, :])

            def attention(p):
                steps = [(qb, h) for qb in range(p.NT) for h in range(HEADS)]

                def width(qb):
                    return 0 if p.ctx else (3 - (qb == 0) - (qb == p.NT - 1)) * P

                def maximum(n):
                    qb, h = steps[n]
                    L, c, s = width(qb), 2 * (n % 2), n % 2
                    eng.wait_ge(sem["score"], tally.take("score"))
                    view = ps[:, c:c + 2, :].rearrange("p a n -> p (a n)")[:, 512 - L:512 + CTX]
                    eng.tensor_reduce(soft[:, s, 0:1], view, AX.X, ALU.max).then_inc(sem["dve_own"], tally.up("dve_own"))
                    eng.wait_ge(sem["dve_own"], tally.now("dve_own"))
                    eng.tensor_scalar(soft[:, s, 1:2], soft[:, s, 0:1], -SCALE, sink[:, 1, h:h + 1],
                                           ALU.mult, ALU.min).then_inc(sem["max"], tally.up("max"))

                def scale(n):
                    qb, h = steps[n]
                    s, w = n % 2, width(qb) + CTX
                    eng.wait_ge(sem["prob"], tally.take("prob"))
                    tt(soft[:, s, 4:5], soft[:, s, 2:3], soft[:, s, 3:4], ALU.add).then_inc(sem["dve_own"], tally.up("dve_own"))
                    eng.wait_ge(sem["dve_own"], tally.now("dve_own"))
                    eng.reciprocal(soft[:, s, 5:6], soft[:, s, 4:5]).then_inc(sem["dve_own"], tally.up("dve_own"))
                    eng.wait_ge(sem["dve_own"], tally.now("dve_own"))
                    eng.tensor_scalar(prob[:, s, 0:w], prob[:, s, 0:w], soft[:, s, 5:6], None, ALU.mult).then_inc(sem["prob_scaled"], tally.up("prob_scaled"))

                def gated(n):
                    qb, h = steps[n]
                    kv = h // 4
                    eng.wait_ge(sem["pv"], tally.take("pv"))
                    for half in range(2):
                        rows = slice(half * HD, half * HD + HD)
                        zz = z_pass[p.s][rows, qb // p.TB, 2 * kv:2 * kv + 2, (qb % p.TB) * P:(qb % p.TB + 1) * P]
                        o = ps[0:HD, 6 + kv, :].rearrange("p (t h n) -> p t h n", t=2, h=2)[:, :, half, :]
                        ins = tt(zz, o, zz)
                        ins.then_inc(sem["pv_free"], tally.up("pv_free")) if half else ins.then_inc(sem["dve_own"], tally.up("dve_own"))

                maximum(0)
                for n in range(len(steps)):
                    if n + 1 < len(steps):
                        maximum(n + 1)
                    scale(n)
                    if n % 4 == 1 and n > 4:
                        gated(n - 2)
                gated(len(steps) - 1)

            def convolution(p):
                for j in range(2):
                    src = buf[raw_no[p.n, B_C + j] % 2]
                    placed(p, B_C + j)
                    eng.memset(c_cu[:, j, 1:2], 0.0).then_inc(sem["dve_own"], tally.up("dve_own"))
                    eng.memset(c_cu[:, j, 2 + p.T:3 + p.T], 0.0).then_inc(sem["dve_own"], tally.up("dve_own"))
                    tt(c_cu[:, j, 2:2 + p.T], src[:, 0:p.T], c_u[:, j, 0:p.T]).then_inc(sem["raw_free"], tally.up("raw_free"))
                    eng.wait_ge(sem["raw_free"], tally.now("raw_free"))
                    eng.wait_ge(sem["dve_own"], tally.now("dve_own"))
                    y, u = c_y[:, j, 0:p.T], c_cu[:, j, :]
                    eng.tensor_scalar(y, u[:, 1:1 + p.T], convw[:, j, 0:1], convw[:, j, 3:4], ALU.mult, ALU.add).then_inc(sem["dve_own"], tally.up("dve_own"))
                    eng.wait_ge(sem["dve_own"], tally.now("dve_own"))
                    eng.scalar_tensor_tensor(y, u[:, 2:2 + p.T], convw[:, j, 1:2], y, ALU.mult, ALU.add).then_inc(sem["dve_own"], tally.up("dve_own"))
                    eng.wait_ge(sem["dve_own"], tally.now("dve_own"))
                    eng.scalar_tensor_tensor(y, u[:, 3:3 + p.T], convw[:, j, 2:3], y, ALU.mult, ALU.add).then_inc(sem["dve_own"], tally.up("dve_own"))
                    eng.wait_ge(sem["dve_own"], tally.now("dve_own"))
                    tt(y, y, c_b[:, j, 0:p.T]).then_inc(sem["dve_own"], tally.up("dve_own"))
                    eng.wait_ge(sem["dve_own"], tally.now("dve_own"))
                for j in range(2):
                    placed(p, B_Z + j)
                    zz = z_tile(p, Z_B + j)[:, :, 0, :]
                    tt(zz, zz, c_y[:, j, 0:p.T].rearrange("p (b n) -> p b n", b=p.NB)).then_inc(sem["dve_own"], tally.up("dve_own"))

            def decay_tables():
                for h in range(RH):
                    eng.wait_ge(sem["ret_exp"], tally.take("ret_exp"))
                    tt(r_e[:, 0, :], r_e[:, 0, :], r_tab[:, 1, :]).then_inc(sem["dve_own"], tally.up("dve_own"))
                    eng.wait_ge(sem["dve_own"], tally.now("dve_own"))
                    tt(r_e[:, 1, :], r_e[:, 1, :], r_tab[:, 3, :]).then_inc(sem["dve_own"], tally.up("dve_own"))
                    eng.wait_ge(sem["dve_own"], tally.now("dve_own"))
                    tt(dt_[:, h, :], r_e[:, 0, :], r_e[:, 1, :], ALU.add).then_inc(sem["ret_tab"], tally.up("ret_tab"))
                eng.wait_ge(sem["ret_tab"], tally.now("ret_tab"))

            def states(p):
                for n in range(p.NT):
                    eng.wait_ge(sem["k_turned"], tally.take("k_turned"))
                    k = ps[:, 4 + n % 2, 0:RH * HD].rearrange("p (h d) -> p h d", h=RH)
                    for d in range(2):
                        ins = tt(r_kz[:, n % 2, :, d, :], k, zeta[:, d, :].unsqueeze(2).to_broadcast([P, RH, HD]))
                        ins.then_inc(sem["kz"], tally.up("kz")) if d else ins.then_inc(sem["dve_own"], tally.up("dve_own"))
                eng.wait_ge(sem["inc_saved"], tally.take("inc_saved", p.NT))
                order = [list(range(p.NT)), list(range(p.NT))[::-1]]
                rows = [slice(0, HD), slice(HD, P)]
                for d in range(2):
                    dst = r_prev[rows[d], order[d][0], :, :]
                    (eng.memset(dst, 0.0) if p.ctx else eng.tensor_copy(dst, state_c[rows[d], :, :])).then_inc(sem["dve_own"], tally.up("dve_own"))
                eng.wait_ge(sem["dve_own"], tally.now("dve_own"))
                for s in range(p.NT if p.ctx else p.NT - 1):
                    new = [r_prev[rows[d], order[d][s + 1], :, :] if s + 1 < p.NT else state_c[rows[d], :, :]
                           for d in range(2)]
                    for d in range(2):
                        g = gch[rows[d], :].unsqueeze(2).to_broadcast([HD, RH, HD])
                        tt(new[d], r_prev[rows[d], order[d][s], :, :], g).then_inc(sem["dve_own"], tally.up("dve_own"))
                    eng.wait_ge(sem["dve_own"], tally.now("dve_own"))
                    for d in range(2):
                        tt(new[d], new[d], r_inc[rows[d], order[d][s], :, :], ALU.add).then_inc(sem["dve_own"], tally.up("dve_own"))
                    eng.wait_ge(sem["dve_own"], tally.now("dve_own"))

            def retention(p):
                for n in range(p.NT):
                    c = slice(n * P, (n + 1) * P)
                    eng.wait_ge(sem["ret_y"], tally.take("ret_y"))
                    tt(r_qx[:, n % 2, :, :], qd[:, :, c], xi[:, :, :]).then_inc(sem["dve_own"], tally.up("dve_own"))
                    eng.wait_ge(sem["sT"], tally.take("sT"))
                    for h in range(2):
                        ins = tt(r_sc[:, n % 2, h::2, :],
                                 ps[:, n % 2 + 4 * h, 0:2 * P].rearrange("p (j n) -> p j n", j=2), dt_[:, h::2, :])
                        ins.then_inc(sem["sc"], tally.up("sc")) if h else ins.then_inc(sem["dve_own"], tally.up("dve_own"))
                m = p.NT * RH
                y = r_y[:, 0:p.NT, :, :].rearrange("p c h d -> p (c h) d")
                sq = r_sq[:, 0:p.NT, :, :].rearrange("p c h d -> p (c h) d")

                def spread(i):
                    return r_stat[:, i, 0:m].unsqueeze(2).to_broadcast([P, m, HD])
                eng.wait_ge(sem["ret_y_saved"], tally.take("ret_y_saved", p.NT))
                eng.tensor_reduce(r_stat[:, 0, 0:m], y, AX.X, ALU.add).then_inc(sem["dve_own"], tally.up("dve_own"))
                eng.wait_ge(sem["dve_own"], tally.now("dve_own"))
                eng.tensor_scalar(r_stat[:, 0, 0:m], r_stat[:, 0, 0:m], 1.0 / HD, None, ALU.mult).then_inc(sem["dve_own"], tally.up("dve_own"))
                eng.wait_ge(sem["dve_own"], tally.now("dve_own"))
                tt(y, y, spread(0), ALU.subtract).then_inc(sem["ret_mean"], tally.up("ret_mean"))
                eng.wait_ge(sem["ret_square"], tally.take("ret_square"))
                eng.tensor_reduce(r_stat[:, 3, 0:m], sq, AX.X, ALU.add).then_inc(sem["dve_own"], tally.up("dve_own"))
                eng.wait_ge(sem["dve_own"], tally.now("dve_own"))
                eng.tensor_scalar(r_stat[:, 1, 0:m], r_stat[:, 3, 0:m], 1.0 / HD, EPS, ALU.mult, ALU.add).then_inc(sem["ret_var"], tally.up("ret_var"))
                eng.wait_ge(sem["ret_root"], tally.take("ret_root"))
                eng.reciprocal(r_stat[:, 0, 0:m], r_stat[:, 2, 0:m]).then_inc(sem["dve_own"], tally.up("dve_own"))
                eng.wait_ge(sem["dve_own"], tally.now("dve_own"))
                tt(y, y, spread(0)).then_inc(sem["ret_norm"], tally.up("ret_norm"))
                for j in range(2):
                    for b in range(p.NB):
                        eng.wait_ge(sem["ret_yT"], tally.take("ret_yT"))
                        zz = z_pass[p.s][:, b, Z_R + j, :]
                        tt(zz, ps[:, 4 + 2 * j + b, 0:p.BW], zz).then_inc(sem["dve_own"], tally.up("dve_own"))

            def fourier(p):
                for n in range(p.NT):
                    eng.wait_ge(sem["four_hi"], tally.take("four_hi"))
                    tt(f_ab[1][:, n, :, :, :].rearrange("p j c n -> p (j c n)"), ps[:, 4 + n % 2, :],
                            f_ab[0][:, n, :, :, :].bitcast(F32).rearrange("p j c n -> p (j c n)"), ALU.subtract).then_inc(sem["four_done"], tally.up("four_done"))
                placed(p, F_Z + 1)
                eng.wait_ge(sem["w_used"], tally.now("w_used__done", units_of(p)[0]))
                for half in range(p.NB):
                    for j in range(2):
                        zz = z_pass[p.s][:, half, Z_F + j, :]
                        tt(zz, ps[:, 4 + 2 * half + j, 0:p.BW], zz).then_inc(sem["dve_own"], tally.up("dve_own"))

            def units_of(p):
                return 2 * F_Z + (2 if p.ctx else 32), 2 * MERGE + (2 if p.ctx else 32)

            def merge(p, b):
                tmp = tmp_blk[b]
                for tile, count in BRANCH:
                    eng.wait_ge(sem["y_hi"], tally.take("y_hi"))
                    tt(yT[1][1][:, tile:tile + count, 0:p.BW], z_pass[p.s][:, b, tile:tile + count, :],
                            yT[1][0][:, tile:tile + count, 0:p.BW].bitcast(F32), ALU.subtract).then_inc(sem["y_split"], tally.up("y_split"))
                eng.wait_ge(sem["y_split"], tally.now("y_split"))
                acc = tmp[:, 2, 0:p.BW]

                def body(i):
                    for j in range(4):
                        eng.wait_ge(sem["gate"], tally.take("gate"))
                        eng.wait_ge(sem["w_used"], tally.take("w_used__done", 3))
                        g, o = tmp[:, j % 2, 0:p.BW], ps[:, 2 + j % 2, 0:p.BW]
                        eng.wait_ge(sem["dve_own"], tally.now("dve_own"))
                        if j == 0:
                            tt(acc, g, o).then_inc(sem["opart_free"], tally.up("opart_free"))
                        else:
                            t = tmp[:, 3, 0:p.BW]
                            tt(t, g, o).then_inc(sem["opart_free"], tally.up("opart_free"))
                            eng.wait_ge(sem["opart_free"], tally.now("opart_free"))
                            tt(acc, acc, t, ALU.add).then_inc(sem["dve_own"], tally.up("dve_own"))
                    eng.wait_ge(sem["dve_own"], tally.now("dve_own"))
                    eng.tensor_copy(tot[0][:, bass.ds(i, 1), 0:p.BW], acc.unsqueeze(1)).then_inc(sem["dve_own"], tally.up("dve_own"))
                    eng.wait_ge(sem["dve_own"], tally.now("dve_own"))
                    tt(tot[1][:, bass.ds(i, 1), 0:p.BW], acc.unsqueeze(1),
                            tot[0][:, bass.ds(i, 1), 0:p.BW].bitcast(F32), ALU.subtract).then_inc(sem["tot_done"], tally.up("tot_done"))
                    eng.wait_ge(sem["tot_done"], tally.now("tot_done"))
                tally.loop(KT, body, gate=4, w_used__done=12, opart_free=4, dve_own=4, tot_done=1)
                for half in range(2):
                    eng.wait_ge(sem["w_used"], tally.take("w_used__done", KT))
                    for t in range(p.TB):
                        eng.tensor_copy(y_post[:, t, half * 512:(half + 1) * 512], ps[:, 4 - 4 * half + t, :]).then_inc(sem["y_out"], tally.up("y_out"))
                eng.wait_ge(sem["out_square"], tally.take("out_square", 2 * p.TB))
                eng.wait_ge(sem["y_out"], tally.now("y_out"))
                tt(stat[:, 1, 4:4 + p.TB], stat[:, 0, 0:p.TB], stat[:, 0, 4:4 + p.TB], ALU.add).then_inc(sem["dve_own"], tally.up("dve_own"))
                eng.wait_ge(sem["dve_own"], tally.now("dve_own"))
                eng.tensor_scalar(stat[:, 1, 0:p.TB], stat[:, 1, 4:4 + p.TB], 1.0 / D, EPS, ALU.mult, ALU.add).then_inc(sem["out_mean"], tally.up("out_mean"))
                eng.wait_ge(sem["out_root"], tally.take("out_root"))
                eng.reciprocal(stat[:, 1, 0:p.TB], stat[:, 2, 0:p.TB]).then_inc(sem["dve_own"], tally.up("dve_own"))
                eng.wait_ge(sem["dve_own"], tally.now("dve_own"))
                eng.wait_ge(sem["post_in"], tally.take("post_in", 32))
                for t in range(p.TB):
                    eng.scalar_tensor_tensor(y_post[:, t, :], y_post[:, t, :], stat[:, 1, t:t + 1], gp_blk[b][:, :], ALU.mult, ALU.mult).then_inc(sem["dve_own"], tally.up("dve_own"))
                    eng.wait_ge(sem["dve_own"], tally.now("dve_own"))
                    tt(x_post[:, t, :], x_post[:, t, :], y_post[:, t, :], ALU.add).then_inc(sem["x_new"], tally.up("x_new"))

            constants()
            stage_end(eng, tally, "dve")
            for p in passes:
                if p.ctx:
                    modulation(p.layer)
                    stage_end(eng, tally, "dve")
                norm(p)
                stage_end(eng, tally, "dve")
                if not p.full:
                    a_keys(p)
                    r_keys(p)
                    tally.skip("w_used__done", 2 * len(p.tiles))
                    stage_end(eng, tally, "dve")
                    states(p)
                    stage_end(eng, tally, "dve")
                    continue
                if not p.ctx:
                    eng.wait_ge(sem["rope_in"], tally.take("rope_in", 16))
                for t in range(4):
                    to(p, A_Q + t, [(qT[:, t, 0:p.T], 0, P)])
                a_keys(p)
                stage_end(eng, tally, "dve")
                attention(p)
                stage_end(eng, tally, "dve")
                convolution(p)
                stage_end(eng, tally, "dve")
                for j in range(2):
                    to(p, R_Q + j, halves(qd[:, 2 * j, 0:p.T], qd[:, 2 * j + 1, 0:p.T]))
                r_keys(p)
                stage_end(eng, tally, "dve")
                decay_tables()
                states(p)
                retention(p)
                stage_end(eng, tally, "dve")
                fourier(p)
                tally.skip("w_used__done", units_of(p)[1])
                stage_end(eng, tally, "dve")
                for b in range(p.NB):
                    merge(p, b)
                    stage_end(eng, tally, "dve")


INPUTS = ("x", "ctx", "w_ada", "b_ada", "norm_post", "w_in", "attn_sink", "ret_decay", "w_o_attn", "w_out")
TABLES = ("rope", "dft_x", "dft_c", "dft_head", "mask", "ident", "ret", "small")


def kernel(**inputs):
    import concourse.bacc as bacc
    from concourse.bass_utils import run_bass_kernel_spmd

    nc = bacc.Bacc("TRN2", target_bir_lowering=False, num_devices=1)
    arrays = {n: np.ascontiguousarray(inputs[n]) for n in INPUTS}
    arrays["w_o_rest"] = np.concatenate([inputs["w_o_conv"], inputs["w_o_ret"], inputs["w_o_fourier"]], axis=1)
    arrays["c_cols"] = np.stack([np.reshape(inputs["c"], (KT, P)), np.reshape(inputs["c_ctx"], (KT, P))]).transpose(2, 0, 1)
    arrays["norm_pre_cols"] = np.reshape(inputs["norm_pre"], (DEPTH, KT, P)).transpose(0, 2, 1)
    conv = np.concatenate([inputs["conv_w"], np.asarray(inputs["conv_b"])[:, None, :]], axis=1)
    arrays["conv_cols"] = conv.reshape(DEPTH, 4, 2, P).transpose(0, 3, 2, 1)
    arrays = {n: np.ascontiguousarray(v) for n, v in arrays.items()}
    arrays.update(tables())
    arrays = {f"in_{n}": v for n, v in arrays.items()}
    aps = {n[3:]: nc.dram_tensor(n, v.shape, mybir.dt.from_np(v.dtype), kind="ExternalInput").ap()
           for n, v in arrays.items()}
    out = nc.dram_tensor("out", (1, SEQ, D), F32, kind="ExternalOutput").ap()
    trunk(nc, aps, out)
    return run_bass_kernel_spmd(nc, [arrays], core_ids=[0]).results[0]["out"]
```

```python
from contextlib import ExitStack

import concourse.bass as bass
from concourse import mybir
import numpy as np

F32 = mybir.dt.float32
F32R = mybir.dt.float32r
BF16 = mybir.dt.bfloat16
ALU = mybir.AluOpType
ACT = mybir.ActivationFunctionType
AX = mybir.AxisListType

P = 128
D = 1024
KT = D // P
SEQ = 1024
CTX = 256
DEPTH = 2
GRID_W = 64
HD = 64
EPS = 1e-6
NEG = -1e30
HEADS = 8
RH = 4
SCALE = HD ** -0.5
UNIT = 512
RING = 4
LOOK = 3
ADA_AHEAD = 5
SBUF_START = 16512

A_Q, A_K, A_V, A_Z, B_U, B_B, B_C, B_Z, R_Q, R_K, R_V, R_Z, F_U, F_Z, MERGE = (
    0, 4, 5, 6, 10, 12, 14, 16, 18, 20, 22, 24, 26, 28, 30)
Z_A, Z_B, Z_R, Z_F, ZT = 0, 4, 6, 8, 10
BRANCH = ((Z_A, 4), (Z_B, 2), (Z_R, 2), (Z_F, 2))


class Pass:

    def __init__(self, layer, ctx, full):
        self.layer, self.ctx, self.full = layer, ctx, full
        self.s = 1 if ctx else 0
        self.T = CTX if ctx else SEQ
        self.BW = min(512, self.T)
        self.NB = self.T // self.BW
        self.NT = self.T // P
        self.TB = self.BW // P


class Count:

    def __init__(self, eng):
        self.eng, self.n, self.i, self.per = eng, {}, None, {}

    def now(self, name, more=0):
        v = self.n.get(name, 0) + more
        if self.i is not None and self.per.get(name):
            return self.i * self.per[name] + v
        return v

    def take(self, name, by=1):
        self.n[name] = self.n.get(name, 0) + by
        return self.now(name)

    def up(self, name, by=1):
        self.n[name] = self.n.get(name, 0) + by
        return by

    def skip(self, name, by):
        self.n[name] = self.n.get(name, 0) + by

    def loop(self, times, body, **per):
        before = dict(self.n)
        with self.eng.Fori(0, times) as i:
            self.i, self.per = i, per
            body(i)
            self.i, self.per = None, {}
        for name in self.n:
            made = self.n[name] - before.get(name, 0)
            assert made == per.get(name, 0), (name, made, per.get(name, 0))
            self.n[name] = before.get(name, 0) + times * made


def tables():
    out = {}
    n = np.arange(SEQ)
    half = HD // 2
    inv = (10000.0 ** (-np.arange(0, half, 2, dtype=np.float64) / half)).astype(np.float32)
    pos = np.stack([n // GRID_W, n % GRID_W]).astype(np.float32)
    p = np.arange(P) % HD
    axis, r = p // 32, p % 32
    ang = (pos[axis] * inv[r % 16][:, None]).astype(np.float64)
    sign = np.where(r < 16, -1.0, 1.0)[:, None]
    out["rope"] = np.stack([np.cos(ang), sign * np.sin(ang)], 1).astype(np.float32)
    for size, name in ((SEQ, "dft_x"), (CTX, "dft_c")):
        k = np.arange(size)
        a = 2 * np.pi * (np.outer(k, k) % size) / size
        out[name] = np.stack([np.cos(a), np.sin(a)]).astype(np.float32)
    k = np.arange(HD)
    a = 2 * np.pi * (np.outer(k, k) % HD) / HD
    bd = np.zeros((2, P, 2, P), np.float64)
    for s, size in enumerate((SEQ, CTX)):
        norm = (size * HD) ** -0.5
        for g in range(2):
            bd[s, g * HD:(g + 1) * HD, 0, g * HD:(g + 1) * HD] = np.cos(a) * norm
            bd[s, g * HD:(g + 1) * HD, 1, g * HD:(g + 1) * HD] = -np.sin(a) * norm
    out["dft_head"] = bd.astype(np.float32)
    i, j = np.arange(P)[:, None], np.arange(P)[None, :]
    out["mask"] = np.stack([np.where(j >= i, 0, NEG), np.where(j <= i, 0, NEG)], 1).astype(np.float32)
    out["ident"] = np.eye(P, dtype=np.float32)
    xidx = np.where(i < HD, j + 1, P - j)
    out["ret"] = np.stack([np.maximum(j - i, 0), SCALE * (j >= i), np.maximum(i - j, 0), SCALE * (i >= j), xidx], 1).astype(np.float32)
    sel = np.zeros((P, 2), np.float32)
    sel[[0, 64], 0] = 1
    sel[[32, 96], 1] = 1
    small = np.concatenate([sel, (P - 1 - i).astype(np.float32), i.astype(np.float32)], 1)
    out["small"] = small
    return out


def trunk(nc, a, out):
    with ExitStack() as ctx:
        def at(name, shape, offset, dt=F32):
            words = int(np.prod(shape[1:])) * (1 if dt != BF16 else 0.5)
            assert SBUF_START + 4 * (offset + words) <= 229368, name
            return nc.alloc_sbuf_tensor_at(name, shape, dt, offset=SBUF_START + 4 * offset)

        hT = [at("hT_hi", [P, KT, SEQ], 0, F32R), at("hT_lo", [P, KT, SEQ], 8192, F32R)]
        Z = 16384
        z_pass = {0: at("z_x", [P, 2, ZT, 512], Z), 1: at("z_c", [P, 1, ZT, 256], Z)}
        RAW = Z + 2 * ZT * 512
        raw = at("w_raw", [P, RING, UNIT], RAW)
        w_hi = at("w_hi", [P, RING, UNIT], RAW + 2048, F32R)
        w_lo = at("w_lo", [P, RING, UNIT], RAW + 4096, F32R)
        W = RAW + 6144
        C = W + 18432

        class Const:
            top = C

        def const(name, shape, dt=F32):
            t = at(name, shape, Const.top, dt)
            words = int(np.prod(shape[1:]))
            Const.top += -(-(words if dt != BF16 else (words + 1) // 2) // 8) * 8
            return t

        ident = const("ident", [P, P])
        ones = const("ones", [P, P])
        ident_bf = const("ident_bf", [P, P], BF16)
        mask_bf = const("mask_bf", [P, 2, P], BF16)
        kd_c = const("keysT_ctx", [P, 2, CTX])
        v_c = const("values_ctx", [P, 2, P])
        state_c = const("state_ctx", [P, RH, HD])
        small = const("small", [P, 4])
        cT = const("cT", [P, 2, KT])
        sT = const("silu_cT", [P, 2, KT])
        gpre = const("norm_preT", [P, KT])
        mod = const("modT", [P, 2, 2, KT])
        sink = const("sink", [P, 2, HEADS])
        decay = const("decay", [P, 2 * RH])
        lg = const("log_gamma", [P, 2 * RH])
        lt = const("log_tmp", [P, 6, 2 * RH])
        lgd = const("log_gamma_dir", [P, RH])
        gch = const("gamma_chunk", [P, RH])
        zeta = const("zeta", [P, 2, RH])
        convw = const("conv_wT", [P, 2, 4])
        stat = const("token_stats", [P, 3, 8])
        soft = const("softmax_stats", [P, 4, 8])

        rope = at("rope", [P, 2, SEQ], W + 14336)
        buf = [at("proj_raw0", [P, SEQ], W + 10240), at("proj_raw1", [P, SEQ], W + 11264)]
        turned = at("rope_turned", [P, SEQ], W + 12288)
        w_ada = at("w_ada", [P, KT, 3 * D], 0)
        m_rows = at("mod_rows", [P, 3 * D], W)
        m_bias = at("mod_bias", [P, 3 * D], W + 5120)
        m_gpost = at("mod_gpost", [P, D], W + 8192)
        m_gate = at("mod_gate", [P, D], W + 9216)
        x_tile = at("x_tile", [P, 8, D], W + 10240)
        m_mask = at("mask_f32", [P, 2, P], W + 10240)
        n_sq = at("norm_square", [P, D], W)
        n_tmp = at("norm_tmp", [P, 2, 512], W + 1024)
        qT = at("a_qT", [P, 4, SEQ], W)
        kx = at("a_kT", [P, 2, 2, SEQ], W + 4096, F32R)
        vx = at("a_v", [P, 8, 2, 2, HD], W + 8192, F32R)
        prob = at("a_prob", [P, 3, 640], W + 10240)
        pT_hi = at("a_probT_hi", [P, 5, 4, P], W + 12160, F32R)
        qs = at("a_q_split", [P, 2, 4, 2, P], W + 14720, F32R)
        o_low = at("a_out_low", [HD, 4, P], W + 16768)
        o_sum = at("a_out_sum", [P, 2, 2, P], W + 17280)
        kc = at("a_kT_ctx", [P, 2, 2, CTX], Z + 2048, F32R)
        vc = at("a_v_ctx", [P, 2, 2, 2, HD], Z + 3072, F32R)
        pT_lo = at("a_probT_lo", [P, 5, 4, P], Z + 7168, F32R)
        c_u = at("b_u", [P, 2, SEQ], W)
        c_b = at("b_b", [P, 2, SEQ], W + 2048)
        c_cu = at("b_cu", [P, 2, SEQ + 4], W + 4096)
        c_y = at("b_y", [P, 2, SEQ], W + 6400)
        qd = at("r_qT", [P, RH, SEQ], W)
        rk = at("r_kT", [P, 2, SEQ], W + 4096)
        rv = at("r_v", [P, 8, 2, P], W + 6144)
        r_prev = at("r_prev", [P, 8, RH, HD], W + 8192)
        r_inc = at("r_inc", [P, 8, RH, HD], W + 10240)
        r_kz = at("r_kzeta", [P, 2, RH, 2, HD], W + 12288)
        xi = at("r_xi", [P, RH, P], W + 13312)
        dt_ = at("r_decay", [P, RH, P], W + 13824)
        r_y = at("r_y", [P, 8, RH, HD], W + 14336)
        r_sc = at("r_scoresT", [P, 2, RH, P], W + 16384)
        r_qx = at("r_qxi", [P, 2, RH, P], W + 17408)
        r_sq = at("r_square", [P, HD], W + 12288)
        r_stat = at("r_stat", [P, 4, 8 * RH], W + 12352)
        r_e = at("r_exp", [P, RH, 2, P], W + 16384)
        r_tab = at("r_table", [P, 5, P], W + 17408)
        f_u = at("f_uT", [P, 2, SEQ], W)
        f_ab = [at("f_ab_hi", [P, 8, 2, 2, P], W + 2048, F32R), at("f_ab_lo", [P, 8, 2, 2, P], W + 6144, F32R)]
        f_bd = at("f_head", [P, 2 * P], W + 16384)
        yT = {1: [at("yT_hi", [P, ZT, 512], W, F32R), at("yT_lo", [P, ZT, 512], W + 5120, F32R)]}
        tot = [at("total_hi", [P, KT, 512], W + 10240, F32R), at("total_lo", [P, KT, 512], W + 14336, F32R)]
        y_post = at("y_post", [P, KT, 512], W)
        x_post = at("x_post", [P, KT, 512], W + 4096)
        y_first = at("y_post_first", [P, KT, SEQ], 0)
        x_first = at("x_post_first", [P, KT, SEQ], 8192)
        sq_junk = at("square_junk", [P, 512], Z + 3072)
        tmp_blk = [at(f"merge_tmp{b}", [P, 4, 512], Z + b * ZT * 512) for b in range(2)]
        gp_blk = [at(f"gate_row{b}", [P, D], Z + b * ZT * 512 + 2048) for b in range(2)]
        assert Const.top - 0 <= 53210, Const.top

        ps = ctx.enter_context(nc.psum_tensor("ps", [P, 8, 512], F32))

        x_mid = nc.dram_tensor("x_mid", (SEQ, D), F32, kind="Internal").ap()
        c_mid = nc.dram_tensor("c_mid", (CTX, D), F32, kind="Internal").ap()
        gate_rows = nc.dram_tensor("gate_rows", (DEPTH, 2, D), F32, kind="Internal").ap()

        names = (
            "act_own", "dve_own",
            "w_high", "w_split", "w_slot", "w_used",
            "const_in", "c_in", "small_in", "gate_out", "x_out", "rope_in", "ret_in", "head_in", "post_in",
            "silu_c", "mod_rows", "mod_saved", "mod_cols", "gate_made", "log_exp", "log_one", "log_ln",
            "log_gamma", "zeta_exp",
            "square", "mean", "root", "normed", "turned", "hT_pre", "hT_high",
            "proj_out", "raw_free", "v_turned",
            "score", "max_own", "max", "prob", "prob_scaled", "probT", "probT_high", "probT_saved", "pv",
            "a_split_high", "a_split", "v_high", "q_high", "q_split", "out_low", "out_sum", "gated",
            "ret_exp", "ret_qx", "k_turned", "kz", "inc", "inc_saved", "sT", "sc", "ret_y", "ret_y_saved",
            "ret_mean", "ret_square", "ret_var", "ret_root", "ret_norm", "ret_yT",
            "four", "four_hi", "four_done",
            "gate", "opart_free", "y_hi", "y_split", "tot_done",
            "y_gate", "y_out", "row_in", "out_mean", "out_root", "x_new",
        )
        sem = {n: ctx.enter_context(nc.semaphore(n)) for n in names}
        landed = [ctx.enter_context(nc.semaphore(f"w_landed{r}")) for r in range(RING)]
        x_in = [ctx.enter_context(nc.semaphore(f"x_in{b}")) for b in range(2)]
        ada_in = [ctx.enter_context(nc.semaphore(f"w_ada_in{k}")) for k in range(KT)]
        ended = {who: ctx.enter_context(nc.semaphore(f"ended_{who}")) for who in ("act", "dve", "pe")}
        block = ctx.enter_context(nc.Block())

        def stage_end(eng, tally, who):
            eng.drain().then_inc(ended[who], tally.up(f"ended_{who}"))
            for other in ended:
                if other != who:
                    eng.wait_ge(ended[other], tally.take(f"ended_{other}"))

        passes = []
        for layer in range(DEPTH):
            passes.append(Pass(layer, True, layer < DEPTH - 1))
            passes.append(Pass(layer, False, True))

        units, tile_no, raw_no, turned_no = 0, {}, {}, {}
        for n, p in enumerate(passes):
            p.tiles = list(range(MERGE)) if p.full else [A_K, A_V, R_K, R_K + 1, R_V, R_V + 1]
            for t in p.tiles:
                tile_no[n, t] = len(tile_no)
                if t < A_Z or B_C <= t < B_Z or R_Q <= t < R_Z:
                    raw_no[n, t] = len(raw_no)
                if t in (A_V, R_V, R_V + 1):
                    turned_no[n, t] = len(turned_no)
            p.n = n
            p.units = 2 * len(p.tiles)
            p.stage = passes[n - 1].stage + passes[n - 1].stages if n else 1
            p.stages = (1 if p.ctx else 0) + (8 if p.full else 3)
            if p.full:
                p.units += (2 if p.ctx else 32) + p.NB * (12 * KT + 2 * KT)
            units += p.units
        total_units = units

        def outside_in(p):
            return [c for k in range(p.NT // 2) for c in (k, p.NT - 1 - k)]

        def turned_at(n, count):
            first = 5 * 512 + 512 - P if n % 2 and count == 5 else (6 if n % 2 else 4) * 512
            return [((first + j * P) // 512, (first + j * P) % 512) for j in range(count)]

        def turned_view(n, count):
            first = turned_at(n, count)[0]
            start = (first[0] - 4) * 512 + first[1]
            return ps[:, 4:7, :].rearrange("p a n -> p (a n)")[:, start:start + count * P].rearrange(
                "p (j n) -> p j n", n=P)

        def results(p, b):
            if b < p.NB - 1:
                return y_first[:, :, 0:512], x_first[:, :, 0:512]
            return y_post[:, :, :], x_post[:, :, :]

        def z_tile(p, tile, count=1):
            return z_pass[p.s][:, 0:p.NB, tile:tile + count, :]

        def banks(first, p):
            return ps[:, first:first + p.NB, 0:p.BW]

        @block.sync
        def _(eng):
            tally = Count(eng)
            unit = [0]

            def load(source, shape=None):
                src = source() if callable(source) else source
                r = unit[0] % RING
                unit[0] += 1
                dst = raw[:, r, :]
                if shape:
                    dst = dst.rearrange(f"p ({' '.join(shape)}) -> p {' '.join(shape)}", **shape)
                eng.wait_ge(sem["w_split"], tally.take("w_split"))
                if tally.i is not None:
                    eng.sem_inc(sem["w_slot"], 1)
                eng.dma_start(dst, src).then_inc(landed[r], tally.up(f"w_landed{r}", 16))

            def rounds(times, body, units):
                assert units % RING == 0
                tally.loop(times, body, w_split=units, **{f"w_landed{r}": 16 * units // RING for r in range(RING)})

            def cols(w, k0, col, kk=4):
                return w[k0 * P:(k0 + kk) * P, bass.ds(eng.snap(col), P)].rearrange("(k p) n -> p k n", p=P)

            k4 = {"k": 4, "n": P}

            def tiles(l, first, count):
                w = a["w_in"][l]

                def body(i):
                    for t in range(2):
                        for u in range(2):
                            load(cols(w, 4 * u, i * (2 * P) + (first + t) * P), k4)
                rounds(count // 2, body, 4)

            def ada(layer, k):
                if k > 1:
                    eng.wait_ge(ada_in[k - 2], 16 * (layer + 1))
                eng.dma_start(w_ada[:, k, :], a["w_ada"][layer][k * P:(k + 1) * P, :]).then_inc(ada_in[k], 16)

            def modulation(p):
                if p.layer:
                    for who in ended:
                        eng.wait_ge(ended[who], p.stage)
                for k in range(ADA_AHEAD if p.layer else 0, KT):
                    ada(p.layer, k)

            def fourier(p):
                if p.ctx:
                    for n in range(2):
                        load(a["dft_c"][:, n * P:(n + 1) * P, :].rearrange("c p n -> p c n"), {"c": 2, "n": 256})
                    return
                for half in range(2):
                    for n in range(8):
                        for c in range(2):
                            load(a["dft_x"][c, n * P:(n + 1) * P, half * 512:(half + 1) * 512])

            def merge(p, b):
                l = p.layer
                wo = ((a["w_o_attn"][l], 0), (a["w_o_rest"][l], 0), (a["w_o_rest"][l], 2), (a["w_o_rest"][l], 2))

                def body(i):
                    for j in range(4):
                        for u in range(2):
                            load(cols(a["w_in"][l], 4 * u, i * P + (MERGE + 8 * j) * P), k4)
                        load(cols(*wo[j], i * P), k4)
                rounds(KT, body, 12)
                for half in range(2):
                    for k in range(KT):
                        load(a["w_out"][l][k * P:(k + 1) * P, half * 512:(half + 1) * 512])
                        n = half * KT + k
                        if l + 1 < DEPTH and not p.ctx and b == p.NB - 1 and n % 3 == 2 and n // 3 < ADA_AHEAD:
                            if n // 3 == 0:
                                eng.wait_ge(sem["tot_done"], KT * sum(q.NB for q in passes[:p.n + 1] if q.full))
                                eng.wait_ge(sem["x_out"], 16 * (sum(q.NT for q in passes[:p.n + 1] if q.full) - p.TB))
                            ada(l + 1, n // 3)

            for p in passes:
                l = p.layer
                if not p.full:
                    tiles(l, A_K, 2)
                    modulation(p)
                    tiles(l, R_K, 4)
                    continue
                tiles(l, A_Q, 2)
                if p.ctx:
                    modulation(p)
                tiles(l, A_Q + 2, F_U - 2)
                tiles(l, F_U, 2)
                fourier(p)
                tiles(l, F_Z, 2)
                for b in range(p.NB):
                    merge(p, b)

        @block.gpsimd
        def _(eng):
            tally = Count(eng)
            eng.sem_inc(sem["w_split"], tally.up("w_split", RING))

            def low(r):
                eng.wait_ge(sem["w_high"], tally.take("w_high"))
                eng.tensor_tensor(w_lo[:, r, :], raw[:, r, :], w_hi[:, r, :].bitcast(F32),
                                  ALU.subtract).then_inc(sem["w_split"], tally.up("w_split"))

            unit = [0]

            def low_parts(last):
                while unit[0] % RING and unit[0] < last:
                    low(unit[0] % RING)
                    unit[0] += 1
                rounds = (last - unit[0]) // RING

                def body(i):
                    for r in range(RING):
                        low(r)
                if rounds:
                    tally.loop(rounds, body, w_high=RING, w_split=RING)
                    unit[0] += RING * rounds
                while unit[0] < last:
                    low(unit[0] % RING)
                    unit[0] += 1

            def attention(p):
                groups = p.NT * 2

                def gated(g):
                    qb, kv = g // 2, g % 2
                    eng.wait_ge(sem["out_sum"], tally.take("out_sum"))
                    zz = z_pass[p.s][:, qb // p.TB, 2 * kv:2 * kv + 2, (qb % p.TB) * P:(qb % p.TB + 1) * P]
                    eng.tensor_tensor(zz, o_sum[:, g % 2, :, :], zz, ALU.mult).then_inc(sem["gated"], tally.up("gated"))

                for g in range(groups):
                    gated(g)

            def retention(p):
                eng.wait_ge(ended["dve"], p.stage + (6 if p.ctx else 5))
                for i, n in enumerate(outside_in(p)[::-1]):
                    eng.wait_ge(sem["ret_y"], tally.take("ret_y"))
                    eng.tensor_tensor(r_qx[:, i % 2, :, :], qd[:, :, n * P:(n + 1) * P], xi[:, :, :],
                                      ALU.mult).then_inc(sem["ret_qx"], tally.up("ret_qx"))

            first = 0
            for p in passes:
                if p.full:
                    low_parts(first + 2 * B_U + LOOK)
                    attention(p)
                    low_parts(first + 2 * F_U + LOOK)
                    retention(p)
                first += p.units
            low_parts(total_units)

        @block.tensor
        def _(eng):
            tally = Count(eng)
            eng.sem_inc(sem["w_used"], tally.up("w_used", RING))
            eng.sem_inc(sem["ret_y"], tally.up("ret_y", 2))
            tally.skip("w_split", RING)
            unit = [0]

            def mm(dst, lhsT, rhs, start, stop):
                return eng.matmul(dst, lhsT, rhs, start=start, stop=stop)

            def slot():
                eng.wait_ge(sem["w_split"], tally.take("w_split"))
                unit[0] += 1
                return (unit[0] - 1) % RING

            def three(dst, a_hi, a_lo, b_hi, b_lo, start, stop):
                mm(dst, a_hi, b_hi, start, False)
                mm(dst, a_hi, b_lo, False, False)
                return mm(dst, a_lo, b_hi, False, stop)

            def modulation(l):
                if l == 0:
                    eng.wait_ge(sem["silu_c"], tally.take("silu_c"))
                else:
                    eng.wait_ge(sem["y_out"], tally.now("y_out"))
                for k in range(KT):
                    eng.wait_ge(ada_in[k], 16 * (l + 1))
                    for n in range(6):
                        ins = mm(ps[0:2, n, :], sT[:, :, k], w_ada[:, k, n * 512:(n + 1) * 512], k == 0, k == KT - 1)
                        if k == KT - 1:
                            ins.then_inc(sem["mod_rows"], tally.up("mod_rows"))
                for c in range(2 * KT):
                    if c % 4 == 0:
                        eng.wait_ge(sem["mod_saved"], tally.take("mod_saved"))
                    last = eng.transpose(ps[:, 6, 2 * c:2 * c + 2], m_rows[0:2, c * P:(c + 1) * P], ident[0:2, 0:2])
                last.then_inc(sem["mod_cols"], tally.up("mod_cols"))
                tally.skip("mod_saved", 2)

            def norm(p):
                for b in range(p.NB):
                    eng.wait_ge(sem["normed"], tally.take("normed", p.TB))
                    for k in range(KT):
                        eng.wait_ge(sem["hT_pre"], tally.take("hT_pre"))
                        for t in range(p.TB):
                            last = eng.transpose(ps[:, k % 4, t * P:(t + 1) * P],
                                                 x_tile[:, b * p.TB + t, k * P:(k + 1) * P], ident[:, :])
                        last.then_inc(sem["turned"], tally.up("turned"))

            def project(p, count):
                def body(i):
                    for t in range(2):
                        eng.wait_ge(sem["proj_out"], tally.take("proj_out"))
                        for u in range(2):
                            r = slot()
                            for b in range(p.NB):
                                for k in range(4):
                                    kk, at_ = 4 * u + k, slice(b * p.BW, (b + 1) * p.BW)
                                    w = slice(k * P, (k + 1) * P)
                                    last = three(ps[:, 2 * t + b, 0:p.BW], w_hi[:, r, w], w_lo[:, r, w],
                                                 hT[0][:, kk, at_], hT[1][:, kk, at_], kk == 0, kk == KT - 1)
                            last.then_inc(sem["w_used"], tally.up("w_used"))
                tally.loop(count // 2, body, proj_out=2, w_split=4, w_used=4)

            def turn_values(p, t, before):
                eng.wait_ge(sem["proj_out"], 2 + tile_no[p.n, t] + 1)
                if before is not None:
                    eng.wait_ge(sem["raw_free"], 2 + raw_no[p.n, before] + 1)
                src = buf[raw_no[p.n, t] % 2]
                for n in range(p.NT):
                    last = eng.transpose(ps[:, 4 + n // 4, (n % 4) * P:(n % 4 + 1) * P],
                                         src[:, n * P:(n + 1) * P], ident[:, :])
                last.then_inc(sem["v_turned"], tally.up("v_turned"))

            def attention(p):
                steps = [(qb, h) for qb in range(p.NT) for h in range(HEADS)]

                def window(qb):
                    if p.ctx:
                        return 0, 0
                    return max(qb - 1, 0), min(qb + 1, p.NT - 1) + 1

                def scores(n):
                    qb, h = steps[n]
                    kv, c = h // 4, 2 * (n % 2)
                    lo, hi = window(qb)
                    q = qs[:, qb % 2, h // 2, h % 2, :]
                    if h % 4 == 0:
                        eng.wait_ge(sem["q_split"], tally.take("q_split"))
                    eng.wait_ge(sem["prob"], tally.take("prob"))
                    if hi > lo:
                        L = (hi - lo) * P
                        parts = []
                        if lo < qb:
                            parts.append((512 - L, 0))
                        if hi - 1 > qb:
                            parts.append((512 - P, 1))
                        mm(ps[:, c, 512 - L:512], q, kx[:, kv, 0, lo * P:hi * P], True, False)
                        mm(ps[:, c, 512 - L:512], q, kx[:, kv, 1, lo * P:hi * P], False, not parts)
                        for m, (col, which) in enumerate(parts):
                            mm(ps[:, c, col:col + P], ident_bf[:, :], mask_bf[:, which, :], False, m == len(parts) - 1)
                    mm(ps[:, c + 1, 0:CTX], q, kc[:, kv, 0, :], True, False)
                    mm(ps[:, c + 1, 0:CTX], q, kc[:, kv, 1, :], False, True).then_inc(sem["score"], tally.up("score"))

                def turn(n):
                    qb, h = steps[n]
                    lo, hi = window(qb)
                    places = turned_at(n, hi - lo + 2)
                    eng.wait_ge(sem["prob_scaled"], tally.take("prob_scaled"))
                    eng.wait_ge(sem["probT_saved"], tally.take("probT_saved"))
                    order = sorted(range(len(places)), key=lambda j: places[j][0] == 5)
                    for j in order:
                        bank, col = places[j]
                        if bank == 5:
                            eng.wait_ge(sem["probT_saved"], tally.now("probT_saved", 1))
                        last = eng.transpose(ps[:, bank, col:col + P], prob[:, n % 3, j * P:(j + 1) * P], ident[:, :])
                    last.then_inc(sem["probT"], tally.up("probT"))

                def values(n):
                    qb, h = steps[n]
                    lo, hi = window(qb)
                    kv, count, pair = h // 4, hi - lo + 2, h // 2 % 2
                    if pair == 0:
                        if tally.now("out_sum"):
                            eng.wait_ge(sem["out_sum"], tally.now("out_sum"))
                        tally.skip("out_sum", 1)
                    dst, heads = ps[:, 7, pair * 2 * P:(pair + 1) * 2 * P], slice(2 * pair, 2 * pair + 2)
                    for j in range(count):
                        v = vx[:, lo + j, kv, :, :] if j < hi - lo else vc[:, j - (hi - lo), kv, :, :]
                        mm(dst, v, pT_hi[:, j, heads, :], j == 0, False)
                        last = mm(dst, v, pT_lo[:, j, heads, :], False, j == count - 1)
                    if pair:
                        last.then_inc(sem["pv"], tally.up("pv"))

                eng.wait_ge(sem["a_split"], tally.take("a_split"))
                scores(0)
                scores(1)
                for n in range(len(steps)):
                    if n + 2 < len(steps):
                        scores(n + 2)
                    turn(n)
                    if n and n % 2 == 0:
                        eng.wait_ge(sem["probT_saved"], tally.now("probT_saved", 1))
                        values(n - 1)
                eng.wait_ge(sem["probT_saved"], tally.now("probT_saved", 2))
                values(len(steps) - 1)

            def states(p):
                order = outside_in(p)

                def turn_keys(i):
                    for j in range(2):
                        last = eng.transpose(ps[:, 4 + i % 2, j * P:(j + 1) * P],
                                             rk[:, j, order[i] * P:(order[i] + 1) * P], ident[:, :])
                    last.then_inc(sem["k_turned"], tally.up("k_turned"))
                turn_keys(0)
                for i, n in enumerate(order):
                    if i + 1 < p.NT:
                        turn_keys(i + 1)
                    eng.wait_ge(sem["kz"], tally.take("kz"))
                    eng.wait_ge(sem["inc_saved"], tally.take("inc_saved"))
                    for h in range(RH):
                        v = rv[:, n, h // 2, h % 2 * HD:h % 2 * HD + HD]
                        last = mm(ps[:, 6 + i % 2, h * HD:(h + 1) * HD], r_kz[:, i % 2, h, :, :], v, True, True)
                    last.then_inc(sem["inc"], tally.up("inc"))

            def retention(p):
                order = outside_in(p)[::-1]

                def scores(i):
                    c = slice(order[i] * P, (order[i] + 1) * P)
                    for h in range(RH):
                        rows = slice(h % 2 * HD, h % 2 * HD + HD)
                        last = mm(ps[:, i % 2 + 4 * (h % 2), h // 2 * P:(h // 2 + 1) * P], rk[rows, h // 2, c],
                                  qd[rows, h, c], True, True)
                    last.then_inc(sem["sT"], tally.up("sT"))
                scores(0)
                for i, n in enumerate(order):
                    if i + 1 < p.NT:
                        scores(i + 1)
                    eng.wait_ge(sem["sc"], tally.take("sc"))
                    eng.wait_ge(sem["ret_qx"], tally.take("ret_qx"))
                    eng.wait_ge(sem["ret_y_saved"], tally.take("ret_y_saved"))
                    for h in range(RH):
                        dst = ps[:, 2 + i % 2, h * HD:(h + 1) * HD]
                        v = rv[:, n, h // 2, h % 2 * HD:h % 2 * HD + HD]
                        mm(dst, r_sc[:, i % 2, h, :], v, True, False)
                        last = mm(dst, r_qx[:, i % 2, h, :], r_prev[:, n, h, :], False, True)
                    last.then_inc(sem["ret_y"], tally.up("ret_y"))
                for b in range(p.NB):
                    eng.wait_ge(sem["ret_norm"], tally.take("ret_norm"))
                    for j in range(2):
                        for t in range(p.TB):
                            last = eng.transpose(ps[:, 4 + 2 * j + b, t * P:(t + 1) * P],
                                                 r_y[:, b * p.TB + t, 2 * j:2 * j + 2, :], ident[:, :])
                        last.then_inc(sem["ret_yT"], tally.up("ret_yT"))

            def fourier(p):
                eng.wait_ge(sem["proj_out"], 2 + tile_no[p.n, F_U + 1] + 1)
                eng.wait_ge(sem["head_in"], tally.take("head_in", 16))
                for n in range(p.NT):
                    eng.wait_ge(sem["four_done"], tally.take("four_done"))
                    for j in range(2):
                        last = mm(ps[:, 4 + n % 2, j * 256:(j + 1) * 256], f_u[:, j, n * P:(n + 1) * P],
                                  f_bd[:, :], True, True)
                    last.then_inc(sem["four"], tally.up("four"))
                eng.wait_ge(sem["four_done"], tally.now("four_done", 2))
                for half in range(p.NB):
                    for n in range(p.NT):
                        for c in range(2):
                            if not p.ctx or c == 0:
                                r = slot()
                            w = slice(c * p.BW, (c + 1) * p.BW) if p.ctx else slice(0, 512)
                            for j in range(2):
                                last = three(ps[:, 4 + 2 * half + j, 0:p.BW], f_ab[0][:, n, j, c, :],
                                             f_ab[1][:, n, j, c, :], w_hi[:, r, w], w_lo[:, r, w],
                                             n == 0 and c == 0, n == p.NT - 1 and c == 1)
                            if not p.ctx or c == 1:
                                last.then_inc(sem["w_used"], tally.up("w_used"))

            def merge(p, b):
                at_ = slice(b * p.BW, (b + 1) * p.BW)
                if b:
                    eng.wait_ge(sem["y_out"], tally.now("y_out"))

                def body(i, first=False):
                    for j, (tile, count) in enumerate(BRANCH):
                        eng.wait_ge(sem["gate"], tally.take("gate"))
                        for u in range(2):
                            r = slot()
                            for k in range(4):
                                kk, w = 4 * u + k, slice(k * P, (k + 1) * P)
                                last = three(ps[:, j % 2, 0:p.BW], w_hi[:, r, w], w_lo[:, r, w],
                                             hT[0][:, kk, at_], hT[1][:, kk, at_], kk == 0, kk == KT - 1)
                            last.then_inc(sem["w_used"], tally.up("w_used"))
                        eng.wait_ge(sem["opart_free"], tally.take("opart_free"))
                        r = slot()
                        if first:
                            eng.wait_ge(sem["y_split"], tally.take("y_split"))
                        for k in range(count):
                            kk = k + (2 if j == 3 else 0)
                            w = slice(kk * P, (kk + 1) * P)
                            last = three(ps[:, 2 + j % 2, 0:p.BW], w_hi[:, r, w], w_lo[:, r, w],
                                         yT[1][0][:, tile + k, 0:p.BW], yT[1][1][:, tile + k, 0:p.BW],
                                         k == 0, k == count - 1)
                        last.then_inc(sem["w_used"], tally.up("w_used"))
                body(0, True)
                tally.loop(KT - 1, body, gate=4, w_split=12, w_used=12, opart_free=4)
                eng.wait_ge(sem["gate"], tally.now("gate", 2))
                eng.wait_ge(sem["opart_free"], tally.now("opart_free", 2))
                eng.wait_ge(sem["tot_done"], tally.take("tot_done", KT))
                for half in range(2):
                    if half == 1:
                        tally.skip("y_out", 2 * p.TB)
                    for k in range(KT):
                        r = slot()
                        for t in range(p.TB):
                            w = slice(t * P, (t + 1) * P)
                            last = three(ps[:, 4 - 4 * half + t, :], tot[0][:, k, w], tot[1][:, k, w],
                                         w_hi[:, r, :], w_lo[:, r, :], k == 0, k == KT - 1)
                        last.then_inc(sem["w_used"], tally.up("w_used"))

            stage_end(eng, tally, "pe")
            for p in passes:
                if p.ctx:
                    modulation(p.layer)
                    stage_end(eng, tally, "pe")
                norm(p)
                stage_end(eng, tally, "pe")
                if not p.full:
                    project(p, 2)
                    turn_values(p, A_V, None)
                    project(p, 4)
                    turn_values(p, R_V, A_V)
                    turn_values(p, R_V + 1, R_V)
                    stage_end(eng, tally, "pe")
                    states(p)
                    stage_end(eng, tally, "pe")
                    continue
                project(p, 6)
                turn_values(p, A_V, None)
                project(p, 4)
                stage_end(eng, tally, "pe")
                attention(p)
                stage_end(eng, tally, "pe")
                project(p, 8)
                stage_end(eng, tally, "pe")
                project(p, 6)
                turn_values(p, R_V, A_V)
                turn_values(p, R_V + 1, R_V)
                project(p, 2)
                stage_end(eng, tally, "pe")
                states(p)
                retention(p)
                stage_end(eng, tally, "pe")
                project(p, 2)
                fourier(p)
                project(p, 2)
                stage_end(eng, tally, "pe")
                for b in range(p.NB):
                    merge(p, b)
                if p.ctx or p.layer + 1 == DEPTH:
                    stage_end(eng, tally, "pe")
                else:
                    eng.drain().then_inc(ended["pe"], tally.up("ended_pe"))
                    tally.skip("ended_act", 1)
                    tally.skip("ended_dve", 1)

        @block.scalar
        def _(eng):
            tally = Count(eng)
            eng.sem_inc(sem["proj_out"], tally.up("proj_out", 2))
            eng.sem_inc(sem["prob"], tally.up("prob", 2))
            eng.sem_inc(sem["inc_saved"], tally.up("inc_saved", 2))
            eng.sem_inc(sem["ret_y_saved"], tally.up("ret_y_saved", 2))
            eng.sem_inc(sem["gate"], tally.up("gate", 2))
            tally.skip("hT_pre", 4)
            tally.skip("ret_y", 2)
            tally.skip("w_used__done", RING)
            split = [0]

            def act(dst, src, func=ACT.Copy, **kw):
                return eng.activation(dst, src, func, **kw)

            def split_high(count):
                for _ in range(count):
                    if split[0] >= total_units:
                        return
                    r = split[0] % RING
                    split[0] += 1
                    eng.wait_ge(landed[r], tally.take(f"w_landed{r}", 16))
                    eng.wait_ge(sem["w_used"], tally.take("w_used"))
                    act(w_hi[:, r, :], raw[:, r, :]).then_inc(sem["w_high"], tally.up("w_high"))

            def constants():
                eng.dma_start(cT[:, :, :], a["c_cols"]).then_inc(sem["c_in"], tally.up("c_in", 16))
                eng.dma_start(ident[:, :], a["ident"]).then_inc(sem["const_in"], tally.up("const_in", 16))
                eng.dma_start(m_mask[:, :, :], a["mask"]).then_inc(sem["const_in"], tally.up("const_in", 16))
                eng.dma_start(small[:, :], a["small"]).then_inc(sem["const_in"], tally.up("const_in", 16))
                eng.wait_ge(sem["c_in"], tally.now("c_in"))
                act(sT[:, :, :], cT[:, :, :], ACT.Silu).then_inc(sem["silu_c"], tally.up("silu_c"))
                split_high(LOOK)

            def modulation(l):
                eng.dma_start(gpre[:, :], a["norm_pre_cols"][l]).then_inc(sem["small_in"], tally.up("small_in", 16))
                eng.dma_start(convw[:, :, :], a["conv_cols"][l]).then_inc(sem["small_in"], tally.up("small_in", 16))
                eng.dma_start(m_bias[0:2, :], a["b_ada"][l:l + 1, :].partition_broadcast(2).rearrange("p a n -> p (a n)")).then_inc(sem["small_in"], tally.up("small_in", 16))
                eng.dma_start(m_gpost[0:2, :], a["norm_post"][l:l + 1, :].partition_broadcast(2).rearrange("p a n -> p (a n)")).then_inc(sem["small_in"], tally.up("small_in", 16))
                eng.dma_start(sink[:, 0, :], a["attn_sink"][l:l + 1, :].partition_broadcast(P).rearrange("p a n -> p (a n)")).then_inc(sem["small_in"], tally.up("small_in", 16))
                eng.dma_start(decay[:, :], a["ret_decay"][l:l + 1].rearrange("a d h -> a (d h)").partition_broadcast(P)
                     .rearrange("p a n -> p (a n)")).then_inc(sem["small_in"], tally.up("small_in", 16))
                eng.wait_ge(sem["small_in"], tally.now("small_in"))
                eng.wait_ge(sem["log_one"], tally.take("log_one"))
                act(lt[:, 1, :], lt[:, 0, :], ACT.Exp, scale=-1.0).then_inc(sem["log_exp"], tally.up("log_exp"))
                eng.wait_ge(sem["log_one"], tally.take("log_one"))
                act(lt[:, 3, :], lt[:, 2, :], ACT.Ln).then_inc(sem["log_ln"], tally.up("log_ln"))
                eng.wait_ge(sem["log_gamma"], tally.take("log_gamma"))
                for d in range(2):
                    act(zeta[:, d, :], lg[:, d * RH:(d + 1) * RH], ACT.Exp, scale=small[:, 2 + d:3 + d]).then_inc(sem["act_own"], tally.up("act_own"))
                act(gch[:, :], lgd[:, :], ACT.Exp, scale=float(P)).then_inc(sem["zeta_exp"], tally.up("zeta_exp"))
                eng.wait_ge(sem["gate_made"], tally.take("gate_made"))
                eng.dma_start(gate_rows[l], m_gate[0:2, :]).then_inc(sem["gate_out"], tally.up("gate_out", 16))
                eng.wait_ge(sem["gate_out"], tally.now("gate_out"))

            def norm(p):
                src = (a["ctx"][0] if p.ctx else a["x"][0]) if p.layer == 0 else (c_mid if p.ctx else x_mid)
                src = src.rearrange("(t p) n -> p t n", p=P)
                for b in range(p.NB):
                    at_ = slice(b * p.TB, (b + 1) * p.TB)
                    eng.dma_start(x_tile[:, at_, :], src[:, at_, :]).then_inc(x_in[b], tally.up(f"x_in{b}", 16))
                for b in range(p.NB):
                    eng.wait_ge(x_in[b], tally.now(f"x_in{b}"))
                    for t in range(b * p.TB, (b + 1) * p.TB):
                        if tally.now("square"):
                            eng.wait_ge(sem["square"], tally.now("square"))
                        act(n_sq[:, :], x_tile[:, t, :], ACT.Square, accum_out=stat[:, 0, t:t + 1]).then_inc(sem["square"], tally.up("square"))
                    eng.wait_ge(sem["mean"], tally.take("mean"))
                    at_ = slice(b * p.TB, (b + 1) * p.TB)
                    act(stat[:, 2, at_], stat[:, 1, at_], ACT.Sqrt).then_inc(sem["root"], tally.up("root"))
                    for k in range(KT):
                        eng.wait_ge(sem["hT_pre"], tally.take("hT_pre"))
                        act(hT[0][:, k, b * p.BW:(b + 1) * p.BW], n_tmp[:, k % 2, 0:p.BW]).then_inc(sem["hT_high"], tally.up("hT_high"))

            def evacuate(p, t, dst, func=ACT.Copy):
                split_high(2)
                if dst is None:
                    eng.wait_ge(sem["raw_free"], tally.take("raw_free"))
                    dst = buf[raw_no[p.n, t] % 2][:, 0:p.T]
                if len(dst.shape) == 2:
                    dst = dst.rearrange("p (b n) -> p b n", b=p.NB)
                eng.wait_ge(sem["w_used"], tally.take("w_used__done", 2))
                act(dst, banks(2 * (tile_no[p.n, t] % 2), p), func).then_inc(sem["proj_out"], tally.up("proj_out"))

            def values_high(p):
                eng.wait_ge(sem["v_turned"], turned_no[p.n, A_V] + 1)
                for b in range(p.NB):
                    eng.activation(vx[:, 4 * b:4 * b + 4, :, 0, :], ps[:, 4 + b, :].rearrange(
                        "p (t k d) -> p t k d", k=2, d=HD), ACT.Copy).then_inc(sem["v_high"], tally.up("v_high"))

            def tile_range(p, first, last):
                for t in range(first, last):
                    for z0, zt, count in ((A_Z, Z_A, 4), (B_Z, Z_B, 2), (R_Z, Z_R, 2), (F_Z, Z_F, 2)):
                        if z0 <= t < z0 + count:
                            evacuate(p, t, z_tile(p, zt + t - z0)[:, :, 0, :], ACT.Silu)
                            break
                    else:
                        dst = None
                        if B_U <= t < B_C:
                            dst = (c_u if t < B_B else c_b)[:, t % 2, 0:p.T]
                        elif F_U <= t:
                            dst = f_u[:, t - F_U, 0:p.T]
                        evacuate(p, t, dst)

            def attention(p):
                steps = [(qb, h) for qb in range(p.NT) for h in range(HEADS)]

                def width(qb):
                    return 0 if p.ctx else (3 - (qb == 0) - (qb == p.NT - 1)) * P

                def queries(m):
                    qb, kv = m // 2, m % 2
                    for hh in range(2):
                        rows, t = slice(hh * HD, hh * HD + HD), slice(2 * kv, 2 * kv + 2)
                        last = eng.activation(qs[rows, qb % 2, t, hh, :], qT[rows, t, qb * P:(qb + 1) * P], ACT.Copy)
                        if hh == 0:
                            last.then_inc(sem["act_own"], tally.up("act_own"))
                    last.then_inc(sem["q_high"], tally.up("q_high"))

                def exps(n):
                    qb, h = steps[n]
                    L, c, k = width(qb), 2 * (n % 2), n % 4
                    eng.wait_ge(sem["max"], tally.take("max"))
                    s_view = ps[:, c:c + 2, :].rearrange("p a n -> p (a n)")[:, 512 - L:512 + CTX]
                    eng.activation(prob[:, n % 3, 0:L + CTX], s_view, ACT.Exp, bias=soft[:, k, 1:2], scale=SCALE,
                                   accum_out=soft[:, k, 2:3]).then_inc(sem["act_own"], tally.up("act_own"))
                    eng.activation(soft[:, k, 3:4], soft[:, k, 1:2], ACT.Exp, bias=sink[:, 0, h:h + 1],
                                   scale=1.0).then_inc(sem["prob"], tally.up("prob"))

                def save(n):
                    qb, h = steps[n]
                    count = (width(qb) + CTX) // P
                    eng.wait_ge(sem["probT"], tally.take("probT"))
                    src = turned_view(n, count)
                    eng.activation(pT_hi[:, 0:count, h % 4, :], src, ACT.Copy).then_inc(
                        sem["probT_high"], tally.up("probT_high"))

                def low_half():
                    eng.wait_ge(sem["pv"], tally.take("pv"))
                    if tally.now("out_sum"):
                        eng.wait_ge(sem["out_sum"], tally.now("out_sum"))
                    tally.skip("out_sum", 1)
                    eng.activation(o_low[:, :, :].rearrange("p h n -> p (h n)"), ps[HD:P, 7, :],
                                   ACT.Copy).then_inc(sem["out_low"], tally.up("out_low"))

                eng.activation(kc[:, :, 0, :], kd_c[:, :, :], ACT.Copy).then_inc(sem["act_own"], tally.up("act_own"))
                eng.activation(vc[:, :, :, 0, :], v_c[:, :, :].rearrange("p t (k d) -> p t k d", k=2),
                               ACT.Copy).then_inc(sem["a_split_high"], tally.up("a_split_high"))
                queries(0)
                queries(1)
                groups = len(steps) // 4
                exps(0)
                for n in range(len(steps)):
                    if n + 1 < len(steps):
                        exps(n + 1)
                    save(n)
                    if n and n % 4 == 0:
                        low_half()
                    if n % 4 == 2 and n // 4 + 2 < groups:
                        queries(n // 4 + 2)
                low_half()

            def decay_tables():
                eng.wait_ge(sem["ret_in"], tally.now("ret_in"))
                for h in range(RH):
                    act(xi[:, h, :], r_tab[:, 4, :], ACT.Exp, scale=lgd[:, h:h + 1]).then_inc(sem["act_own"], tally.up("act_own"))
                for h in range(RH):
                    act(r_e[:, h, 0, :], r_tab[:, 0, :], ACT.Exp, scale=lg[:, h:h + 1]).then_inc(sem["act_own"], tally.up("act_own"))
                    act(r_e[:, h, 1, :], r_tab[:, 2, :], ACT.Exp, scale=lg[:, RH + h:RH + h + 1]).then_inc(sem["ret_exp"], tally.up("ret_exp"))

            def states(p):
                for i, n in enumerate(outside_in(p)):
                    eng.wait_ge(sem["inc"], tally.take("inc"))
                    act(r_inc[:, n, :, :], ps[:, 6 + i % 2, 0:RH * HD].rearrange("p (h d) -> p h d", h=RH)).then_inc(sem["inc_saved"], tally.up("inc_saved"))

            def retention(p):
                order = outside_in(p)[::-1]

                def squares(i):
                    eng.wait_ge(sem["ret_mean"], tally.take("ret_mean"))
                    for h in range(RH):
                        if tally.now("ret_square"):
                            eng.wait_ge(sem["ret_square"], tally.now("ret_square"))
                        act(r_sq[:, :], r_y[:, order[i], h, :], ACT.Square,
                            accum_out=r_stat[:, 3, order[i] * RH + h:order[i] * RH + h + 1]).then_inc(
                                sem["ret_square"], tally.up("ret_square"))
                for i, n in enumerate(order):
                    eng.wait_ge(sem["ret_y"], tally.take("ret_y"))
                    for h in range(RH):
                        ins = act(r_y[:, n, h, :], ps[:, 2 + i % 2, h * HD:(h + 1) * HD],
                                  accum_out=r_stat[:, 0, n * RH + h:n * RH + h + 1])
                        ins.then_inc(sem["ret_y_saved"], tally.up("ret_y_saved")) if h == RH - 1 else ins.then_inc(
                            sem["act_own"], tally.up("act_own"))
                    if i > 1:
                        squares(i - 2)
                for i in range(p.NT - 2, p.NT):
                    squares(i)
                eng.wait_ge(sem["ret_var"], tally.take("ret_var"))
                act(r_stat[:, 2, 0:p.NT * RH], r_stat[:, 1, 0:p.NT * RH], ACT.Sqrt).then_inc(sem["ret_root"], tally.up("ret_root"))

            def fourier(p):
                for n in range(p.NT):
                    eng.wait_ge(sem["four"], tally.take("four"))
                    act(f_ab[0][:, n, :, :, :].rearrange("p j c n -> p (j c n)"), ps[:, 4 + n % 2, :]).then_inc(sem["four_hi"], tally.up("four_hi"))
                split_high(2 if p.ctx else 32)
                tally.skip("w_used__done", 2 if p.ctx else 32)

            def gated_high(p, b):
                for tile, count in BRANCH:
                    src = z_pass[p.s][:, b, tile:tile + count, :]
                    act(yT[1][0][:, tile:tile + count, 0:p.BW], src).then_inc(sem["y_hi"], tally.up("y_hi"))

            def sources(p, b):
                src = (a["ctx"][0] if p.ctx else a["x"][0]) if p.layer == 0 else (c_mid if p.ctx else x_mid)
                dst = (out[0] if p.layer == DEPTH - 1 else x_mid) if not p.ctx else c_mid
                rows = slice(b * p.BW, (b + 1) * p.BW)
                return [m[rows, :].rearrange("(t p) n -> p t n", p=P) for m in (src, dst)]

            def send(p, b):
                dst = sources(p, b)[1]
                for t in range(p.TB):
                    eng.wait_ge(sem["x_new"], tally.take("x_new"))
                    eng.dma_start(dst[:, t, :].rearrange("p (h n) -> p h n", h=2), results(p, b)[1][:, 2 * t:2 * t + 2, :]).then_inc(sem["x_out"], tally.up("x_out", 16))

            def merge(p, b):
                tmp = tmp_blk[b]
                eng.wait_ge(sem["y_split"], tally.take("y_split__all", len(BRANCH)))
                eng.dma_start(gp_blk[b][:, :], gate_rows[p.layer, p.s:p.s + 1, :].partition_broadcast(P)
                              .rearrange("p a n -> p (a n)")).then_inc(sem["row_in"], tally.up("row_in", 16))

                def body(i, first=False):
                    for j in range(4):
                        split_high(3)
                        if first and b and j == 2:
                            send(p, b - 1)
                        eng.wait_ge(sem["w_used"], tally.take("w_used__done", 2))
                        eng.wait_ge(sem["opart_free"], tally.take("opart_free"))
                        act(tmp[:, j % 2, 0:p.BW], ps[:, j % 2, 0:p.BW], ACT.Sigmoid).then_inc(sem["gate"], tally.up("gate"))
                        tally.skip("w_used__done", 1)
                body(0, True)
                tally.loop(KT - 1, body, w_high=12, w_used=12, w_used__done=12, opart_free=4, gate=4,
                       **{f"w_landed{r}": 48 for r in range(RING)})
                split[0] += 12 * (KT - 2)
                for half in range(2):
                    split_high(8)
                    if half == 0:
                        eng.wait_ge(sem["tot_done"], tally.take("tot_done", KT))
                        for t in range(p.TB):
                            eng.dma_start(results(p, b)[1][:, 2 * t:2 * t + 2, :], sources(p, b)[0][:, t, :]
                                          .rearrange("p (h n) -> p h n", h=2)).then_inc(sem["post_in"], tally.up("post_in", 16))
                        if b + 1 < p.NB:
                            gated_high(p, b + 1)
                    eng.wait_ge(sem["w_used"], tally.take("w_used__done", 8))
                    for t in range(p.TB):
                        if tally.now("y_out"):
                            eng.wait_ge(sem["y_out"], tally.now("y_out"))
                        eng.wait_ge(sem["y_gate"], tally.take("y_gate"))
                        act(sq_junk[:, :], ps[:, 4 - 4 * half + t, :], ACT.Square,
                                 accum_out=stat[:, 0, 4 * half + t:4 * half + t + 1]).then_inc(sem["y_out"], tally.up("y_out"))
                eng.wait_ge(sem["out_mean"], tally.take("out_mean"))
                act(stat[:, 2, 0:p.TB], stat[:, 1, 0:p.TB], ACT.Sqrt).then_inc(sem["out_root"], tally.up("out_root"))

            constants()
            stage_end(eng, tally, "act")
            for p in passes:
                if p.ctx:
                    modulation(p.layer)
                    stage_end(eng, tally, "act")
                norm(p)
                stage_end(eng, tally, "act")
                if not p.full:
                    tile_range(p, A_K, A_Z)
                    tile_range(p, R_K, R_Z)
                    stage_end(eng, tally, "act")
                    states(p)
                    stage_end(eng, tally, "act")
                    continue
                if not p.ctx:
                    eng.dma_start(rope[:, :, :], a["rope"]).then_inc(sem["rope_in"], tally.up("rope_in", 16))
                tile_range(p, A_Q, A_Z)
                if not p.ctx:
                    values_high(p)
                tile_range(p, A_Z, B_U)
                stage_end(eng, tally, "act")
                attention(p)
                stage_end(eng, tally, "act")
                eng.dma_start(r_tab[:, :, :], a["ret"]).then_inc(sem["ret_in"], tally.up("ret_in", 16))
                tile_range(p, B_U, B_B)
                decay_tables()
                tile_range(p, B_B, R_Q)
                stage_end(eng, tally, "act")
                if not p.ctx:
                    eng.dma_start(rope[:, :, :], a["rope"]).then_inc(sem["rope_in"], tally.up("rope_in", 16))
                tile_range(p, R_Q, F_U)
                stage_end(eng, tally, "act")
                states(p)
                retention(p)
                stage_end(eng, tally, "act")
                eng.dma_start(f_bd[:, :], a["dft_head"][p.s].rearrange("p c n -> p (c n)")).then_inc(sem["head_in"], tally.up("head_in", 16))
                tile_range(p, F_U, F_Z)
                fourier(p)
                tile_range(p, F_Z, MERGE)
                stage_end(eng, tally, "act")
                gated_high(p, 0)
                for b in range(p.NB):
                    merge(p, b)
                send(p, p.NB - 1)
                eng.wait_ge(sem["x_out"], tally.now("x_out"))
                stage_end(eng, tally, "act")

        @block.vector
        def _(eng):
            tally = Count(eng)
            eng.sem_inc(sem["hT_pre"], tally.up("hT_pre", 4))
            eng.sem_inc(sem["raw_free"], tally.up("raw_free", 2))
            eng.sem_inc(sem["probT_saved"], tally.up("probT_saved", 2))
            eng.sem_inc(sem["four_done"], tally.up("four_done", 2))
            eng.sem_inc(sem["opart_free"], tally.up("opart_free", 2))
            tally.skip("w_used__done", RING)
            tally.skip("prob", 2)
            tally.skip("gate", 2)
            tally.skip("inc_saved", 2)
            tally.skip("ret_y_saved", 2)

            def tt(dst, x, y, op=ALU.mult):
                return eng.tensor_tensor(dst, x, y, op)

            def constants():
                eng.memset(ones[:, :], 1.0).then_inc(sem["dve_own"], tally.up("dve_own"))
                eng.wait_ge(sem["const_in"], tally.take("const_in", 48))
                eng.tensor_copy(ident_bf[:, :], ident[:, :]).then_inc(sem["dve_own"], tally.up("dve_own"))
                eng.tensor_copy(mask_bf[:, :, :], m_mask[:, :, :]).then_inc(sem["dve_own"], tally.up("dve_own"))
                eng.wait_ge(sem["dve_own"], tally.now("dve_own"))

            def modulation(l):
                eng.wait_ge(sem["small_in"], tally.take("small_in", 16 * 6))
                eng.tensor_scalar(sink[:, 1, :], sink[:, 0, :], -1.0, None, ALU.mult).then_inc(sem["dve_own"], tally.up("dve_own"))
                eng.wait_ge(sem["dve_own"], tally.now("dve_own"))
                eng.tensor_scalar(lt[:, 1, :], decay[:, :], -1.0, None, ALU.mult).then_inc(sem["dve_own"], tally.up("dve_own"))
                eng.wait_ge(sem["dve_own"], tally.now("dve_own"))
                tt(lt[:, 0, :], decay[:, :], lt[:, 1, :], ALU.max).then_inc(sem["log_one"], tally.up("log_one"))
                eng.wait_ge(sem["log_exp"], tally.take("log_exp"))
                eng.tensor_scalar(lt[:, 2, :], lt[:, 1, :], 1.0, None, ALU.add).then_inc(sem["log_one"], tally.up("log_one"))
                eng.wait_ge(sem["log_one"], tally.now("log_one"))
                eng.tensor_scalar(lt[:, 4, :], lt[:, 2, :], -1.0, None, ALU.add).then_inc(sem["dve_own"], tally.up("dve_own"))
                eng.wait_ge(sem["dve_own"], tally.now("dve_own"))
                tt(lt[:, 4, :], lt[:, 1, :], lt[:, 4, :], ALU.subtract).then_inc(sem["dve_own"], tally.up("dve_own"))
                eng.wait_ge(sem["dve_own"], tally.now("dve_own"))
                eng.reciprocal(lt[:, 5, :], lt[:, 2, :]).then_inc(sem["dve_own"], tally.up("dve_own"))
                eng.wait_ge(sem["dve_own"], tally.now("dve_own"))
                tt(lt[:, 4, :], lt[:, 4, :], lt[:, 5, :]).then_inc(sem["dve_own"], tally.up("dve_own"))
                eng.wait_ge(sem["dve_own"], tally.now("dve_own"))
                eng.wait_ge(sem["log_ln"], tally.take("log_ln"))
                tt(lt[:, 4, :], lt[:, 4, :], lt[:, 3, :], ALU.add).then_inc(sem["dve_own"], tally.up("dve_own"))
                eng.wait_ge(sem["dve_own"], tally.now("dve_own"))
                eng.tensor_scalar(lt[:, 5, :], decay[:, :], 0.0, None, ALU.min).then_inc(sem["dve_own"], tally.up("dve_own"))
                eng.wait_ge(sem["dve_own"], tally.now("dve_own"))
                tt(lg[:, :], lt[:, 5, :], lt[:, 4, :], ALU.subtract).then_inc(sem["dve_own"], tally.up("dve_own"))
                eng.wait_ge(sem["dve_own"], tally.now("dve_own"))
                eng.tensor_copy(lgd[0:HD, :], lg[0:HD, 0:RH]).then_inc(sem["dve_own"], tally.up("dve_own"))
                eng.wait_ge(sem["dve_own"], tally.now("dve_own"))
                eng.tensor_copy(lgd[HD:P, :], lg[HD:P, RH:2 * RH]).then_inc(sem["log_gamma"], tally.up("log_gamma"))
                eng.wait_ge(sem["zeta_exp"], tally.take("zeta_exp"))
                eng.tensor_scalar(zeta[:, :, :], zeta[:, :, :], SCALE, None, ALU.mult).then_inc(sem["dve_own"], tally.up("dve_own"))
                for n in range(6):
                    eng.wait_ge(sem["mod_rows"], tally.take("mod_rows"))
                    c = slice(n * 512, (n + 1) * 512)
                    tt(m_rows[0:2, c], ps[0:2, n, :], m_bias[0:2, c], ALU.add).then_inc(sem["mod_saved"], tally.up("mod_saved"))
                eng.wait_ge(sem["mod_saved"], tally.now("mod_saved"))
                tt(m_gate[0:2, :], m_rows[0:2, 2 * D:3 * D], m_gpost[0:2, :]).then_inc(sem["gate_made"], tally.up("gate_made"))
                eng.wait_ge(sem["mod_cols"], tally.take("mod_cols"))
                cols = ps[:, 6, 0:4 * KT].rearrange("p (k s) -> p k s", s=2)
                for s in range(2):
                    eng.tensor_copy(mod[:, s, 1, :], cols[:, 0:KT, s]).then_inc(sem["dve_own"], tally.up("dve_own"))
                    eng.scalar_tensor_tensor(mod[:, s, 0, :], cols[:, KT:2 * KT, s], 1.0, gpre[:, :],
                                                  ALU.add, ALU.mult).then_inc(sem["dve_own"], tally.up("dve_own"))
                eng.wait_ge(sem["dve_own"], tally.now("dve_own"))

            def norm(p):
                for b in range(p.NB):
                    at_ = slice(b * p.TB, (b + 1) * p.TB)
                    eng.wait_ge(sem["square"], tally.take("square", p.TB))
                    eng.tensor_scalar(stat[:, 1, at_], stat[:, 0, at_], 1.0 / D, EPS, ALU.mult, ALU.add).then_inc(sem["mean"], tally.up("mean"))
                    eng.wait_ge(sem["root"], tally.take("root"))
                    eng.reciprocal(stat[:, 0, at_], stat[:, 2, at_]).then_inc(sem["dve_own"], tally.up("dve_own"))
                    eng.wait_ge(sem["dve_own"], tally.now("dve_own"))
                    for t in range(b * p.TB, (b + 1) * p.TB):
                        eng.tensor_scalar(x_tile[:, t, :], x_tile[:, t, :], stat[:, 0, t:t + 1], None, ALU.mult).then_inc(sem["normed"], tally.up("normed"))

                    def low(k):
                        eng.wait_ge(sem["hT_high"], tally.take("hT_high"))
                        c = slice(b * p.BW, (b + 1) * p.BW)
                        tt(hT[1][:, k, c], n_tmp[:, k % 2, 0:p.BW], hT[0][:, k, c].bitcast(F32), ALU.subtract).then_inc(sem["dve_own"], tally.up("dve_own"))
                    for k in range(KT):
                        eng.wait_ge(sem["turned"], tally.take("turned"))
                        eng.wait_ge(sem["dve_own"], tally.now("dve_own"))
                        eng.tensor_scalar(n_tmp[:, k % 2, 0:p.BW], ps[:, k % 4, 0:p.BW], mod[:, p.s, 0, k:k + 1],
                                               mod[:, p.s, 1, k:k + 1], ALU.mult, ALU.add).then_inc(sem["hT_pre"], tally.up("hT_pre"))
                        if k:
                            low(k - 1)
                    low(KT - 1)

            def placed(p, t):
                eng.wait_ge(sem["proj_out"], 2 + tile_no[p.n, t] + 1)

            def to(p, t, outs, last=True):
                src = buf[raw_no[p.n, t] % 2]
                placed(p, t)
                if not p.ctx:
                    eng.wait_ge(sem["raw_free"], tally.now("raw_free"))
                    eng.stream_shuffle(turned[:, 0:p.T], src[:, 0:p.T], [(i + 16) % 32 for i in range(32)]).then_inc(sem["dve_own"], tally.up("dve_own"))
                    eng.wait_ge(sem["dve_own"], tally.now("dve_own"))
                    tt(src[:, 0:p.T], src[:, 0:p.T], rope[:, 0, :]).then_inc(sem["dve_own"], tally.up("dve_own"))
                    tt(turned[:, 0:p.T], turned[:, 0:p.T], rope[:, 1, :]).then_inc(sem["dve_own"], tally.up("dve_own"))
                    eng.wait_ge(sem["dve_own"], tally.now("dve_own"))
                for n, (dst, row, rows) in enumerate(outs):
                    x = src[row:row + rows, 0:p.T]
                    ins = eng.tensor_copy(dst, x) if p.ctx else tt(dst, x, turned[row:row + rows, 0:p.T], ALU.add)
                    ins.then_inc(sem["raw_free"], tally.up("raw_free")) if last and n == len(outs) - 1 else ins.then_inc(sem["dve_own"], tally.up("dve_own"))

            def save_values(p, t, dst):
                eng.wait_ge(sem["v_turned"], turned_no[p.n, t] + 1)
                if p.NT == 8:
                    eng.tensor_copy(dst[:, 0:4, :], ps[:, 4, :].rearrange("p (n d) -> p n d", d=P)).then_inc(sem["dve_own"], tally.up("dve_own"))
                n0 = p.NT - p.NT // p.NB
                eng.tensor_copy(dst[:, n0:p.NT, :], ps[:, 3 + p.NB, 0:(p.NT - n0) * P]
                                     .rearrange("p (n d) -> p n d", d=P)).then_inc(sem["raw_free"], tally.up("raw_free"))

            def halves(first, second):
                return [(place[r:r + HD], row, HD) for place, row in ((first, 0), (second, HD)) for r in (0, HD)]

            def a_keys(p):
                if p.ctx:
                    to(p, A_K, halves(kd_c[:, 0, :], kd_c[:, 1, :]))
                    save_values(p, A_V, v_c)
                    return
                key = buf[raw_no[p.n, A_K] % 2]
                to(p, A_K, [(key[:, :], 0, P)], False)
                eng.wait_ge(sem["dve_own"], tally.now("dve_own"))
                for which in range(2):
                    outs = halves(kx[:, 0, which, :], kx[:, 1, which, :])
                    for n, (dst, row, rows) in enumerate(outs):
                        src = key[row:row + rows, :]
                        if which == 0:
                            ins = eng.tensor_copy(dst, src)
                        else:
                            high = kx[row:row + rows, row // HD, 0, :]
                            ins = tt(dst, src, high.bitcast(F32), ALU.subtract)
                        name = "raw_free" if which and n == len(outs) - 1 else "dve_own"
                        ins.then_inc(sem[name], tally.up(name))
                    eng.wait_ge(sem["dve_own"], tally.now("dve_own"))
                for b in range(p.NB):
                    eng.wait_ge(sem["v_high"], tally.take("v_high"))
                    at_ = slice(4 * b, 4 * b + 4)
                    name = "raw_free" if b == p.NB - 1 else "dve_own"
                    tt(vx[:, at_, :, 1, :], ps[:, 4 + b, :].rearrange("p (t k d) -> p t k d", k=2, d=HD),
                       vx[:, at_, :, 0, :].bitcast(F32), ALU.subtract).then_inc(sem[name], tally.up(name))

            def r_keys(p):
                for j in range(2):
                    to(p, R_K + j, [(rk[:, j, 0:p.T], 0, P)])
                for j in range(2):
                    save_values(p, R_V + j, rv[:, 0:p.NT, j, :])

            def attention(p):
                steps = [(qb, h) for qb in range(p.NT) for h in range(HEADS)]

                def width(qb):
                    return 0 if p.ctx else (3 - (qb == 0) - (qb == p.NT - 1)) * P

                def queries(m):
                    qb, kv = m // 2, m % 2
                    eng.wait_ge(sem["q_high"], tally.take("q_high"))
                    for hh in range(2):
                        rows, t = slice(hh * HD, hh * HD + HD), slice(2 * kv, 2 * kv + 2)
                        other = slice(HD - hh * HD, P - hh * HD)
                        ins = tt(qs[other, qb % 2, t, hh, :], qT[rows, t, qb * P:(qb + 1) * P],
                                 qs[rows, qb % 2, t, hh, :].bitcast(F32), ALU.subtract)
                        ins.then_inc(sem["q_split"], tally.up("q_split")) if hh else ins.then_inc(
                            sem["dve_own"], tally.up("dve_own"))

                def maximum(n):
                    c = 2 * (n % 2)
                    eng.wait_ge(sem["score"], tally.take("score"))
                    view = ps[:, c:c + 2, :].rearrange("p a n -> p (a n)")[:, 512 - width(steps[n][0]):512 + CTX]
                    eng.tensor_reduce(soft[:, n % 4, 0:1], view, AX.X, ALU.max).then_inc(
                        sem["max_own"], tally.up("max_own"))

                def bias(n):
                    k, h = n % 4, steps[n][1]
                    eng.wait_ge(sem["max_own"], tally.now("max_own"))
                    eng.tensor_scalar(soft[:, k, 1:2], soft[:, k, 0:1], -SCALE, sink[:, 1, h:h + 1],
                                      ALU.mult, ALU.min).then_inc(sem["max"], tally.up("max"))

                def total(n):
                    k = n % 4
                    eng.wait_ge(sem["prob"], tally.take("prob"))
                    tt(soft[:, k, 4:5], soft[:, k, 2:3], soft[:, k, 3:4], ALU.add).then_inc(
                        sem["dve_own"], tally.up("dve_own"))

                def scale(n):
                    k, w = n % 4, width(steps[n][0]) + CTX
                    eng.wait_ge(sem["dve_own"], tally.now("dve_own"))
                    eng.reciprocal(soft[:, k, 5:6], soft[:, k, 4:5]).then_inc(sem["dve_own"], tally.up("dve_own"))
                    eng.wait_ge(sem["dve_own"], tally.now("dve_own"))
                    eng.tensor_scalar(prob[:, n % 3, 0:w], prob[:, n % 3, 0:w], soft[:, k, 5:6], None,
                                      ALU.mult).then_inc(sem["prob_scaled"], tally.up("prob_scaled"))

                def low(n):
                    qb, h = steps[n]
                    count = (width(qb) + CTX) // P
                    eng.wait_ge(sem["probT_high"], tally.take("probT_high"))
                    src = turned_view(n, count)
                    tt(pT_lo[:, 0:count, h % 4, :], src, pT_hi[:, 0:count, h % 4, :].bitcast(F32),
                       ALU.subtract).then_inc(sem["probT_saved"], tally.up("probT_saved"))

                def add_halves(g):
                    eng.wait_ge(sem["out_low"], tally.take("out_low"))
                    if tally.now("gated") + g > 1:
                        eng.wait_ge(sem["gated"], tally.now("gated", g - 1))
                    for half in range(2):
                        rows = slice(half * HD, half * HD + HD)
                        ins = tt(o_sum[rows, g % 2, :, :], ps[0:HD, 7, :].rearrange("p (h n) -> p h n", h=4)[:, half::2, :],
                                 o_low[:, half::2, :], ALU.add)
                        ins.then_inc(sem["out_sum"], tally.up("out_sum")) if half else ins.then_inc(
                            sem["dve_own"], tally.up("dve_own"))

                eng.wait_ge(sem["a_split_high"], tally.take("a_split_high"))
                tt(kc[:, :, 1, :], kd_c[:, :, :], kc[:, :, 0, :].bitcast(F32), ALU.subtract).then_inc(
                    sem["dve_own"], tally.up("dve_own"))
                tt(vc[:, :, :, 1, :], v_c[:, :, :].rearrange("p t (k d) -> p t k d", k=2),
                   vc[:, :, :, 0, :].bitcast(F32), ALU.subtract).then_inc(sem["a_split"], tally.up("a_split"))
                groups = len(steps) // 4
                queries(0)
                queries(1)
                maximum(0)
                bias(0)
                maximum(1)
                for n in range(len(steps)):
                    total(n)
                    if n + 1 < len(steps):
                        bias(n + 1)
                    scale(n)
                    if n:
                        low(n - 1)
                    if n + 2 < len(steps):
                        maximum(n + 2)
                    if n > 4 and n % 4 == 1:
                        add_halves(n // 4 - 1)
                    if n % 4 == 3 and n // 4 + 2 < groups:
                        queries(n // 4 + 2)
                low(len(steps) - 1)
                add_halves(groups - 1)
                tally.skip("gated", groups)
                eng.wait_ge(sem["gated"], tally.now("gated"))

            def convolution(p):
                for j in range(2):
                    src = buf[raw_no[p.n, B_C + j] % 2]
                    placed(p, B_C + j)
                    eng.memset(c_cu[:, j, 1:2], 0.0).then_inc(sem["dve_own"], tally.up("dve_own"))
                    eng.memset(c_cu[:, j, 2 + p.T:3 + p.T], 0.0).then_inc(sem["dve_own"], tally.up("dve_own"))
                    tt(c_cu[:, j, 2:2 + p.T], src[:, 0:p.T], c_u[:, j, 0:p.T]).then_inc(sem["raw_free"], tally.up("raw_free"))
                    eng.wait_ge(sem["raw_free"], tally.now("raw_free"))
                    eng.wait_ge(sem["dve_own"], tally.now("dve_own"))
                    y, u = c_y[:, j, 0:p.T], c_cu[:, j, :]
                    eng.tensor_scalar(y, u[:, 1:1 + p.T], convw[:, j, 0:1], convw[:, j, 3:4], ALU.mult, ALU.add).then_inc(sem["dve_own"], tally.up("dve_own"))
                    eng.wait_ge(sem["dve_own"], tally.now("dve_own"))
                    eng.scalar_tensor_tensor(y, u[:, 2:2 + p.T], convw[:, j, 1:2], y, ALU.mult, ALU.add).then_inc(sem["dve_own"], tally.up("dve_own"))
                    eng.wait_ge(sem["dve_own"], tally.now("dve_own"))
                    eng.scalar_tensor_tensor(y, u[:, 3:3 + p.T], convw[:, j, 2:3], y, ALU.mult, ALU.add).then_inc(sem["dve_own"], tally.up("dve_own"))
                    eng.wait_ge(sem["dve_own"], tally.now("dve_own"))
                    tt(y, y, c_b[:, j, 0:p.T]).then_inc(sem["dve_own"], tally.up("dve_own"))
                    eng.wait_ge(sem["dve_own"], tally.now("dve_own"))
                for j in range(2):
                    placed(p, B_Z + j)
                    zz = z_tile(p, Z_B + j)[:, :, 0, :]
                    tt(zz, zz, c_y[:, j, 0:p.T].rearrange("p (b n) -> p b n", b=p.NB)).then_inc(sem["dve_own"], tally.up("dve_own"))

            def decay_tables():
                eng.wait_ge(sem["ret_exp"], tally.take("ret_exp", RH))
                for d in range(2):
                    side = r_tab[:, 1 + 2 * d, :].unsqueeze(1).to_broadcast([P, RH, P])
                    tt(r_e[:, :, d, :], r_e[:, :, d, :], side).then_inc(sem["dve_own"], tally.up("dve_own"))
                eng.wait_ge(sem["dve_own"], tally.now("dve_own"))
                tt(dt_[:, :, :], r_e[:, :, 0, :], r_e[:, :, 1, :], ALU.add).then_inc(sem["dve_own"], tally.up("dve_own"))

            def scan(p, d, s):
                rows = slice(d * HD, (d + 1) * HD)
                order = list(range(p.NT))[::-1] if d else list(range(p.NT))
                new = r_prev[rows, order[s + 1], :, :] if s + 1 < p.NT else state_c[rows, :, :]
                for h in range(RH):
                    eng.scalar_tensor_tensor(new[:, h, :], r_prev[rows, order[s], h, :], gch[rows, h:h + 1],
                                             r_inc[rows, order[s], h, :], ALU.mult, ALU.add).then_inc(
                                                 sem["dve_own"], tally.up("dve_own"))

            def states(p):
                for d in range(2):
                    rows = slice(d * HD, (d + 1) * HD)
                    dst = r_prev[rows, d * (p.NT - 1), :, :]
                    (eng.memset(dst, 0.0) if p.ctx else eng.tensor_copy(dst, state_c[rows, :, :])).then_inc(sem["dve_own"], tally.up("dve_own"))

                def taken(i):
                    eng.wait_ge(sem["inc_saved"], tally.take("inc_saved"))
                    eng.wait_ge(sem["dve_own"], tally.now("dve_own"))
                    scan(p, i % 2, i // 2)
                for i in range(p.NT):
                    eng.wait_ge(sem["k_turned"], tally.take("k_turned"))
                    k = ps[:, 4 + i % 2, 0:RH * HD].rearrange("p (h d) -> p h d", h=RH)
                    for d in range(2):
                        ins = tt(r_kz[:, i % 2, :, d, :], k, zeta[:, d, :].unsqueeze(2).to_broadcast([P, RH, HD]))
                        ins.then_inc(sem["kz"], tally.up("kz")) if d else ins.then_inc(sem["dve_own"], tally.up("dve_own"))
                    if i > 1:
                        taken(i - 2)
                for i in range(p.NT - 2, p.NT):
                    taken(i)

            def last_states(p, i):
                s = p.NT // 2 + i
                if s < (p.NT if p.ctx else p.NT - 1):
                    eng.wait_ge(sem["dve_own"], tally.now("dve_own"))
                    for d in range(2):
                        scan(p, d, s)

            def retention(p):
                order = outside_in(p)[::-1]

                def center(i):
                    n = order[i]
                    m = slice(n * RH, (n + 1) * RH)
                    eng.wait_ge(sem["ret_y_saved"], tally.take("ret_y_saved"))
                    eng.tensor_scalar(r_stat[:, 0, m], r_stat[:, 0, m], 1.0 / HD, None, ALU.mult).then_inc(sem["dve_own"], tally.up("dve_own"))
                    eng.wait_ge(sem["dve_own"], tally.now("dve_own"))
                    tt(r_y[:, n, :, :], r_y[:, n, :, :], r_stat[:, 0, m].unsqueeze(2).to_broadcast([P, RH, HD]),
                       ALU.subtract).then_inc(sem["ret_mean"], tally.up("ret_mean"))
                for i, n in enumerate(order):
                    eng.wait_ge(sem["sT"], tally.take("sT"))
                    if i > 1:
                        eng.wait_ge(sem["ret_y"], tally.take("ret_y"))
                    for h in range(2):
                        ins = tt(r_sc[:, i % 2, h::2, :],
                                 ps[:, i % 2 + 4 * h, 0:2 * P].rearrange("p (j n) -> p j n", j=2), dt_[:, h::2, :])
                        ins.then_inc(sem["sc"], tally.up("sc")) if h else ins.then_inc(sem["dve_own"], tally.up("dve_own"))
                    if i % 2 == 0:
                        last_states(p, i // 2)
                    if i > 1:
                        center(i - 2)
                for i in range(p.NT - 2, p.NT):
                    center(i)
                tally.skip("ret_y", 2)
                m = p.NT * RH
                eng.wait_ge(sem["ret_square"], tally.take("ret_square", m))
                eng.tensor_scalar(r_stat[:, 1, 0:m], r_stat[:, 3, 0:m], 1.0 / HD, EPS, ALU.mult, ALU.add).then_inc(sem["ret_var"], tally.up("ret_var"))
                eng.wait_ge(sem["ret_root"], tally.take("ret_root"))
                eng.reciprocal(r_stat[:, 0, 0:m], r_stat[:, 2, 0:m]).then_inc(sem["dve_own"], tally.up("dve_own"))
                eng.wait_ge(sem["dve_own"], tally.now("dve_own"))
                eng.wait_ge(sem["ret_mean"], tally.now("ret_mean"))
                for b in range(p.NB):
                    g, c = slice(b * p.TB * RH, (b + 1) * p.TB * RH), slice(b * p.TB, (b + 1) * p.TB)
                    y = r_y[:, c, :, :].rearrange("p c h d -> p (c h) d")
                    tt(y, y, r_stat[:, 0, g].unsqueeze(2).to_broadcast([P, p.TB * RH, HD])).then_inc(sem["ret_norm"], tally.up("ret_norm"))
                for b in range(p.NB):
                    for j in range(2):
                        eng.wait_ge(sem["ret_yT"], tally.take("ret_yT"))
                        zz = z_pass[p.s][:, b, Z_R + j, :]
                        tt(zz, ps[:, 4 + 2 * j + b, 0:p.BW], zz).then_inc(sem["dve_own"], tally.up("dve_own"))

            def fourier(p):
                for n in range(p.NT):
                    eng.wait_ge(sem["four_hi"], tally.take("four_hi"))
                    tt(f_ab[1][:, n, :, :, :].rearrange("p j c n -> p (j c n)"), ps[:, 4 + n % 2, :],
                            f_ab[0][:, n, :, :, :].bitcast(F32).rearrange("p j c n -> p (j c n)"), ALU.subtract).then_inc(sem["four_done"], tally.up("four_done"))
                placed(p, F_Z + 1)
                eng.wait_ge(sem["w_used"], tally.now("w_used__done", units_of(p)[0]))
                for half in range(p.NB):
                    for j in range(2):
                        zz = z_pass[p.s][:, half, Z_F + j, :]
                        tt(zz, ps[:, 4 + 2 * half + j, 0:p.BW], zz).then_inc(sem["dve_own"], tally.up("dve_own"))

            def units_of(p):
                return 2 * F_Z + (2 if p.ctx else 32), 2 * MERGE + (2 if p.ctx else 32)

            def gated_low(p, b):
                for tile, count in BRANCH:
                    eng.wait_ge(sem["y_hi"], tally.take("y_hi"))
                    tt(yT[1][1][:, tile:tile + count, 0:p.BW], z_pass[p.s][:, b, tile:tile + count, :],
                            yT[1][0][:, tile:tile + count, 0:p.BW].bitcast(F32), ALU.subtract).then_inc(sem["y_split"], tally.up("y_split"))

            def merge(p, b):
                tmp = tmp_blk[b]
                eng.wait_ge(sem["y_split"], tally.now("y_split"))
                acc = tmp[:, 2, 0:p.BW]

                def body(i):
                    for j in range(4):
                        eng.wait_ge(sem["gate"], tally.take("gate"))
                        eng.wait_ge(sem["w_used"], tally.take("w_used__done", 3))
                        g, o = tmp[:, j % 2, 0:p.BW], ps[:, 2 + j % 2, 0:p.BW]
                        eng.wait_ge(sem["dve_own"], tally.now("dve_own"))
                        if j == 0:
                            tt(acc, g, o).then_inc(sem["opart_free"], tally.up("opart_free"))
                        else:
                            t = tmp[:, 3, 0:p.BW]
                            tt(t, g, o).then_inc(sem["opart_free"], tally.up("opart_free"))
                            eng.wait_ge(sem["opart_free"], tally.now("opart_free"))
                            tt(acc, acc, t, ALU.add).then_inc(sem["dve_own"], tally.up("dve_own"))
                    eng.wait_ge(sem["dve_own"], tally.now("dve_own"))
                    eng.tensor_copy(tot[0][:, bass.ds(i, 1), 0:p.BW], acc.unsqueeze(1)).then_inc(sem["dve_own"], tally.up("dve_own"))
                    eng.wait_ge(sem["dve_own"], tally.now("dve_own"))
                    tt(tot[1][:, bass.ds(i, 1), 0:p.BW], acc.unsqueeze(1),
                            tot[0][:, bass.ds(i, 1), 0:p.BW].bitcast(F32), ALU.subtract).then_inc(sem["tot_done"], tally.up("tot_done"))
                    eng.wait_ge(sem["tot_done"], tally.now("tot_done"))
                tally.loop(KT, body, gate=4, w_used__done=12, opart_free=4, dve_own=4, tot_done=1)
                if b + 1 < p.NB:
                    gated_low(p, b + 1)
                y, x = results(p, b)
                eng.wait_ge(sem["row_in"], tally.take("row_in", 16))
                for half in range(2):
                    eng.wait_ge(sem["w_used"], tally.take("w_used__done", KT))
                    for t in range(p.TB):
                        tt(y[:, 2 * t + half, :], ps[:, 4 - 4 * half + t, :],
                           gp_blk[b][:, half * 512:(half + 1) * 512]).then_inc(sem["y_gate"], tally.up("y_gate"))
                eng.wait_ge(sem["y_out"], tally.take("y_out", 2 * p.TB))
                tt(stat[:, 1, 4:4 + p.TB], stat[:, 0, 0:p.TB], stat[:, 0, 4:4 + p.TB], ALU.add).then_inc(sem["dve_own"], tally.up("dve_own"))
                eng.wait_ge(sem["dve_own"], tally.now("dve_own"))
                eng.tensor_scalar(stat[:, 1, 0:p.TB], stat[:, 1, 4:4 + p.TB], 1.0 / D, EPS, ALU.mult, ALU.add).then_inc(sem["out_mean"], tally.up("out_mean"))
                eng.wait_ge(sem["out_root"], tally.take("out_root"))
                eng.reciprocal(stat[:, 1, 0:p.TB], stat[:, 2, 0:p.TB]).then_inc(sem["dve_own"], tally.up("dve_own"))
                eng.wait_ge(sem["dve_own"], tally.now("dve_own"))
                eng.wait_ge(sem["post_in"], tally.take("post_in", 16 * p.TB))
                eng.wait_ge(sem["y_gate"], tally.now("y_gate"))
                for t in range(p.TB):
                    at_ = slice(2 * t, 2 * t + 2)
                    eng.scalar_tensor_tensor(x[:, at_, :], y[:, at_, :], stat[:, 1, t:t + 1], x[:, at_, :], ALU.mult, ALU.add).then_inc(sem["x_new"], tally.up("x_new"))

            constants()
            stage_end(eng, tally, "dve")
            for p in passes:
                if p.ctx:
                    modulation(p.layer)
                    stage_end(eng, tally, "dve")
                norm(p)
                stage_end(eng, tally, "dve")
                if not p.full:
                    a_keys(p)
                    r_keys(p)
                    tally.skip("w_used__done", 2 * len(p.tiles))
                    stage_end(eng, tally, "dve")
                    states(p)
                    last_states(p, 0)
                    stage_end(eng, tally, "dve")
                    continue
                if not p.ctx:
                    eng.wait_ge(sem["rope_in"], tally.take("rope_in", 16))
                for t in range(4):
                    to(p, A_Q + t, [(qT[:, t, 0:p.T], 0, P)])
                a_keys(p)
                stage_end(eng, tally, "dve")
                attention(p)
                stage_end(eng, tally, "dve")
                convolution(p)
                decay_tables()
                stage_end(eng, tally, "dve")
                if not p.ctx:
                    eng.wait_ge(sem["rope_in"], tally.take("rope_in", 16))
                for j in range(2):
                    to(p, R_Q + j, halves(qd[:, 2 * j, 0:p.T], qd[:, 2 * j + 1, 0:p.T]))
                r_keys(p)
                stage_end(eng, tally, "dve")
                states(p)
                retention(p)
                stage_end(eng, tally, "dve")
                fourier(p)
                tally.skip("w_used__done", units_of(p)[1])
                stage_end(eng, tally, "dve")
                gated_low(p, 0)
                for b in range(p.NB):
                    merge(p, b)
                stage_end(eng, tally, "dve")


INPUTS = ("x", "ctx", "w_ada", "b_ada", "norm_post", "w_in", "attn_sink", "ret_decay", "w_o_attn", "w_out")
TABLES = ("rope", "dft_x", "dft_c", "dft_head", "mask", "ident", "ret", "small")


def kernel(**inputs):
    import concourse.bacc as bacc
    from concourse.bass_utils import run_bass_kernel_spmd

    nc = bacc.Bacc("TRN2", target_bir_lowering=False, num_devices=1)
    arrays = {n: np.ascontiguousarray(inputs[n]) for n in INPUTS}
    arrays["w_o_rest"] = np.concatenate([inputs["w_o_conv"], inputs["w_o_ret"], inputs["w_o_fourier"]], axis=1)
    arrays["c_cols"] = np.stack([np.reshape(inputs["c"], (KT, P)), np.reshape(inputs["c_ctx"], (KT, P))]).transpose(2, 0, 1)
    arrays["norm_pre_cols"] = np.reshape(inputs["norm_pre"], (DEPTH, KT, P)).transpose(0, 2, 1)
    conv = np.concatenate([inputs["conv_w"], np.asarray(inputs["conv_b"])[:, None, :]], axis=1)
    arrays["conv_cols"] = conv.reshape(DEPTH, 4, 2, P).transpose(0, 3, 2, 1)
    arrays = {n: np.ascontiguousarray(v) for n, v in arrays.items()}
    arrays.update(tables())
    arrays = {f"in_{n}": v for n, v in arrays.items()}
    aps = {n[3:]: nc.dram_tensor(n, v.shape, mybir.dt.from_np(v.dtype), kind="ExternalInput").ap()
           for n, v in arrays.items()}
    out = nc.dram_tensor("out", (1, SEQ, D), F32, kind="ExternalOutput").ap()
    trunk(nc, aps, out)
    return run_bass_kernel_spmd(nc, [arrays], core_ids=[0]).results[0]["out"]
```

```python
from contextlib import ExitStack

import concourse.bass as bass
from concourse import mybir
import numpy as np

F32 = mybir.dt.float32
F32R = mybir.dt.float32r
BF16 = mybir.dt.bfloat16
ALU = mybir.AluOpType
ACT = mybir.ActivationFunctionType
AX = mybir.AxisListType

P = 128
D = 1024
KT = D // P
SEQ = 1024
CTX = 256
DEPTH = 2
GRID_W = 64
HD = 64
EPS = 1e-6
NEG = -1e30
HEADS = 8
RH = 4
SCALE = HD ** -0.5
UNIT = 512
RING = 4
LOOK = 3
ADA_AHEAD = 5
SBUF_START = 16512

A_Q, A_K, A_V, A_Z, B_U, B_B, B_C, B_Z, R_Q, R_K, R_V, R_Z, F_U, F_Z, MERGE = (
    0, 4, 5, 6, 10, 12, 14, 16, 18, 20, 22, 24, 26, 28, 30)
Z_A, Z_B, Z_R, Z_F, ZT = 0, 4, 6, 8, 10
BRANCH = ((Z_A, 4), (Z_B, 2), (Z_R, 2), (Z_F, 2))


class Pass:

    def __init__(self, layer, ctx, full):
        self.layer, self.ctx, self.full = layer, ctx, full
        self.s = 1 if ctx else 0
        self.T = CTX if ctx else SEQ
        self.BW = min(512, self.T)
        self.NB = self.T // self.BW
        self.NT = self.T // P
        self.TB = self.BW // P


class Count:

    def __init__(self, eng):
        self.eng, self.n, self.i, self.per = eng, {}, None, {}

    def now(self, name, more=0):
        v = self.n.get(name, 0) + more
        if self.i is not None and self.per.get(name):
            return self.i * self.per[name] + v
        return v

    def take(self, name, by=1):
        self.n[name] = self.n.get(name, 0) + by
        return self.now(name)

    def up(self, name, by=1):
        self.n[name] = self.n.get(name, 0) + by
        return by

    def skip(self, name, by):
        self.n[name] = self.n.get(name, 0) + by

    def loop(self, times, body, **per):
        before = dict(self.n)
        with self.eng.Fori(0, times) as i:
            self.i, self.per = i, per
            body(i)
            self.i, self.per = None, {}
        for name in self.n:
            made = self.n[name] - before.get(name, 0)
            assert made == per.get(name, 0), (name, made, per.get(name, 0))
            self.n[name] = before.get(name, 0) + times * made


def tables():
    out = {}
    n = np.arange(SEQ)
    half = HD // 2
    inv = (10000.0 ** (-np.arange(0, half, 2, dtype=np.float64) / half)).astype(np.float32)
    pos = np.stack([n // GRID_W, n % GRID_W]).astype(np.float32)
    p = np.arange(P) % HD
    axis, r = p // 32, p % 32
    ang = (pos[axis] * inv[r % 16][:, None]).astype(np.float64)
    sign = np.where(r < 16, -1.0, 1.0)[:, None]
    out["rope"] = np.stack([np.cos(ang), sign * np.sin(ang)], 1).astype(np.float32)
    k = np.arange(CTX)
    a = 2 * np.pi * (np.outer(k, k) % CTX) / CTX
    out["dft_c"] = np.stack([np.cos(a), np.sin(a)]).astype(np.float32)
    n, m = np.arange(SEQ // 2), np.arange(SEQ // 2)
    a = np.stack([2 * np.pi * (np.outer(n, 2 * m + odd) % SEQ) / SEQ for odd in range(2)])
    out["dft_x"] = np.stack([np.cos(a), np.sin(a)], 1).astype(np.float32)
    k = np.arange(HD)
    a = 2 * np.pi * (np.outer(k, k) % HD) / HD
    bd = np.zeros((2, P, 2, P), np.float64)
    for s, size in enumerate((SEQ, CTX)):
        norm = (size * HD) ** -0.5
        for g in range(2):
            bd[s, g * HD:(g + 1) * HD, 0, g * HD:(g + 1) * HD] = np.cos(a) * norm
            bd[s, g * HD:(g + 1) * HD, 1, g * HD:(g + 1) * HD] = -np.sin(a) * norm
    out["dft_head"] = bd.astype(np.float32)
    i, j = np.arange(P)[:, None], np.arange(P)[None, :]
    out["mask"] = np.stack([np.where(j >= i, 0, NEG), np.where(j <= i, 0, NEG)], 1).astype(np.float32)
    out["ident"] = np.eye(P, dtype=np.float32)
    xidx = np.where(i < HD, j + 1, P - j)
    out["ret"] = np.stack([np.maximum(j - i, 0), SCALE * (j >= i), np.maximum(i - j, 0), SCALE * (i >= j), xidx], 1).astype(np.float32)
    out["small"] = np.concatenate([P - 1 - i, i], 1).astype(np.float32)
    return out


def trunk(nc, a, out):
    with ExitStack() as ctx:
        def at(name, shape, offset, dt=F32):
            words = int(np.prod(shape[1:])) * (1 if dt != BF16 else 0.5)
            assert SBUF_START + 4 * (offset + words) <= 229368, name
            return nc.alloc_sbuf_tensor_at(name, shape, dt, offset=SBUF_START + 4 * offset)

        hT = [at("hT_hi", [P, KT, SEQ], 0, F32R), at("hT_lo", [P, KT, SEQ], 8192, F32R)]
        Z = 16384
        z_pass = {0: at("z_x", [P, 2, ZT, 512], Z), 1: at("z_c", [P, 1, ZT, 256], Z)}
        RAW = Z + 2 * ZT * 512
        raw = at("w_raw", [P, RING, UNIT], RAW)
        w_hi = at("w_hi", [P, RING, UNIT], RAW + 2048, F32R)
        w_lo = at("w_lo", [P, RING, UNIT], RAW + 4096, F32R)
        W = RAW + 6144
        C = W + 18432

        class Const:
            top = C

        def const(name, shape, dt=F32):
            t = at(name, shape, Const.top, dt)
            words = int(np.prod(shape[1:]))
            Const.top += -(-(words if dt != BF16 else (words + 1) // 2) // 8) * 8
            return t

        ident = const("ident", [P, P])
        ones = const("ones", [P, P])
        ident_bf = const("ident_bf", [P, P], BF16)
        mask_bf = const("mask_bf", [P, 2, P], BF16)
        kd_c = const("keysT_ctx", [P, 2, CTX])
        v_c = const("values_ctx", [P, 2, P])
        state_c = const("state_ctx", [P, RH, HD])
        small = const("small", [P, 2])
        cT = const("cT", [P, 2, KT])
        sT = const("silu_cT", [P, 2, KT])
        gpre = const("norm_preT", [P, KT])
        mod = const("modT", [P, 2, 2, KT])
        sink = const("sink", [P, 2, HEADS])
        decay = const("decay", [P, 2 * RH])
        lg = const("log_gamma", [P, 2 * RH])
        lt = const("log_tmp", [P, 6, 2 * RH])
        lgd = const("log_gamma_dir", [P, RH])
        gch = const("gamma_chunk", [P, RH])
        zeta = const("zeta", [P, 2, RH])
        convw = const("conv_wT", [P, 2, 4])
        stat = const("token_stats", [P, 3, 8])
        n_stat = const("norm_stats", [P, 3, 8])
        soft = const("softmax_stats", [P, 4, 8])

        rope = at("rope", [P, 2, SEQ], W + 14336)
        buf = [at("proj_raw0", [P, SEQ], W + 10240), at("proj_raw1", [P, SEQ], W + 11264)]
        turned = at("rope_turned", [P, SEQ], W + 12288)
        w_ada = at("w_ada", [P, KT, 3 * D], 0)
        m_rows = at("mod_rows", [P, 3 * D], W)
        m_bias = at("mod_bias", [P, 3 * D], W + 3072)
        m_gpost = at("mod_gpost", [P, D], W + 6144)
        m_gate = at("mod_gate", [P, D], W + 7168)
        x_first = at("x_tile_first", [P, 4, D], Z + 4096)
        x_tile = at("x_tile", [P, 4, D], W + 10240)
        m_mask = at("mask_f32", [P, 2, P], W + 10240)
        n_sq = at("norm_square", [P, 4, 512], W + 14336)
        n_tmp = at("norm_tmp", [P, 4, 512], Z + 8192)
        qT = at("a_qT", [P, 4, SEQ], W)
        kx = at("a_kT", [P, 2, 2, SEQ], W + 4096, F32R)
        vx = at("a_v", [P, 8, 2, 2, HD], W + 8192, F32R)
        prob = at("a_prob", [P, 4, 640], W + 10240)
        pT_hi = at("a_probT_hi", [P, 5, 4, P], W + 12800, F32R)
        qs = at("a_q_split", [P, 2, 4, 2, P], W + 15360, F32R)
        o_low = at("a_out_low", [HD, 4, P], W + 17408)
        o_sum = at("a_out_sum", [P, 2, 2, P], W + 17920)
        kc = at("a_kT_ctx", [P, 2, 2, CTX], Z + 2048, F32R)
        vc = at("a_v_ctx", [P, 2, 2, 2, HD], Z + 3072, F32R)
        pT_lo = at("a_probT_lo", [P, 5, 4, P], Z + 7168, F32R)
        c_u = at("b_u", [P, 2, SEQ], W)
        c_b = at("b_b", [P, 2, SEQ], W + 2048)
        c_cu = at("b_cu", [P, 2, SEQ + 4], W + 4096)
        c_y = at("b_y", [P, 2, SEQ], W + 6400)
        qd = at("r_qT", [P, RH, SEQ], W)
        rk = at("r_kT", [P, 2, SEQ], W + 4096)
        rv = at("r_v", [P, 8, 2, P], W + 6144)
        r_prev = at("r_prev", [P, 8, RH, HD], W + 8192)
        r_inc = at("r_inc", [P, 8, RH, HD], W + 10240)
        r_kz = at("r_kzeta", [P, 2, RH, 2, HD], W + 12288)
        xi = at("r_xi", [P, RH, P], W + 13312)
        dt_ = at("r_decay", [P, RH, P], W + 13824)
        r_y = at("r_y", [P, 8, RH, HD], W + 14336)
        r_sc = at("r_scoresT", [P, 2, RH, P], W + 16384)
        r_qx = at("r_qxi", [P, 2, RH, P], W + 17408)
        r_sq = at("r_square", [P, HD], W + 12288)
        r_stat = at("r_stat", [P, 4, 8 * RH], W + 12352)
        r_e = at("r_exp", [P, RH, 2, P], W + 16384)
        r_tab = at("r_table", [P, 5, P], W + 17408)
        f_u = at("f_uT", [P, 2, SEQ], W)
        f_ab = [at("f_ab_hi", [P, 8, 2, 2, P], W + 2048, F32R), at("f_ab_lo", [P, 8, 2, 2, P], W + 6144, F32R)]
        f_fold = at("f_fold", [P, 2, 2, 512], W + 10240)
        f_bd = at("f_head", [P, 2 * P], W + 12544)
        yT = {1: [at("yT_hi", [P, ZT, 512], W, F32R), at("yT_lo", [P, ZT, 512], W + 5120, F32R)]}
        tot = [at("total_hi", [P, KT, 512], W + 10240, F32R), at("total_lo", [P, KT, 512], W + 14336, F32R)]
        y_post = at("y_post", [P, KT, 512], W)
        x_post = at("x_post", [P, KT, 512], W + 4096)
        y_first = at("y_post_first", [P, KT, SEQ], 0)
        x_post_first = at("x_post_first", [P, KT, SEQ], 8192)
        sq_junk = at("square_junk", [P, 512], Z + 3072)
        tmp_blk = [at(f"merge_tmp{b}", [P, 4, 512], Z + b * ZT * 512) for b in range(2)]
        gp_blk = [at(f"gate_row{b}", [P, D], Z + b * ZT * 512 + 2048) for b in range(2)]

        ps = ctx.enter_context(nc.psum_tensor("ps", [P, 8, 512], F32))

        x_mid = nc.dram_tensor("x_mid", (SEQ, D), F32, kind="Internal").ap()
        c_mid = nc.dram_tensor("c_mid", (CTX, D), F32, kind="Internal").ap()
        gate_rows = nc.dram_tensor("gate_rows", (DEPTH, 2, D), F32, kind="Internal").ap()

        names = (
            "act_own", "dve_own",
            "w_high", "w_split", "w_slot", "w_used",
            "const_in", "c_in", "small_in", "gate_out", "x_out", "rope_in", "ret_in", "head_in", "post_in",
            "silu_c", "mod_rows", "mod_saved", "mod_cols", "gate_made", "log_exp", "log_one", "log_ln",
            "log_gamma", "zeta_exp",
            "square", "mean", "root", "normed", "turned", "hT_pre", "hT_high", "hT_low", "hT_low_odd",
            "proj_out", "raw_free", "v_turned",
            "score", "max_own", "max", "prob", "one_over", "prob_scaled", "probT", "probT_high", "probT_saved", "pv",
            "a_split_high", "a_split", "v_high", "q_high", "q_split", "out_low", "out_sum", "gated",
            "ret_exp", "ret_qx", "k_turned", "kz", "inc", "inc_saved", "sT", "sc", "ret_y", "ret_y_saved",
            "ret_mean", "ret_square", "ret_var", "ret_root", "ret_norm", "ret_yT", "ret_done",
            "folded", "four", "four_hi", "four_done",
            "gate", "opart_free", "y_hi", "y_split", "tot_done",
            "y_gate", "y_out", "row_in", "out_mean", "out_root", "x_new",
        )
        sem = {n: ctx.enter_context(nc.semaphore(n)) for n in names}
        landed = [ctx.enter_context(nc.semaphore(f"w_landed{r}")) for r in range(RING)]
        x_in = [ctx.enter_context(nc.semaphore(f"x_in{t}")) for t in range(SEQ // P)]
        ada_in = [ctx.enter_context(nc.semaphore(f"w_ada_in{k}")) for k in range(KT)]
        ended = {who: ctx.enter_context(nc.semaphore(f"ended_{who}")) for who in ("act", "dve", "pe")}
        block = ctx.enter_context(nc.Block())

        def stage_end(eng, tally, who):
            eng.drain().then_inc(ended[who], tally.up(f"ended_{who}"))
            for other in ended:
                if other != who:
                    eng.wait_ge(ended[other], tally.take(f"ended_{other}"))

        def pe_goes_on(eng, tally):
            eng.drain().then_inc(ended["pe"], tally.up("ended_pe"))
            tally.skip("ended_act", 1)
            tally.skip("ended_dve", 1)

        passes = []
        for layer in range(DEPTH):
            passes.append(Pass(layer, True, layer < DEPTH - 1))
            passes.append(Pass(layer, False, True))

        units, tile_no, raw_no, turned_no = 0, {}, {}, {}
        for n, p in enumerate(passes):
            p.tiles = list(range(MERGE)) if p.full else [A_K, A_V, R_K, R_K + 1, R_V, R_V + 1]
            for t in p.tiles:
                tile_no[n, t] = len(tile_no)
                if t < A_Z or B_C <= t < B_Z or R_Q <= t < R_Z:
                    raw_no[n, t] = len(raw_no)
                if t in (A_V, R_V, R_V + 1):
                    turned_no[n, t] = len(turned_no)
            p.n = n
            p.units = 2 * len(p.tiles)
            p.stage = passes[n - 1].stage + passes[n - 1].stages if n else 1
            p.stages = 8 if p.full else 3
            if p.full:
                p.units += (2 if p.ctx else 16) + p.NB * (12 * KT + 2 * KT)
            units += p.units
        total_units = units

        def outside_in(p):
            return [c for k in range(p.NT // 2) for c in (k, p.NT - 1 - k)]

        def turned_at(n, count):
            first = 5 * 512 + 512 - P if n % 2 and count == 5 else (6 if n % 2 else 4) * 512
            return [((first + j * P) // 512, (first + j * P) % 512) for j in range(count)]

        def turned_view(n, count):
            first = turned_at(n, count)[0]
            start = (first[0] - 4) * 512 + first[1]
            return ps[:, 4:7, :].rearrange("p a n -> p (a n)")[:, start:start + count * P].rearrange(
                "p (j n) -> p j n", n=P)

        def results(p, b):
            if b < p.NB - 1:
                return y_first[:, :, 0:512], x_post_first[:, :, 0:512]
            return y_post[:, :, :], x_post[:, :, :]

        def token_tile(p, t):
            return x_first[:, t, :] if not p.ctx and t < p.TB else x_tile[:, t % p.TB, :]

        def z_tile(p, tile, count=1):
            return z_pass[p.s][:, 0:p.NB, tile:tile + count, :]

        def banks(first, p):
            return ps[:, first:first + p.NB, 0:p.BW]

        @block.sync
        def _(eng):
            tally = Count(eng)
            unit = [0]

            def load(source, shape=None):
                src = source() if callable(source) else source
                r = unit[0] % RING
                unit[0] += 1
                dst = raw[:, r, :]
                if shape:
                    dst = dst.rearrange(f"p ({' '.join(shape)}) -> p {' '.join(shape)}", **shape)
                eng.wait_ge(sem["w_split"], tally.take("w_split"))
                if tally.i is not None:
                    eng.sem_inc(sem["w_slot"], 1)
                eng.dma_start(dst, src).then_inc(landed[r], tally.up(f"w_landed{r}", 16))

            def rounds(times, body, units):
                assert units % RING == 0
                tally.loop(times, body, w_split=units, **{f"w_landed{r}": 16 * units // RING for r in range(RING)})

            def cols(w, k0, col, kk=4):
                return w[k0 * P:(k0 + kk) * P, bass.ds(eng.snap(col), P)].rearrange("(k p) n -> p k n", p=P)

            k4 = {"k": 4, "n": P}

            def tiles(l, first, count):
                w = a["w_in"][l]

                def body(i):
                    for t in range(2):
                        for u in range(2):
                            load(cols(w, 4 * u, i * (2 * P) + (first + t) * P), k4)
                rounds(count // 2, body, 4)

            def ada(layer, k):
                if k > 1:
                    eng.wait_ge(ada_in[k - 2], 16 * (layer + 1))
                eng.dma_start(w_ada[:, k, :], a["w_ada"][layer][k * P:(k + 1) * P, :]).then_inc(ada_in[k], 16)

            def modulation(p):
                if p.layer:
                    for who in ended:
                        eng.wait_ge(ended[who], p.stage)
                for k in range(ADA_AHEAD if p.layer else 0, KT):
                    ada(p.layer, k)

            def fourier(p):
                if p.ctx:
                    for n in range(2):
                        load(a["dft_c"][:, n * P:(n + 1) * P, :].rearrange("c p n -> p c n"), {"c": 2, "n": 256})
                    return
                for odd in range(2):
                    for n in range(4):
                        for c in range(2):
                            load(a["dft_x"][odd, c, n * P:(n + 1) * P, :])

            def merge(p, b):
                l = p.layer
                wo = ((a["w_o_attn"][l], 0), (a["w_o_rest"][l], 0), (a["w_o_rest"][l], 2), (a["w_o_rest"][l], 2))

                def body(i):
                    for j in range(4):
                        for u in range(2):
                            load(cols(a["w_in"][l], 4 * u, i * P + (MERGE + 8 * j) * P), k4)
                        load(cols(*wo[j], i * P), k4)
                rounds(KT, body, 12)
                for half in range(2):
                    for k in range(KT):
                        load(a["w_out"][l][k * P:(k + 1) * P, half * 512:(half + 1) * 512])
                        n = half * KT + k
                        if l + 1 < DEPTH and not p.ctx and b == p.NB - 1 and n % 3 == 2 and n // 3 < ADA_AHEAD:
                            if n // 3 == 0:
                                eng.wait_ge(sem["tot_done"], KT * sum(q.NB for q in passes[:p.n + 1] if q.full))
                                eng.wait_ge(sem["x_out"], 16 * (sum(q.NT for q in passes[:p.n + 1] if q.full) - p.TB))
                            ada(l + 1, n // 3)

            for p in passes:
                l = p.layer
                if not p.full:
                    tiles(l, A_K, 2)
                    modulation(p)
                    tiles(l, R_K, 4)
                    continue
                tiles(l, A_Q, 2)
                if p.ctx:
                    modulation(p)
                tiles(l, A_Q + 2, F_U - 2)
                tiles(l, F_U, 2)
                fourier(p)
                tiles(l, F_Z, 2)
                for b in range(p.NB):
                    merge(p, b)

        @block.gpsimd
        def _(eng):
            tally = Count(eng)
            eng.sem_inc(sem["w_split"], tally.up("w_split", RING))

            def low(r):
                eng.wait_ge(sem["w_high"], tally.take("w_high"))
                eng.tensor_tensor(w_lo[:, r, :], raw[:, r, :], w_hi[:, r, :].bitcast(F32),
                                  ALU.subtract).then_inc(sem["w_split"], tally.up("w_split"))

            unit = [0]

            def low_parts(last):
                while unit[0] % RING and unit[0] < last:
                    low(unit[0] % RING)
                    unit[0] += 1
                rounds = (last - unit[0]) // RING

                def body(i):
                    for r in range(RING):
                        low(r)
                if rounds:
                    tally.loop(rounds, body, w_high=RING, w_split=RING)
                    unit[0] += RING * rounds
                while unit[0] < last:
                    low(unit[0] % RING)
                    unit[0] += 1

            def attention(p):
                groups = p.NT * 2

                def gated(g):
                    qb, kv = g // 2, g % 2
                    eng.wait_ge(sem["out_sum"], tally.take("out_sum"))
                    zz = z_pass[p.s][:, qb // p.TB, 2 * kv:2 * kv + 2, (qb % p.TB) * P:(qb % p.TB + 1) * P]
                    eng.tensor_tensor(zz, o_sum[:, g % 2, :, :], zz, ALU.mult).then_inc(sem["gated"], tally.up("gated"))

                for n in range(p.NT * HEADS):
                    qb = n // HEADS
                    w = CTX + (0 if p.ctx else (3 - (qb == 0) - (qb == p.NT - 1)) * P)
                    eng.wait_ge(sem["one_over"], tally.take("one_over"))
                    eng.tensor_tensor(prob[:, n % 4, 0:w], prob[:, n % 4, 0:w], soft[:, n % 4, 5:6].to_broadcast([P, w]),
                                      ALU.mult).then_inc(sem["prob_scaled"], tally.up("prob_scaled"))
                    if n > 4 and n % 4 == 3:
                        gated(n // 4 - 1)
                gated(groups - 1)

            def retention(p):
                eng.wait_ge(ended["dve"], p.stage + 5)
                for i, n in enumerate(outside_in(p)[::-1]):
                    eng.wait_ge(sem["ret_y"], tally.take("ret_y"))
                    eng.tensor_tensor(r_qx[:, i % 2, :, :], qd[:, :, n * P:(n + 1) * P], xi[:, :, :],
                                      ALU.mult).then_inc(sem["ret_qx"], tally.up("ret_qx"))

            def norm(p):
                for b in range(p.NB):
                    for k in range(0, KT, 2):
                        eng.wait_ge(sem["hT_high"], tally.take("hT_high"))
                        c = slice(b * p.BW, (b + 1) * p.BW)
                        eng.tensor_tensor(hT[1][:, k, c], n_tmp[:, k % 4, 0:p.BW], hT[0][:, k, c].bitcast(F32),
                                          ALU.subtract).then_inc(sem["hT_low"], tally.up("hT_low"))
                        tally.skip("hT_high", 1)

            first = 0
            for p in passes:
                low_parts(first + LOOK)
                norm(p)
                if p.full:
                    low_parts(first + 2 * B_U + LOOK)
                    attention(p)
                    low_parts(first + 2 * F_U + LOOK)
                    retention(p)
                first += p.units
            low_parts(total_units)

        @block.tensor
        def _(eng):
            tally = Count(eng)
            eng.sem_inc(sem["w_used"], tally.up("w_used", RING))
            eng.sem_inc(sem["ret_y"], tally.up("ret_y", 2))
            tally.skip("w_split", RING)
            unit = [0]

            def mm(dst, lhsT, rhs, start, stop):
                return eng.matmul(dst, lhsT, rhs, start=start, stop=stop)

            def slot():
                eng.wait_ge(sem["w_split"], tally.take("w_split"))
                unit[0] += 1
                return (unit[0] - 1) % RING

            def three(dst, a_hi, a_lo, b_hi, b_lo, start, stop):
                mm(dst, a_hi, b_hi, start, False)
                mm(dst, a_hi, b_lo, False, False)
                return mm(dst, a_lo, b_hi, False, stop)

            def modulation(l):
                if l == 0:
                    eng.wait_ge(sem["silu_c"], tally.take("silu_c"))
                else:
                    eng.wait_ge(sem["y_out"], tally.now("y_out"))
                for k in range(KT):
                    eng.wait_ge(ada_in[k], 16 * (l + 1))
                    for n in range(6):
                        ins = mm(ps[0:2, n, :], sT[:, :, k], w_ada[:, k, n * 512:(n + 1) * 512], k == 0, k == KT - 1)
                        if k == KT - 1:
                            ins.then_inc(sem["mod_rows"], tally.up("mod_rows"))
                eng.wait_ge(sem["mod_saved"], tally.take("mod_saved", 6))
                for c in range(2 * KT):
                    last = eng.transpose(ps[:, 6, 2 * c:2 * c + 2], m_rows[0:2, c * P:(c + 1) * P], ident[0:2, 0:2])
                last.then_inc(sem["mod_cols"], tally.up("mod_cols"))

            def norm(p):
                for b in range(p.NB):
                    eng.wait_ge(sem["normed"], tally.take("normed", p.TB))
                    for k in range(KT):
                        eng.wait_ge(sem["hT_pre"], tally.take("hT_pre"))
                        for t in range(p.TB):
                            last = eng.transpose(ps[:, k % 4, t * P:(t + 1) * P],
                                                 token_tile(p, b * p.TB + t)[:, k * P:(k + 1) * P], ident[:, :])
                        last.then_inc(sem["turned"], tally.up("turned"))

            def project(p, count, first=False, between=None):
                def body(i, first=False):
                    for t in range(2):
                        if between and t:
                            between()
                        eng.wait_ge(sem["proj_out"], tally.take("proj_out"))
                        for u in range(2):
                            r = slot()
                            for b in range(p.NB):
                                if first and t == 0:
                                    for name in ("hT_low", "hT_low_odd"):
                                        eng.wait_ge(sem[name], tally.now(name, KT // 2 * b + 2 * u + 2))
                                for k in range(4):
                                    kk, at_ = 4 * u + k, slice(b * p.BW, (b + 1) * p.BW)
                                    w = slice(k * P, (k + 1) * P)
                                    last = three(ps[:, 2 * t + b, 0:p.BW], w_hi[:, r, w], w_lo[:, r, w],
                                                 hT[0][:, kk, at_], hT[1][:, kk, at_], kk == 0, kk == KT - 1)
                            last.then_inc(sem["w_used"], tally.up("w_used"))
                if between:
                    body(0)
                    count -= 2
                if first:
                    body(0, True)
                    tally.skip("hT_low", KT // 2 * p.NB)
                    tally.skip("hT_low_odd", KT // 2 * p.NB)
                    count -= 2
                if count:
                    tally.loop(count // 2, body, proj_out=2, w_split=4, w_used=4)

            def turn_values(p, t, before):
                eng.wait_ge(sem["proj_out"], 2 + tile_no[p.n, t] + 1)
                if before is not None:
                    eng.wait_ge(sem["raw_free"], 2 + raw_no[p.n, before] + 1)
                src = buf[raw_no[p.n, t] % 2]
                for n in range(p.NT):
                    last = eng.transpose(ps[:, 4 + n // 4, (n % 4) * P:(n % 4 + 1) * P],
                                         src[:, n * P:(n + 1) * P], ident[:, :])
                last.then_inc(sem["v_turned"], tally.up("v_turned"))

            def attention(p):
                steps = [(qb, h) for qb in range(p.NT) for h in range(HEADS)]

                def window(qb):
                    if p.ctx:
                        return 0, 0
                    return max(qb - 1, 0), min(qb + 1, p.NT - 1) + 1

                def scores(n):
                    qb, h = steps[n]
                    kv, c = h // 4, 2 * (n % 2)
                    lo, hi = window(qb)
                    q = qs[:, qb % 2, h // 2, h % 2, :]
                    if h % 4 == 0:
                        eng.wait_ge(sem["q_split"], tally.take("q_split"))
                    eng.wait_ge(sem["prob"], tally.take("prob"))
                    if hi > lo:
                        L = (hi - lo) * P
                        parts = []
                        if lo < qb:
                            parts.append((512 - L, 0))
                        if hi - 1 > qb:
                            parts.append((512 - P, 1))
                        mm(ps[:, c, 512 - L:512], q, kx[:, kv, 0, lo * P:hi * P], True, False)
                        mm(ps[:, c, 512 - L:512], q, kx[:, kv, 1, lo * P:hi * P], False, not parts)
                        for m, (col, which) in enumerate(parts):
                            mm(ps[:, c, col:col + P], ident_bf[:, :], mask_bf[:, which, :], False, m == len(parts) - 1)
                    mm(ps[:, c + 1, 0:CTX], q, kc[:, kv, 0, :], True, False)
                    mm(ps[:, c + 1, 0:CTX], q, kc[:, kv, 1, :], False, True).then_inc(sem["score"], tally.up("score"))

                def turn(n):
                    qb, h = steps[n]
                    lo, hi = window(qb)
                    places = turned_at(n, hi - lo + 2)
                    eng.wait_ge(sem["prob_scaled"], tally.take("prob_scaled"))
                    eng.wait_ge(sem["probT_saved"], tally.take("probT_saved"))
                    order = sorted(range(len(places)), key=lambda j: places[j][0] == 5)
                    for j in order:
                        bank, col = places[j]
                        if bank == 5:
                            eng.wait_ge(sem["probT_saved"], tally.now("probT_saved", 1))
                        last = eng.transpose(ps[:, bank, col:col + P], prob[:, n % 4, j * P:(j + 1) * P], ident[:, :])
                    last.then_inc(sem["probT"], tally.up("probT"))

                def values(n):
                    qb, h = steps[n]
                    lo, hi = window(qb)
                    kv, count, pair = h // 4, hi - lo + 2, h // 2 % 2
                    if pair == 0:
                        if tally.now("out_sum"):
                            eng.wait_ge(sem["out_sum"], tally.now("out_sum"))
                        tally.skip("out_sum", 1)
                    dst, heads = ps[:, 7, pair * 2 * P:(pair + 1) * 2 * P], slice(2 * pair, 2 * pair + 2)
                    for j in range(count):
                        v = vx[:, lo + j, kv, :, :] if j < hi - lo else vc[:, j - (hi - lo), kv, :, :]
                        mm(dst, v, pT_hi[:, j, heads, :], j == 0, False)
                        last = mm(dst, v, pT_lo[:, j, heads, :], False, j == count - 1)
                    if pair:
                        last.then_inc(sem["pv"], tally.up("pv"))

                eng.wait_ge(sem["a_split"], tally.take("a_split"))
                scores(0)
                scores(1)
                for n in range(len(steps) + 1):
                    if n + 2 < len(steps):
                        scores(n + 2)
                    if n:
                        turn(n - 1)
                    if n > 1 and n % 2 == 1:
                        eng.wait_ge(sem["probT_saved"], tally.now("probT_saved", 1))
                        values(n - 2)
                eng.wait_ge(sem["probT_saved"], tally.now("probT_saved", 2))
                values(len(steps) - 1)

            def states(p):
                order = outside_in(p)

                def turn_keys(i):
                    for j in range(2):
                        last = eng.transpose(ps[:, 4 + i % 2, j * P:(j + 1) * P],
                                             rk[:, j, order[i] * P:(order[i] + 1) * P], ident[:, :])
                    last.then_inc(sem["k_turned"], tally.up("k_turned"))
                turn_keys(0)
                for i, n in enumerate(order):
                    if i + 1 < p.NT:
                        turn_keys(i + 1)
                    eng.wait_ge(sem["kz"], tally.take("kz"))
                    eng.wait_ge(sem["inc_saved"], tally.take("inc_saved"))
                    for h in range(RH):
                        v = rv[:, n, h // 2, h % 2 * HD:h % 2 * HD + HD]
                        last = mm(ps[:, 6 + i % 2, h * HD:(h + 1) * HD], r_kz[:, i % 2, h, :, :], v, True, True)
                    last.then_inc(sem["inc"], tally.up("inc"))

            def retention(p):
                order = outside_in(p)[::-1]

                def scores(i):
                    c = slice(order[i] * P, (order[i] + 1) * P)
                    for h in range(RH):
                        rows = slice(h % 2 * HD, h % 2 * HD + HD)
                        last = mm(ps[:, i % 2 + 4 * (h % 2), h // 2 * P:(h // 2 + 1) * P], rk[rows, h // 2, c],
                                  qd[rows, h, c], True, True)
                    last.then_inc(sem["sT"], tally.up("sT"))
                scores(0)
                for i, n in enumerate(order):
                    if i + 1 < p.NT:
                        scores(i + 1)
                    eng.wait_ge(sem["sc"], tally.take("sc"))
                    eng.wait_ge(sem["ret_qx"], tally.take("ret_qx"))
                    eng.wait_ge(sem["ret_y_saved"], tally.take("ret_y_saved"))
                    for h in range(RH):
                        dst = ps[:, 2 + i % 2, h * HD:(h + 1) * HD]
                        v = rv[:, n, h // 2, h % 2 * HD:h % 2 * HD + HD]
                        mm(dst, r_sc[:, i % 2, h, :], v, True, False)
                        last = mm(dst, r_qx[:, i % 2, h, :], r_prev[:, n, h, :], False, True)
                    last.then_inc(sem["ret_y"], tally.up("ret_y"))
                eng.wait_ge(sem["ret_y_saved"], tally.now("ret_y_saved", 2))

                def turn_outputs():
                    for b in range(p.NB):
                        eng.wait_ge(sem["ret_norm"], tally.take("ret_norm"))
                        for j in range(2):
                            for t in range(p.TB):
                                last = eng.transpose(ps[:, 4 + 2 * j + b, t * P:(t + 1) * P],
                                                     r_y[:, b * p.TB + t, 2 * j:2 * j + 2, :], ident[:, :])
                            last.then_inc(sem["ret_yT"], tally.up("ret_yT"))
                project(p, 2, between=turn_outputs)

            def fourier(p):
                eng.wait_ge(sem["proj_out"], 2 + tile_no[p.n, F_U + 1] + 1)
                eng.wait_ge(sem["head_in"], tally.take("head_in", 16))
                if not p.ctx:
                    eng.wait_ge(sem["folded"], tally.take("folded", 2))
                for n in range(p.NT):
                    eng.wait_ge(sem["four_done"], tally.take("four_done"))
                    for j in range(2):
                        u = f_u[:, j, n * P:(n + 1) * P] if p.ctx else f_fold[:, j, n // 4, n % 4 * P:(n % 4 + 1) * P]
                        last = mm(ps[:, 4 + n % 2, j * 256:(j + 1) * 256], u, f_bd[:, :], True, True)
                    last.then_inc(sem["four"], tally.up("four"))
                eng.wait_ge(sem["four_done"], tally.now("four_done", 2))
                parts = 1 if p.ctx else 2
                for part in range(parts):
                    for n in range(p.NT // parts):
                        for c in range(2):
                            if not p.ctx or c == 0:
                                r = slot()
                            w = slice(c * p.BW, (c + 1) * p.BW) if p.ctx else slice(0, 512)
                            m = p.NT // parts * part + n
                            for j in range(2):
                                last = three(ps[:, 4 + 2 * part + j, 0:p.BW], f_ab[0][:, m, j, c, :],
                                             f_ab[1][:, m, j, c, :], w_hi[:, r, w], w_lo[:, r, w],
                                             n == 0 and c == 0, n == p.NT // parts - 1 and c == 1)
                            if not p.ctx or c == 1:
                                last.then_inc(sem["w_used"], tally.up("w_used"))

            def merge(p, b):
                at_ = slice(b * p.BW, (b + 1) * p.BW)
                if b:
                    eng.wait_ge(sem["y_out"], tally.now("y_out", 1 - p.TB))

                def body(i, first=False):
                    for j, (tile, count) in enumerate(BRANCH):
                        eng.wait_ge(sem["gate"], tally.take("gate"))
                        for u in range(2):
                            r = slot()
                            for k in range(4):
                                kk, w = 4 * u + k, slice(k * P, (k + 1) * P)
                                last = three(ps[:, j % 2, 0:p.BW], w_hi[:, r, w], w_lo[:, r, w],
                                             hT[0][:, kk, at_], hT[1][:, kk, at_], kk == 0, kk == KT - 1)
                            last.then_inc(sem["w_used"], tally.up("w_used"))
                        eng.wait_ge(sem["opart_free"], tally.take("opart_free"))
                        r = slot()
                        if first and b and j == 0:
                            eng.wait_ge(sem["y_out"], tally.now("y_out"))
                        if first:
                            eng.wait_ge(sem["y_split"], tally.take("y_split"))
                        for k in range(count):
                            kk = k + (2 if j == 3 else 0)
                            w = slice(kk * P, (kk + 1) * P)
                            last = three(ps[:, 2 + j % 2, 0:p.BW], w_hi[:, r, w], w_lo[:, r, w],
                                         yT[1][0][:, tile + k, 0:p.BW], yT[1][1][:, tile + k, 0:p.BW],
                                         k == 0, k == count - 1)
                        last.then_inc(sem["w_used"], tally.up("w_used"))
                body(0, True)
                tally.loop(KT - 1, body, gate=4, w_split=12, w_used=12, opart_free=4)
                for half in range(2):
                    if half == 1:
                        tally.skip("y_out", 2 * p.TB)
                        eng.wait_ge(sem["gate"], tally.now("gate", 2))
                        eng.wait_ge(sem["opart_free"], tally.now("opart_free", 2))
                    for k in range(KT):
                        if half == 0:
                            eng.wait_ge(sem["tot_done"], tally.take("tot_done"))
                        r = slot()
                        for t in range(p.TB):
                            w = slice(t * P, (t + 1) * P)
                            last = three(ps[:, 4 - 4 * half + t, :], tot[0][:, k, w], tot[1][:, k, w],
                                         w_hi[:, r, :], w_lo[:, r, :], k == 0, k == KT - 1)
                        last.then_inc(sem["w_used"], tally.up("w_used"))

            stage_end(eng, tally, "pe")
            for p in passes:
                if p.ctx:
                    modulation(p.layer)
                norm(p)
                pe_goes_on(eng, tally)
                eng.wait_ge(sem["hT_pre"], tally.now("hT_pre", 4))
                if not p.full:
                    project(p, 2, True)
                    turn_values(p, A_V, None)
                    project(p, 4)
                    turn_values(p, R_V, A_V)
                    turn_values(p, R_V + 1, R_V)
                    stage_end(eng, tally, "pe")
                    states(p)
                    stage_end(eng, tally, "pe")
                    continue
                project(p, 6, True)
                turn_values(p, A_V, None)
                project(p, 4)
                stage_end(eng, tally, "pe")
                attention(p)
                pe_goes_on(eng, tally)
                eng.wait_ge(sem["prob"], tally.now("prob", 2))
                project(p, 8)
                pe_goes_on(eng, tally)
                project(p, 6)
                turn_values(p, R_V, A_V)
                turn_values(p, R_V + 1, R_V)
                project(p, 2)
                stage_end(eng, tally, "pe")
                states(p)
                retention(p)
                pe_goes_on(eng, tally)
                eng.wait_ge(sem["ret_done"], tally.take("ret_done", 2 * p.NB))
                fourier(p)
                project(p, 2)
                pe_goes_on(eng, tally)
                eng.wait_ge(sem["proj_out"], tally.now("proj_out", 2))
                for b in range(p.NB):
                    merge(p, b)
                if p.ctx:
                    pe_goes_on(eng, tally)
                    eng.wait_ge(sem["y_out"], tally.now("y_out"))
                elif p.layer + 1 == DEPTH:
                    stage_end(eng, tally, "pe")
                else:
                    pe_goes_on(eng, tally)

        @block.scalar
        def _(eng):
            tally = Count(eng)
            eng.sem_inc(sem["proj_out"], tally.up("proj_out", 2))
            eng.sem_inc(sem["prob"], tally.up("prob", 2))
            eng.sem_inc(sem["inc_saved"], tally.up("inc_saved", 2))
            eng.sem_inc(sem["ret_y_saved"], tally.up("ret_y_saved", 2))
            eng.sem_inc(sem["gate"], tally.up("gate", 2))
            tally.skip("hT_pre", 4)
            tally.skip("ret_y", 2)
            tally.skip("w_used__done", RING)
            split = [0]

            def act(dst, src, func=ACT.Copy, **kw):
                return eng.activation(dst, src, func, **kw)

            def split_high(count):
                for _ in range(count):
                    if split[0] >= total_units:
                        return
                    r = split[0] % RING
                    split[0] += 1
                    eng.wait_ge(landed[r], tally.take(f"w_landed{r}", 16))
                    eng.wait_ge(sem["w_used"], tally.take("w_used"))
                    act(w_hi[:, r, :], raw[:, r, :]).then_inc(sem["w_high"], tally.up("w_high"))

            def constants():
                eng.dma_start(cT[:, :, :], a["c_cols"]).then_inc(sem["c_in"], tally.up("c_in", 16))
                eng.dma_start(ident[:, :], a["ident"]).then_inc(sem["const_in"], tally.up("const_in", 16))
                eng.dma_start(m_mask[:, :, :], a["mask"]).then_inc(sem["const_in"], tally.up("const_in", 16))
                eng.dma_start(small[:, :], a["small"]).then_inc(sem["const_in"], tally.up("const_in", 16))
                eng.wait_ge(sem["c_in"], tally.now("c_in"))
                act(sT[:, :, :], cT[:, :, :], ACT.Silu).then_inc(sem["silu_c"], tally.up("silu_c"))
                split_high(LOOK)

            def modulation(p):
                l = p.layer
                eng.dma_start(gpre[:, :], a["norm_pre_cols"][l]).then_inc(sem["small_in"], tally.up("small_in", 16))
                eng.dma_start(convw[:, :, :], a["conv_cols"][l]).then_inc(sem["small_in"], tally.up("small_in", 16))
                eng.dma_start(m_bias[0:2, :], a["b_ada"][l:l + 1, :].partition_broadcast(2).rearrange("p a n -> p (a n)")).then_inc(sem["small_in"], tally.up("small_in", 16))
                eng.dma_start(m_gpost[0:2, :], a["norm_post"][l:l + 1, :].partition_broadcast(2).rearrange("p a n -> p (a n)")).then_inc(sem["small_in"], tally.up("small_in", 16))
                eng.dma_start(sink[:, 0, :], a["attn_sink"][l:l + 1, :].partition_broadcast(P).rearrange("p a n -> p (a n)")).then_inc(sem["small_in"], tally.up("small_in", 16))
                eng.dma_start(decay[:, :], a["ret_decay"][l:l + 1].rearrange("a d h -> a (d h)").partition_broadcast(P)
                     .rearrange("p a n -> p (a n)")).then_inc(sem["small_in"], tally.up("small_in", 16))
                eng.wait_ge(sem["small_in"], tally.now("small_in"))
                eng.wait_ge(sem["log_one"], tally.take("log_one"))
                act(lt[:, 1, :], lt[:, 0, :], ACT.Exp, scale=-1.0).then_inc(sem["log_exp"], tally.up("log_exp"))
                eng.wait_ge(sem["log_one"], tally.take("log_one"))
                act(lt[:, 3, :], lt[:, 2, :], ACT.Ln).then_inc(sem["log_ln"], tally.up("log_ln"))
                eng.wait_ge(sem["log_gamma"], tally.take("log_gamma"))
                for d in range(2):
                    act(zeta[:, d, :], lg[:, d * RH:(d + 1) * RH], ACT.Exp, scale=small[:, d:d + 1]).then_inc(sem["act_own"], tally.up("act_own"))
                act(gch[:, :], lgd[:, :], ACT.Exp, scale=float(P)).then_inc(sem["zeta_exp"], tally.up("zeta_exp"))
                tokens(p, 0)
                squares(p, 0)
                eng.wait_ge(sem["gate_made"], tally.take("gate_made"))
                eng.dma_start(gate_rows[l], m_gate[0:2, :]).then_inc(sem["gate_out"], tally.up("gate_out", 16))
                eng.wait_ge(sem["gate_out"], tally.now("gate_out"))

            def tokens(p, b):
                src = (a["ctx"][0] if p.ctx else a["x"][0]) if p.layer == 0 else (c_mid if p.ctx else x_mid)
                for t in range(b * p.TB, (b + 1) * p.TB):
                    eng.dma_start(token_tile(p, t), src[t * P:(t + 1) * P, :]).then_inc(x_in[t], tally.up(f"x_in{t}", 16))

            def square(p, t):
                eng.wait_ge(x_in[t], tally.now(f"x_in{t}"))
                if tally.now("square"):
                    eng.wait_ge(sem["square"], tally.now("square"))
                act(n_sq[:, :, 256:512], token_tile(p, t).rearrange("p (a n) -> p a n", a=4), ACT.Square,
                    accum_out=n_stat[:, 0, t:t + 1]).then_inc(sem["square"], tally.up("square"))

            def root(p, b):
                at_ = slice(b * p.TB, (b + 1) * p.TB)
                eng.wait_ge(sem["mean"], tally.take("mean"))
                act(n_stat[:, 2, at_], n_stat[:, 1, at_], ACT.Sqrt).then_inc(sem["root"], tally.up("root"))

            def squares(p, b):
                for t in range(b * p.TB, (b + 1) * p.TB):
                    square(p, t)
                root(p, b)

            def norm(p):
                for b in range(p.NB):
                    for k in range(KT):
                        eng.wait_ge(sem["hT_pre"], tally.take("hT_pre"))
                        act(hT[0][:, k, b * p.BW:(b + 1) * p.BW], n_tmp[:, k % 4, 0:p.BW]).then_inc(sem["hT_high"], tally.up("hT_high"))
                        if b + 1 < p.NB and k % 2:
                            square(p, p.TB + k // 2)
                    if b + 1 < p.NB:
                        root(p, 1)

            def evacuate(p, t, dst, func=ACT.Copy):
                split_high(2)
                if dst is None:
                    eng.wait_ge(sem["raw_free"], tally.take("raw_free"))
                    dst = buf[raw_no[p.n, t] % 2][:, 0:p.T]
                if len(dst.shape) == 2:
                    dst = dst.rearrange("p (b n) -> p b n", b=p.NB)
                eng.wait_ge(sem["w_used"], tally.take("w_used__done", 2))
                act(dst, banks(2 * (tile_no[p.n, t] % 2), p), func).then_inc(sem["proj_out"], tally.up("proj_out"))

            def values_high(p):
                eng.wait_ge(sem["v_turned"], turned_no[p.n, A_V] + 1)
                for b in range(p.NB):
                    eng.activation(vx[:, 4 * b:4 * b + 4, :, 0, :], ps[:, 4 + b, :].rearrange(
                        "p (t k d) -> p t k d", k=2, d=HD), ACT.Copy).then_inc(sem["v_high"], tally.up("v_high"))

            def tile_range(p, first, last):
                for t in range(first, last):
                    for z0, zt, count in ((A_Z, Z_A, 4), (B_Z, Z_B, 2), (R_Z, Z_R, 2), (F_Z, Z_F, 2)):
                        if z0 <= t < z0 + count:
                            evacuate(p, t, z_tile(p, zt + t - z0)[:, :, 0, :], ACT.Silu)
                            break
                    else:
                        dst = None
                        if B_U <= t < B_C:
                            dst = (c_u if t < B_B else c_b)[:, t % 2, 0:p.T]
                        elif F_U <= t:
                            dst = f_u[:, t - F_U, 0:p.T]
                        evacuate(p, t, dst)

            def attention(p):
                steps = [(qb, h) for qb in range(p.NT) for h in range(HEADS)]

                def width(qb):
                    return 0 if p.ctx else (3 - (qb == 0) - (qb == p.NT - 1)) * P

                def queries(m):
                    qb, kv = m // 2, m % 2
                    for hh in range(2):
                        rows, t = slice(hh * HD, hh * HD + HD), slice(2 * kv, 2 * kv + 2)
                        last = eng.activation(qs[rows, qb % 2, t, hh, :], qT[rows, t, qb * P:(qb + 1) * P], ACT.Copy)
                        if hh == 0:
                            last.then_inc(sem["act_own"], tally.up("act_own"))
                    last.then_inc(sem["q_high"], tally.up("q_high"))

                def exps(n):
                    qb, h = steps[n]
                    L, c, k = width(qb), 2 * (n % 2), n % 4
                    eng.wait_ge(sem["max"], tally.take("max"))
                    s_view = ps[:, c:c + 2, :].rearrange("p a n -> p (a n)")[:, 512 - L:512 + CTX]
                    eng.activation(prob[:, n % 4, 0:L + CTX], s_view, ACT.Exp, bias=soft[:, k, 1:2], scale=SCALE,
                                   accum_out=soft[:, k, 2:3]).then_inc(sem["act_own"], tally.up("act_own"))
                    eng.activation(soft[:, k, 3:4], soft[:, k, 1:2], ACT.Exp, bias=sink[:, 0, h:h + 1],
                                   scale=1.0).then_inc(sem["prob"], tally.up("prob"))

                def save(n):
                    qb, h = steps[n]
                    count = (width(qb) + CTX) // P
                    eng.wait_ge(sem["probT"], tally.take("probT"))
                    src = turned_view(n, count)
                    eng.activation(pT_hi[:, 0:count, h % 4, :], src, ACT.Copy).then_inc(
                        sem["probT_high"], tally.up("probT_high"))

                def low_half():
                    eng.wait_ge(sem["pv"], tally.take("pv"))
                    if tally.now("out_sum"):
                        eng.wait_ge(sem["out_sum"], tally.now("out_sum"))
                    tally.skip("out_sum", 1)
                    eng.activation(o_low[:, :, :].rearrange("p h n -> p (h n)"), ps[HD:P, 7, :],
                                   ACT.Copy).then_inc(sem["out_low"], tally.up("out_low"))

                eng.activation(kc[:, :, 0, :], kd_c[:, :, :], ACT.Copy).then_inc(sem["act_own"], tally.up("act_own"))
                eng.activation(vc[:, :, :, 0, :], v_c[:, :, :].rearrange("p t (k d) -> p t k d", k=2),
                               ACT.Copy).then_inc(sem["a_split_high"], tally.up("a_split_high"))
                queries(0)
                queries(1)
                groups = len(steps) // 4
                exps(0)
                for n in range(len(steps)):
                    if n + 1 < len(steps):
                        exps(n + 1)
                    if n:
                        save(n - 1)
                    if n > 4 and n % 4 == 1:
                        low_half()
                    if n % 4 == 2 and n // 4 + 2 < groups:
                        queries(n // 4 + 2)
                save(len(steps) - 1)
                low_half()

            def decay_tables():
                eng.wait_ge(sem["ret_in"], tally.now("ret_in"))
                for h in range(RH):
                    act(xi[:, h, :], r_tab[:, 4, :], ACT.Exp, scale=lgd[:, h:h + 1]).then_inc(sem["act_own"], tally.up("act_own"))
                for h in range(RH):
                    act(r_e[:, h, 0, :], r_tab[:, 0, :], ACT.Exp, scale=lg[:, h:h + 1]).then_inc(sem["act_own"], tally.up("act_own"))
                    act(r_e[:, h, 1, :], r_tab[:, 2, :], ACT.Exp, scale=lg[:, RH + h:RH + h + 1]).then_inc(sem["ret_exp"], tally.up("ret_exp"))

            def states(p):
                for i, n in enumerate(outside_in(p)):
                    eng.wait_ge(sem["inc"], tally.take("inc"))
                    act(r_inc[:, n, :, :], ps[:, 6 + i % 2, 0:RH * HD].rearrange("p (h d) -> p h d", h=RH)).then_inc(sem["inc_saved"], tally.up("inc_saved"))

            def retention(p):
                order = outside_in(p)[::-1]

                eng.dma_start(f_bd[:, :], a["dft_head"][p.s].rearrange("p c n -> p (c n)")).then_inc(sem["head_in"], tally.up("head_in", 16))

                def squares(i):
                    eng.wait_ge(sem["ret_mean"], tally.take("ret_mean"))
                    for h in range(RH):
                        if tally.now("ret_square"):
                            eng.wait_ge(sem["ret_square"], tally.now("ret_square"))
                        act(r_sq[:, :], r_y[:, order[i], h, :], ACT.Square,
                            accum_out=r_stat[:, 3, order[i] * RH + h:order[i] * RH + h + 1]).then_inc(
                                sem["ret_square"], tally.up("ret_square"))
                for i, n in enumerate(order):
                    eng.wait_ge(sem["ret_y"], tally.take("ret_y"))
                    for h in range(RH):
                        ins = act(r_y[:, n, h, :], ps[:, 2 + i % 2, h * HD:(h + 1) * HD],
                                  accum_out=r_stat[:, 0, n * RH + h:n * RH + h + 1])
                        ins.then_inc(sem["ret_y_saved"], tally.up("ret_y_saved")) if h == RH - 1 else ins.then_inc(
                            sem["act_own"], tally.up("act_own"))
                    if i > 1:
                        squares(i - 2)
                for i in range(p.NT - 2, p.NT):
                    squares(i)
                eng.wait_ge(sem["ret_var"], tally.take("ret_var"))
                act(r_stat[:, 2, 0:p.NT * RH], r_stat[:, 1, 0:p.NT * RH], ACT.Sqrt).then_inc(sem["ret_root"], tally.up("ret_root"))
                tile_range(p, F_U, F_Z)

            def fourier(p):
                for n in range(p.NT):
                    eng.wait_ge(sem["four"], tally.take("four"))
                    act(f_ab[0][:, n, :, :, :].rearrange("p j c n -> p (j c n)"), ps[:, 4 + n % 2, :]).then_inc(sem["four_hi"], tally.up("four_hi"))
                split_high(2 if p.ctx else 16)
                tally.skip("w_used__done", 2 if p.ctx else 16)

            def gated_high(p, b):
                for tile, count in BRANCH:
                    src = z_pass[p.s][:, b, tile:tile + count, :]
                    act(yT[1][0][:, tile:tile + count, 0:p.BW], src).then_inc(sem["y_hi"], tally.up("y_hi"))

            def sources(p, b):
                src = (a["ctx"][0] if p.ctx else a["x"][0]) if p.layer == 0 else (c_mid if p.ctx else x_mid)
                dst = (out[0] if p.layer == DEPTH - 1 else x_mid) if not p.ctx else c_mid
                rows = slice(b * p.BW, (b + 1) * p.BW)
                return [m[rows, :].rearrange("(t p) n -> p t n", p=P) for m in (src, dst)]

            def send(p, b):
                dst = sources(p, b)[1]
                for t in range(p.TB):
                    eng.wait_ge(sem["x_new"], tally.take("x_new"))
                    eng.dma_start(dst[:, t, :].rearrange("p (h n) -> p h n", h=2), results(p, b)[1][:, 2 * t:2 * t + 2, :]).then_inc(sem["x_out"], tally.up("x_out", 16))

            def merge(p, b):
                tmp = tmp_blk[b]
                eng.wait_ge(sem["y_split"], tally.take("y_split__all", len(BRANCH)))
                eng.dma_start(gp_blk[b][:, :], gate_rows[p.layer, p.s:p.s + 1, :].partition_broadcast(P)
                              .rearrange("p a n -> p (a n)")).then_inc(sem["row_in"], tally.up("row_in", 16))
                if p.ctx:
                    tokens(passes[p.n + 1], 0)

                def body(i, first=False):
                    for j in range(4):
                        split_high(3)
                        if first and b and j == 2:
                            send(p, b - 1)
                        eng.wait_ge(sem["w_used"], tally.take("w_used__done", 2))
                        eng.wait_ge(sem["opart_free"], tally.take("opart_free"))
                        act(tmp[:, j % 2, 0:p.BW], ps[:, j % 2, 0:p.BW], ACT.Sigmoid).then_inc(sem["gate"], tally.up("gate"))
                        tally.skip("w_used__done", 1)
                body(0, True)
                tally.loop(KT - 1, body, w_high=12, w_used=12, w_used__done=12, opart_free=4, gate=4,
                       **{f"w_landed{r}": 48 for r in range(RING)})
                split[0] += 12 * (KT - 2)
                def out_squares(half):
                    eng.wait_ge(sem["w_used"], tally.take("w_used__done", 8))
                    for t in range(p.TB):
                        if tally.now("y_out"):
                            eng.wait_ge(sem["y_out"], tally.now("y_out"))
                        eng.wait_ge(sem["y_gate"], tally.take("y_gate"))
                        act(sq_junk[:, :], ps[:, 4 - 4 * half + t, :], ACT.Square,
                                 accum_out=stat[:, 0, 4 * half + t:4 * half + t + 1]).then_inc(sem["y_out"], tally.up("y_out"))
                split_high(8)
                eng.wait_ge(sem["tot_done"], tally.take("tot_done", KT))
                for t in range(p.TB):
                    eng.dma_start(results(p, b)[1][:, 2 * t:2 * t + 2, :], sources(p, b)[0][:, t, :]
                                  .rearrange("p (h n) -> p h n", h=2)).then_inc(sem["post_in"], tally.up("post_in", 16))
                split_high(1)
                if b + 1 < p.NB:
                    gated_high(p, b + 1)
                split_high(3)
                out_squares(0)
                split_high(4)
                out_squares(1)
                eng.wait_ge(sem["out_mean"], tally.take("out_mean"))
                act(stat[:, 2, 0:p.TB], stat[:, 1, 0:p.TB], ACT.Sqrt).then_inc(sem["out_root"], tally.up("out_root"))

            constants()
            stage_end(eng, tally, "act")
            for p in passes:
                if p.ctx:
                    modulation(p)
                else:
                    tokens(p, 1)
                norm(p)
                stage_end(eng, tally, "act")
                if not p.full:
                    after = passes[p.n + 1]
                    tokens(after, 0)
                    for n, t in enumerate(p.tiles):
                        tile_range(p, t, t + 1)
                        if n < after.TB:
                            square(after, n)
                    root(after, 0)
                    stage_end(eng, tally, "act")
                    states(p)
                    stage_end(eng, tally, "act")
                    continue
                if not p.ctx:
                    eng.dma_start(rope[:, :, :], a["rope"]).then_inc(sem["rope_in"], tally.up("rope_in", 16))
                tile_range(p, A_Q, A_Z)
                if not p.ctx:
                    values_high(p)
                tile_range(p, A_Z, B_U)
                stage_end(eng, tally, "act")
                attention(p)
                stage_end(eng, tally, "act")
                eng.dma_start(r_tab[:, :, :], a["ret"]).then_inc(sem["ret_in"], tally.up("ret_in", 16))
                tile_range(p, B_U, B_B)
                decay_tables()
                tile_range(p, B_B, R_Q)
                stage_end(eng, tally, "act")
                if not p.ctx:
                    eng.dma_start(rope[:, :, :], a["rope"]).then_inc(sem["rope_in"], tally.up("rope_in", 16))
                tile_range(p, R_Q, F_U)
                stage_end(eng, tally, "act")
                states(p)
                retention(p)
                stage_end(eng, tally, "act")
                fourier(p)
                tile_range(p, F_Z, MERGE)
                stage_end(eng, tally, "act")
                gated_high(p, 0)
                for b in range(p.NB):
                    merge(p, b)
                if p.ctx:
                    squares(passes[p.n + 1], 0)
                send(p, p.NB - 1)
                eng.wait_ge(sem["x_out"], tally.now("x_out"))
                stage_end(eng, tally, "act")

        @block.vector
        def _(eng):
            tally = Count(eng)
            eng.sem_inc(sem["hT_pre"], tally.up("hT_pre", 4))
            eng.sem_inc(sem["raw_free"], tally.up("raw_free", 2))
            eng.sem_inc(sem["probT_saved"], tally.up("probT_saved", 2))
            eng.sem_inc(sem["four_done"], tally.up("four_done", 2))
            eng.sem_inc(sem["opart_free"], tally.up("opart_free", 2))
            tally.skip("w_used__done", RING)
            tally.skip("prob", 2)
            tally.skip("gate", 2)
            tally.skip("inc_saved", 2)
            tally.skip("ret_y_saved", 2)

            def tt(dst, x, y, op=ALU.mult):
                return eng.tensor_tensor(dst, x, y, op)

            def constants():
                eng.memset(ones[:, :], 1.0).then_inc(sem["dve_own"], tally.up("dve_own"))
                eng.wait_ge(sem["const_in"], tally.take("const_in", 48))
                eng.tensor_copy(ident_bf[:, :], ident[:, :]).then_inc(sem["dve_own"], tally.up("dve_own"))
                eng.tensor_copy(mask_bf[:, :, :], m_mask[:, :, :]).then_inc(sem["dve_own"], tally.up("dve_own"))
                eng.wait_ge(sem["dve_own"], tally.now("dve_own"))

            def modulation(p):
                eng.wait_ge(sem["small_in"], tally.take("small_in", 16 * 6))
                eng.tensor_scalar(sink[:, 1, :], sink[:, 0, :], -1.0, None, ALU.mult).then_inc(sem["dve_own"], tally.up("dve_own"))
                eng.wait_ge(sem["dve_own"], tally.now("dve_own"))
                eng.tensor_scalar(lt[:, 1, :], decay[:, :], -1.0, None, ALU.mult).then_inc(sem["dve_own"], tally.up("dve_own"))
                eng.wait_ge(sem["dve_own"], tally.now("dve_own"))
                tt(lt[:, 0, :], decay[:, :], lt[:, 1, :], ALU.max).then_inc(sem["log_one"], tally.up("log_one"))
                eng.wait_ge(sem["log_exp"], tally.take("log_exp"))
                eng.tensor_scalar(lt[:, 2, :], lt[:, 1, :], 1.0, None, ALU.add).then_inc(sem["log_one"], tally.up("log_one"))
                eng.wait_ge(sem["log_one"], tally.now("log_one"))
                eng.tensor_scalar(lt[:, 4, :], lt[:, 2, :], -1.0, None, ALU.add).then_inc(sem["dve_own"], tally.up("dve_own"))
                eng.wait_ge(sem["dve_own"], tally.now("dve_own"))
                tt(lt[:, 4, :], lt[:, 1, :], lt[:, 4, :], ALU.subtract).then_inc(sem["dve_own"], tally.up("dve_own"))
                eng.wait_ge(sem["dve_own"], tally.now("dve_own"))
                eng.reciprocal(lt[:, 5, :], lt[:, 2, :]).then_inc(sem["dve_own"], tally.up("dve_own"))
                eng.wait_ge(sem["dve_own"], tally.now("dve_own"))
                tt(lt[:, 4, :], lt[:, 4, :], lt[:, 5, :]).then_inc(sem["dve_own"], tally.up("dve_own"))
                eng.wait_ge(sem["dve_own"], tally.now("dve_own"))
                eng.wait_ge(sem["log_ln"], tally.take("log_ln"))
                tt(lt[:, 4, :], lt[:, 4, :], lt[:, 3, :], ALU.add).then_inc(sem["dve_own"], tally.up("dve_own"))
                eng.wait_ge(sem["dve_own"], tally.now("dve_own"))
                eng.tensor_scalar(lt[:, 5, :], decay[:, :], 0.0, None, ALU.min).then_inc(sem["dve_own"], tally.up("dve_own"))
                eng.wait_ge(sem["dve_own"], tally.now("dve_own"))
                tt(lg[:, :], lt[:, 5, :], lt[:, 4, :], ALU.subtract).then_inc(sem["dve_own"], tally.up("dve_own"))
                eng.wait_ge(sem["dve_own"], tally.now("dve_own"))
                eng.tensor_copy(lgd[0:HD, :], lg[0:HD, 0:RH]).then_inc(sem["dve_own"], tally.up("dve_own"))
                eng.wait_ge(sem["dve_own"], tally.now("dve_own"))
                eng.tensor_copy(lgd[HD:P, :], lg[HD:P, RH:2 * RH]).then_inc(sem["log_gamma"], tally.up("log_gamma"))
                eng.wait_ge(sem["zeta_exp"], tally.take("zeta_exp"))
                eng.tensor_scalar(zeta[:, :, :], zeta[:, :, :], SCALE, None, ALU.mult).then_inc(sem["dve_own"], tally.up("dve_own"))
                scaled(p, 0)
                for n in range(6):
                    eng.wait_ge(sem["mod_rows"], tally.take("mod_rows"))
                    c = slice(n * 512, (n + 1) * 512)
                    tt(m_rows[0:2, c], ps[0:2, n, :], m_bias[0:2, c], ALU.add).then_inc(sem["mod_saved"], tally.up("mod_saved"))
                eng.wait_ge(sem["mod_saved"], tally.now("mod_saved"))
                tt(m_gate[0:2, :], m_rows[0:2, 2 * D:3 * D], m_gpost[0:2, :]).then_inc(sem["gate_made"], tally.up("gate_made"))
                eng.wait_ge(sem["mod_cols"], tally.take("mod_cols"))
                cols = ps[:, 6, 0:4 * KT].rearrange("p (k s) -> p k s", s=2)
                for s in range(2):
                    eng.tensor_copy(mod[:, s, 1, :], cols[:, 0:KT, s]).then_inc(sem["dve_own"], tally.up("dve_own"))
                    eng.scalar_tensor_tensor(mod[:, s, 0, :], cols[:, KT:2 * KT, s], 1.0, gpre[:, :],
                                                  ALU.add, ALU.mult).then_inc(sem["dve_own"], tally.up("dve_own"))
                eng.wait_ge(sem["dve_own"], tally.now("dve_own"))

            def scaled(p, b):
                at_ = slice(b * p.TB, (b + 1) * p.TB)
                eng.wait_ge(sem["square"], tally.take("square", p.TB))
                eng.tensor_scalar(n_stat[:, 1, at_], n_stat[:, 0, at_], 1.0 / D, EPS, ALU.mult, ALU.add).then_inc(sem["mean"], tally.up("mean"))
                eng.wait_ge(sem["root"], tally.take("root"))
                eng.reciprocal(n_stat[:, 0, at_], n_stat[:, 2, at_]).then_inc(sem["dve_own"], tally.up("dve_own"))
                eng.wait_ge(sem["dve_own"], tally.now("dve_own"))
                for t in range(b * p.TB, (b + 1) * p.TB):
                    eng.tensor_scalar(token_tile(p, t), token_tile(p, t), n_stat[:, 0, t:t + 1], None, ALU.mult).then_inc(sem["normed"], tally.up("normed"))

            def norm(p):
                for b in range(p.NB):
                    c = slice(b * p.BW, (b + 1) * p.BW)

                    def low(k):
                        eng.wait_ge(sem["hT_high"], tally.take("hT_high", 2))
                        tt(hT[1][:, k, c], n_tmp[:, k % 4, 0:p.BW], hT[0][:, k, c].bitcast(F32), ALU.subtract).then_inc(sem["hT_low_odd"], tally.up("hT_low_odd"))
                    for k in range(KT):
                        eng.wait_ge(sem["turned"], tally.take("turned"))
                        if tally.now("hT_low_odd"):
                            eng.wait_ge(sem["hT_low_odd"], tally.now("hT_low_odd"))
                        if k % 2 == 0 and (b or k > 3):
                            eng.wait_ge(sem["hT_low"], tally.take("hT_low"))
                        eng.tensor_scalar(n_tmp[:, k % 4, 0:p.BW], ps[:, k % 4, 0:p.BW], mod[:, p.s, 0, k:k + 1],
                                               mod[:, p.s, 1, k:k + 1], ALU.mult, ALU.add).then_inc(sem["hT_pre"], tally.up("hT_pre"))
                        if k and k % 2 == 0:
                            low(k - 1)
                    low(KT - 1)
                    if b + 1 < p.NB:
                        scaled(p, 1)
                tally.skip("hT_low", 2)

            def placed(p, t):
                eng.wait_ge(sem["proj_out"], 2 + tile_no[p.n, t] + 1)

            def to(p, t, outs, last=True):
                src = buf[raw_no[p.n, t] % 2]
                placed(p, t)
                if not p.ctx:
                    eng.wait_ge(sem["raw_free"], tally.now("raw_free"))
                    eng.stream_shuffle(turned[:, 0:p.T], src[:, 0:p.T], [(i + 16) % 32 for i in range(32)]).then_inc(sem["dve_own"], tally.up("dve_own"))
                    eng.wait_ge(sem["dve_own"], tally.now("dve_own"))
                    tt(src[:, 0:p.T], src[:, 0:p.T], rope[:, 0, :]).then_inc(sem["dve_own"], tally.up("dve_own"))
                    tt(turned[:, 0:p.T], turned[:, 0:p.T], rope[:, 1, :]).then_inc(sem["dve_own"], tally.up("dve_own"))
                    eng.wait_ge(sem["dve_own"], tally.now("dve_own"))
                for n, (dst, row, rows) in enumerate(outs):
                    x = src[row:row + rows, 0:p.T]
                    ins = eng.tensor_copy(dst, x) if p.ctx else tt(dst, x, turned[row:row + rows, 0:p.T], ALU.add)
                    ins.then_inc(sem["raw_free"], tally.up("raw_free")) if last and n == len(outs) - 1 else ins.then_inc(sem["dve_own"], tally.up("dve_own"))

            def save_values(p, t, dst):
                eng.wait_ge(sem["v_turned"], turned_no[p.n, t] + 1)
                if p.NT == 8:
                    eng.tensor_copy(dst[:, 0:4, :], ps[:, 4, :].rearrange("p (n d) -> p n d", d=P)).then_inc(sem["dve_own"], tally.up("dve_own"))
                n0 = p.NT - p.NT // p.NB
                eng.tensor_copy(dst[:, n0:p.NT, :], ps[:, 3 + p.NB, 0:(p.NT - n0) * P]
                                     .rearrange("p (n d) -> p n d", d=P)).then_inc(sem["raw_free"], tally.up("raw_free"))

            def halves(first, second):
                return [(place[r:r + HD], row, HD) for place, row in ((first, 0), (second, HD)) for r in (0, HD)]

            def a_keys(p):
                if p.ctx:
                    to(p, A_K, halves(kd_c[:, 0, :], kd_c[:, 1, :]))
                    save_values(p, A_V, v_c)
                    return
                key = buf[raw_no[p.n, A_K] % 2]
                to(p, A_K, [(key[:, :], 0, P)], False)
                eng.wait_ge(sem["dve_own"], tally.now("dve_own"))
                for which in range(2):
                    outs = halves(kx[:, 0, which, :], kx[:, 1, which, :])
                    for n, (dst, row, rows) in enumerate(outs):
                        src = key[row:row + rows, :]
                        if which == 0:
                            ins = eng.tensor_copy(dst, src)
                        else:
                            high = kx[row:row + rows, row // HD, 0, :]
                            ins = tt(dst, src, high.bitcast(F32), ALU.subtract)
                        name = "raw_free" if which and n == len(outs) - 1 else "dve_own"
                        ins.then_inc(sem[name], tally.up(name))
                    eng.wait_ge(sem["dve_own"], tally.now("dve_own"))
                for b in range(p.NB):
                    eng.wait_ge(sem["v_high"], tally.take("v_high"))
                    at_ = slice(4 * b, 4 * b + 4)
                    name = "raw_free" if b == p.NB - 1 else "dve_own"
                    tt(vx[:, at_, :, 1, :], ps[:, 4 + b, :].rearrange("p (t k d) -> p t k d", k=2, d=HD),
                       vx[:, at_, :, 0, :].bitcast(F32), ALU.subtract).then_inc(sem[name], tally.up(name))

            def r_keys(p):
                for j in range(2):
                    to(p, R_K + j, [(rk[:, j, 0:p.T], 0, P)])
                for j in range(2):
                    save_values(p, R_V + j, rv[:, 0:p.NT, j, :])

            def attention(p):
                steps = [(qb, h) for qb in range(p.NT) for h in range(HEADS)]

                def width(qb):
                    return 0 if p.ctx else (3 - (qb == 0) - (qb == p.NT - 1)) * P

                def queries(m):
                    qb, kv = m // 2, m % 2
                    eng.wait_ge(sem["q_high"], tally.take("q_high"))
                    for hh in range(2):
                        rows, t = slice(hh * HD, hh * HD + HD), slice(2 * kv, 2 * kv + 2)
                        other = slice(HD - hh * HD, P - hh * HD)
                        ins = tt(qs[other, qb % 2, t, hh, :], qT[rows, t, qb * P:(qb + 1) * P],
                                 qs[rows, qb % 2, t, hh, :].bitcast(F32), ALU.subtract)
                        ins.then_inc(sem["q_split"], tally.up("q_split")) if hh else ins.then_inc(
                            sem["dve_own"], tally.up("dve_own"))

                def maximum(n):
                    c = 2 * (n % 2)
                    eng.wait_ge(sem["score"], tally.take("score"))
                    view = ps[:, c:c + 2, :].rearrange("p a n -> p (a n)")[:, 512 - width(steps[n][0]):512 + CTX]
                    eng.tensor_reduce(soft[:, n % 4, 0:1], view, AX.X, ALU.max).then_inc(
                        sem["max_own"], tally.up("max_own"))

                def bias(n):
                    k, h = n % 4, steps[n][1]
                    eng.wait_ge(sem["max_own"], tally.now("max_own"))
                    eng.tensor_scalar(soft[:, k, 1:2], soft[:, k, 0:1], -SCALE, sink[:, 1, h:h + 1],
                                      ALU.mult, ALU.min).then_inc(sem["max"], tally.up("max"))

                def total(n):
                    k = n % 4
                    eng.wait_ge(sem["prob"], tally.take("prob"))
                    tt(soft[:, k, 4:5], soft[:, k, 2:3], soft[:, k, 3:4], ALU.add).then_inc(
                        sem["dve_own"], tally.up("dve_own"))

                def one_over(n):
                    k = n % 4
                    eng.wait_ge(sem["dve_own"], tally.now("dve_own"))
                    eng.reciprocal(soft[:, k, 5:6], soft[:, k, 4:5]).then_inc(sem["one_over"], tally.up("one_over"))

                def low(n):
                    qb, h = steps[n]
                    count = (width(qb) + CTX) // P
                    eng.wait_ge(sem["probT_high"], tally.take("probT_high"))
                    src = turned_view(n, count)
                    tt(pT_lo[:, 0:count, h % 4, :], src, pT_hi[:, 0:count, h % 4, :].bitcast(F32),
                       ALU.subtract).then_inc(sem["probT_saved"], tally.up("probT_saved"))

                def add_halves(g):
                    eng.wait_ge(sem["out_low"], tally.take("out_low"))
                    if tally.now("gated") + g > 1:
                        eng.wait_ge(sem["gated"], tally.now("gated", g - 1))
                    for half in range(2):
                        rows = slice(half * HD, half * HD + HD)
                        ins = tt(o_sum[rows, g % 2, :, :], ps[0:HD, 7, :].rearrange("p (h n) -> p h n", h=4)[:, half::2, :],
                                 o_low[:, half::2, :], ALU.add)
                        ins.then_inc(sem["out_sum"], tally.up("out_sum")) if half else ins.then_inc(
                            sem["dve_own"], tally.up("dve_own"))

                eng.wait_ge(sem["a_split_high"], tally.take("a_split_high"))
                tt(kc[:, :, 1, :], kd_c[:, :, :], kc[:, :, 0, :].bitcast(F32), ALU.subtract).then_inc(
                    sem["dve_own"], tally.up("dve_own"))
                tt(vc[:, :, :, 1, :], v_c[:, :, :].rearrange("p t (k d) -> p t k d", k=2),
                   vc[:, :, :, 0, :].bitcast(F32), ALU.subtract).then_inc(sem["a_split"], tally.up("a_split"))
                groups = len(steps) // 4
                queries(0)
                queries(1)
                maximum(0)
                bias(0)
                maximum(1)
                for n in range(len(steps)):
                    total(n)
                    if n + 1 < len(steps):
                        bias(n + 1)
                    one_over(n)
                    if n > 1:
                        low(n - 2)
                    if n + 2 < len(steps):
                        maximum(n + 2)
                    if n > 4 and n % 4 == 2:
                        add_halves(n // 4 - 1)
                    if n % 4 == 3 and n // 4 + 2 < groups:
                        queries(n // 4 + 2)
                low(len(steps) - 2)
                low(len(steps) - 1)
                add_halves(groups - 1)
                tally.skip("gated", groups)
                eng.wait_ge(sem["gated"], tally.now("gated"))

            def convolution(p):
                for j in range(2):
                    src = buf[raw_no[p.n, B_C + j] % 2]
                    placed(p, B_C + j)
                    eng.memset(c_cu[:, j, 1:2], 0.0).then_inc(sem["dve_own"], tally.up("dve_own"))
                    eng.memset(c_cu[:, j, 2 + p.T:3 + p.T], 0.0).then_inc(sem["dve_own"], tally.up("dve_own"))
                    tt(c_cu[:, j, 2:2 + p.T], src[:, 0:p.T], c_u[:, j, 0:p.T]).then_inc(sem["raw_free"], tally.up("raw_free"))
                    eng.wait_ge(sem["raw_free"], tally.now("raw_free"))
                    eng.wait_ge(sem["dve_own"], tally.now("dve_own"))
                    y, u = c_y[:, j, 0:p.T], c_cu[:, j, :]
                    eng.tensor_scalar(y, u[:, 1:1 + p.T], convw[:, j, 0:1], convw[:, j, 3:4], ALU.mult, ALU.add).then_inc(sem["dve_own"], tally.up("dve_own"))
                    eng.wait_ge(sem["dve_own"], tally.now("dve_own"))
                    eng.scalar_tensor_tensor(y, u[:, 2:2 + p.T], convw[:, j, 1:2], y, ALU.mult, ALU.add).then_inc(sem["dve_own"], tally.up("dve_own"))
                    eng.wait_ge(sem["dve_own"], tally.now("dve_own"))
                    eng.scalar_tensor_tensor(y, u[:, 3:3 + p.T], convw[:, j, 2:3], y, ALU.mult, ALU.add).then_inc(sem["dve_own"], tally.up("dve_own"))
                    eng.wait_ge(sem["dve_own"], tally.now("dve_own"))
                    tt(y, y, c_b[:, j, 0:p.T]).then_inc(sem["dve_own"], tally.up("dve_own"))
                    eng.wait_ge(sem["dve_own"], tally.now("dve_own"))
                for j in range(2):
                    placed(p, B_Z + j)
                    zz = z_tile(p, Z_B + j)[:, :, 0, :]
                    tt(zz, zz, c_y[:, j, 0:p.T].rearrange("p (b n) -> p b n", b=p.NB)).then_inc(sem["dve_own"], tally.up("dve_own"))

            def decay_tables():
                eng.wait_ge(sem["ret_exp"], tally.take("ret_exp", RH))
                for d in range(2):
                    side = r_tab[:, 1 + 2 * d, :].unsqueeze(1).to_broadcast([P, RH, P])
                    tt(r_e[:, :, d, :], r_e[:, :, d, :], side).then_inc(sem["dve_own"], tally.up("dve_own"))
                eng.wait_ge(sem["dve_own"], tally.now("dve_own"))
                tt(dt_[:, :, :], r_e[:, :, 0, :], r_e[:, :, 1, :], ALU.add).then_inc(sem["dve_own"], tally.up("dve_own"))

            def scan(p, d, s):
                rows = slice(d * HD, (d + 1) * HD)
                order = list(range(p.NT))[::-1] if d else list(range(p.NT))
                new = r_prev[rows, order[s + 1], :, :] if s + 1 < p.NT else state_c[rows, :, :]
                for h in range(RH):
                    eng.scalar_tensor_tensor(new[:, h, :], r_prev[rows, order[s], h, :], gch[rows, h:h + 1],
                                             r_inc[rows, order[s], h, :], ALU.mult, ALU.add).then_inc(
                                                 sem["dve_own"], tally.up("dve_own"))

            def states(p):
                for d in range(2):
                    rows = slice(d * HD, (d + 1) * HD)
                    dst = r_prev[rows, d * (p.NT - 1), :, :]
                    (eng.memset(dst, 0.0) if p.ctx else eng.tensor_copy(dst, state_c[rows, :, :])).then_inc(sem["dve_own"], tally.up("dve_own"))

                def taken(i):
                    eng.wait_ge(sem["inc_saved"], tally.take("inc_saved"))
                    eng.wait_ge(sem["dve_own"], tally.now("dve_own"))
                    scan(p, i % 2, i // 2)
                for i in range(p.NT):
                    eng.wait_ge(sem["k_turned"], tally.take("k_turned"))
                    k = ps[:, 4 + i % 2, 0:RH * HD].rearrange("p (h d) -> p h d", h=RH)
                    for d in range(2):
                        ins = tt(r_kz[:, i % 2, :, d, :], k, zeta[:, d, :].unsqueeze(2).to_broadcast([P, RH, HD]))
                        ins.then_inc(sem["kz"], tally.up("kz")) if d else ins.then_inc(sem["dve_own"], tally.up("dve_own"))
                    if i > 1:
                        taken(i - 2)
                for i in range(p.NT - 2, p.NT):
                    taken(i)

            def last_states(p, i):
                s = p.NT // 2 + i
                if s < (p.NT if p.ctx else p.NT - 1):
                    eng.wait_ge(sem["dve_own"], tally.now("dve_own"))
                    for d in range(2):
                        scan(p, d, s)

            def retention(p):
                order = outside_in(p)[::-1]

                def center(i):
                    n = order[i]
                    m = slice(n * RH, (n + 1) * RH)
                    eng.wait_ge(sem["ret_y_saved"], tally.take("ret_y_saved"))
                    eng.tensor_scalar(r_stat[:, 0, m], r_stat[:, 0, m], 1.0 / HD, None, ALU.mult).then_inc(sem["dve_own"], tally.up("dve_own"))
                    eng.wait_ge(sem["dve_own"], tally.now("dve_own"))
                    tt(r_y[:, n, :, :], r_y[:, n, :, :], r_stat[:, 0, m].unsqueeze(2).to_broadcast([P, RH, HD]),
                       ALU.subtract).then_inc(sem["ret_mean"], tally.up("ret_mean"))
                for i, n in enumerate(order):
                    eng.wait_ge(sem["sT"], tally.take("sT"))
                    if i > 1:
                        eng.wait_ge(sem["ret_y"], tally.take("ret_y"))
                    for h in range(2):
                        ins = tt(r_sc[:, i % 2, h::2, :],
                                 ps[:, i % 2 + 4 * h, 0:2 * P].rearrange("p (j n) -> p j n", j=2), dt_[:, h::2, :])
                        ins.then_inc(sem["sc"], tally.up("sc")) if h else ins.then_inc(sem["dve_own"], tally.up("dve_own"))
                    if i % 2 == 0:
                        last_states(p, i // 2)
                    if i > 1:
                        center(i - 2)
                for i in range(p.NT - 2, p.NT):
                    center(i)
                tally.skip("ret_y", 2)
                m = p.NT * RH
                eng.wait_ge(sem["ret_square"], tally.take("ret_square", m))
                eng.tensor_scalar(r_stat[:, 1, 0:m], r_stat[:, 3, 0:m], 1.0 / HD, EPS, ALU.mult, ALU.add).then_inc(sem["ret_var"], tally.up("ret_var"))
                eng.wait_ge(sem["ret_root"], tally.take("ret_root"))
                eng.reciprocal(r_stat[:, 0, 0:m], r_stat[:, 2, 0:m]).then_inc(sem["dve_own"], tally.up("dve_own"))
                eng.wait_ge(sem["dve_own"], tally.now("dve_own"))
                eng.wait_ge(sem["ret_mean"], tally.now("ret_mean"))
                for b in range(p.NB):
                    g, c = slice(b * p.TB * RH, (b + 1) * p.TB * RH), slice(b * p.TB, (b + 1) * p.TB)
                    y = r_y[:, c, :, :].rearrange("p c h d -> p (c h) d")
                    tt(y, y, r_stat[:, 0, g].unsqueeze(2).to_broadcast([P, p.TB * RH, HD])).then_inc(sem["ret_norm"], tally.up("ret_norm"))
                def fold(j):
                    if not p.ctx:
                        placed(p, F_U + j)
                        first, second = f_u[:, j, 0:512], f_u[:, j, 512:1024]
                        tt(f_fold[:, j, 0, :], first, second, ALU.add).then_inc(sem["dve_own"], tally.up("dve_own"))
                        tt(f_fold[:, j, 1, :], first, second, ALU.subtract).then_inc(sem["folded"], tally.up("folded"))
                fold(0)
                for b in range(p.NB):
                    for j in range(2):
                        eng.wait_ge(sem["ret_yT"], tally.take("ret_yT"))
                        zz = z_pass[p.s][:, b, Z_R + j, :]
                        tt(zz, ps[:, 4 + 2 * j + b, 0:p.BW], zz).then_inc(sem["ret_done"], tally.up("ret_done"))
                fold(1)

            def fourier(p):
                for n in range(p.NT):
                    eng.wait_ge(sem["four_hi"], tally.take("four_hi"))
                    tt(f_ab[1][:, n, :, :, :].rearrange("p j c n -> p (j c n)"), ps[:, 4 + n % 2, :],
                            f_ab[0][:, n, :, :, :].bitcast(F32).rearrange("p j c n -> p (j c n)"), ALU.subtract).then_inc(sem["four_done"], tally.up("four_done"))
                placed(p, F_Z + 1)
                eng.wait_ge(sem["w_used"], tally.now("w_used__done", units_of(p)[0]))
                for part in range(1 if p.ctx else 2):
                    for j in range(2):
                        places = z_tile(p, Z_F + j)[:, :, 0, :]
                        if not p.ctx:
                            places = places[:, :, part::2]
                        tt(places, ps[:, 4 + 2 * part + j, 0:p.BW].rearrange("p (b n) -> p b n", b=p.NB),
                           places).then_inc(sem["dve_own"], tally.up("dve_own"))

            def units_of(p):
                return 2 * F_Z + (2 if p.ctx else 16), 2 * MERGE + (2 if p.ctx else 16)

            def gated_low(p, b):
                for tile, count in BRANCH:
                    eng.wait_ge(sem["y_hi"], tally.take("y_hi"))
                    tt(yT[1][1][:, tile:tile + count, 0:p.BW], z_pass[p.s][:, b, tile:tile + count, :],
                            yT[1][0][:, tile:tile + count, 0:p.BW].bitcast(F32), ALU.subtract).then_inc(sem["y_split"], tally.up("y_split"))

            def merge(p, b):
                tmp = tmp_blk[b]
                eng.wait_ge(sem["y_split"], tally.now("y_split"))
                acc = tmp[:, 2, 0:p.BW]

                def body(i):
                    for j in range(4):
                        eng.wait_ge(sem["gate"], tally.take("gate"))
                        eng.wait_ge(sem["w_used"], tally.take("w_used__done", 3))
                        g, o = tmp[:, j % 2, 0:p.BW], ps[:, 2 + j % 2, 0:p.BW]
                        eng.wait_ge(sem["dve_own"], tally.now("dve_own"))
                        if j == 0:
                            tt(acc, g, o).then_inc(sem["opart_free"], tally.up("opart_free"))
                        else:
                            t = tmp[:, 3, 0:p.BW]
                            tt(t, g, o).then_inc(sem["opart_free"], tally.up("opart_free"))
                            eng.wait_ge(sem["opart_free"], tally.now("opart_free"))
                            tt(acc, acc, t, ALU.add).then_inc(sem["dve_own"], tally.up("dve_own"))
                    eng.wait_ge(sem["dve_own"], tally.now("dve_own"))
                    eng.tensor_copy(tot[0][:, bass.ds(i, 1), 0:p.BW], acc.unsqueeze(1)).then_inc(sem["dve_own"], tally.up("dve_own"))
                    eng.wait_ge(sem["dve_own"], tally.now("dve_own"))
                    tt(tot[1][:, bass.ds(i, 1), 0:p.BW], acc.unsqueeze(1),
                            tot[0][:, bass.ds(i, 1), 0:p.BW].bitcast(F32), ALU.subtract).then_inc(sem["tot_done"], tally.up("tot_done"))
                    eng.wait_ge(sem["tot_done"], tally.now("tot_done"))
                tally.loop(KT, body, gate=4, w_used__done=12, opart_free=4, dve_own=4, tot_done=1)
                if b + 1 < p.NB:
                    gated_low(p, b + 1)
                y, x = results(p, b)
                eng.wait_ge(sem["row_in"], tally.take("row_in", 16))
                for half in range(2):
                    eng.wait_ge(sem["w_used"], tally.take("w_used__done", KT))
                    for t in range(p.TB):
                        tt(y[:, 2 * t + half, :], ps[:, 4 - 4 * half + t, :],
                           gp_blk[b][:, half * 512:(half + 1) * 512]).then_inc(sem["y_gate"], tally.up("y_gate"))
                eng.wait_ge(sem["y_out"], tally.take("y_out", 2 * p.TB))
                tt(stat[:, 1, 4:4 + p.TB], stat[:, 0, 0:p.TB], stat[:, 0, 4:4 + p.TB], ALU.add).then_inc(sem["dve_own"], tally.up("dve_own"))
                eng.wait_ge(sem["dve_own"], tally.now("dve_own"))
                eng.tensor_scalar(stat[:, 1, 0:p.TB], stat[:, 1, 4:4 + p.TB], 1.0 / D, EPS, ALU.mult, ALU.add).then_inc(sem["out_mean"], tally.up("out_mean"))
                eng.wait_ge(sem["out_root"], tally.take("out_root"))
                eng.reciprocal(stat[:, 1, 0:p.TB], stat[:, 2, 0:p.TB]).then_inc(sem["dve_own"], tally.up("dve_own"))
                eng.wait_ge(sem["dve_own"], tally.now("dve_own"))
                eng.wait_ge(sem["post_in"], tally.take("post_in", 16 * p.TB))
                eng.wait_ge(sem["y_gate"], tally.now("y_gate"))
                for t in range(p.TB):
                    at_ = slice(2 * t, 2 * t + 2)
                    eng.scalar_tensor_tensor(x[:, at_, :], y[:, at_, :], stat[:, 1, t:t + 1], x[:, at_, :], ALU.mult, ALU.add).then_inc(sem["x_new"], tally.up("x_new"))

            constants()
            stage_end(eng, tally, "dve")
            for p in passes:
                if p.ctx:
                    modulation(p)
                norm(p)
                stage_end(eng, tally, "dve")
                if not p.full:
                    a_keys(p)
                    r_keys(p)
                    scaled(passes[p.n + 1], 0)
                    tally.skip("w_used__done", 2 * len(p.tiles))
                    stage_end(eng, tally, "dve")
                    states(p)
                    last_states(p, 0)
                    stage_end(eng, tally, "dve")
                    continue
                if not p.ctx:
                    eng.wait_ge(sem["rope_in"], tally.take("rope_in", 16))
                for t in range(4):
                    to(p, A_Q + t, [(qT[:, t, 0:p.T], 0, P)])
                a_keys(p)
                stage_end(eng, tally, "dve")
                attention(p)
                stage_end(eng, tally, "dve")
                convolution(p)
                decay_tables()
                stage_end(eng, tally, "dve")
                if not p.ctx:
                    eng.wait_ge(sem["rope_in"], tally.take("rope_in", 16))
                for j in range(2):
                    to(p, R_Q + j, halves(qd[:, 2 * j, 0:p.T], qd[:, 2 * j + 1, 0:p.T]))
                r_keys(p)
                stage_end(eng, tally, "dve")
                states(p)
                retention(p)
                stage_end(eng, tally, "dve")
                fourier(p)
                tally.skip("w_used__done", units_of(p)[1])
                stage_end(eng, tally, "dve")
                gated_low(p, 0)
                for b in range(p.NB):
                    merge(p, b)
                if p.ctx:
                    scaled(passes[p.n + 1], 0)
                stage_end(eng, tally, "dve")


INPUTS = ("x", "ctx", "w_ada", "b_ada", "norm_post", "w_in", "attn_sink", "ret_decay", "w_o_attn", "w_out")
TABLES = ("rope", "dft_x", "dft_c", "dft_head", "mask", "ident", "ret", "small")


def kernel(**inputs):
    import concourse.bacc as bacc
    from concourse.bass_utils import run_bass_kernel_spmd

    nc = bacc.Bacc("TRN2", target_bir_lowering=False, num_devices=1)
    arrays = {n: np.ascontiguousarray(inputs[n]) for n in INPUTS}
    arrays["w_o_rest"] = np.concatenate([inputs["w_o_conv"], inputs["w_o_ret"], inputs["w_o_fourier"]], axis=1)
    arrays["c_cols"] = np.stack([np.reshape(inputs["c"], (KT, P)), np.reshape(inputs["c_ctx"], (KT, P))]).transpose(2, 0, 1)
    arrays["norm_pre_cols"] = np.reshape(inputs["norm_pre"], (DEPTH, KT, P)).transpose(0, 2, 1)
    conv = np.concatenate([inputs["conv_w"], np.asarray(inputs["conv_b"])[:, None, :]], axis=1)
    arrays["conv_cols"] = conv.reshape(DEPTH, 4, 2, P).transpose(0, 3, 2, 1)
    arrays = {n: np.ascontiguousarray(v) for n, v in arrays.items()}
    arrays.update(tables())
    arrays = {f"in_{n}": v for n, v in arrays.items()}
    aps = {n[3:]: nc.dram_tensor(n, v.shape, mybir.dt.from_np(v.dtype), kind="ExternalInput").ap()
           for n, v in arrays.items()}
    out = nc.dram_tensor("out", (1, SEQ, D), F32, kind="ExternalOutput").ap()
    trunk(nc, aps, out)
    return run_bass_kernel_spmd(nc, [arrays], core_ids=[0]).results[0]["out"]
```
